# Optimizing a Trainium2 kernel written in Bass

```python
import jax, jax.numpy as jnp
from jax import lax
import numpy as np
import math
import jax
import jax.numpy as jnp

D_MODEL = 1024
BATCH = 1
SEQ = 512
DEPTH = 2

GRID_W = 64
CHUNK = 128
Q_BLOCK = 128
N_HEADS = 8
N_KV_HEADS = 2
HEAD_DIM = 64
GQA_GROUP = N_HEADS // N_KV_HEADS
ATTN_WIDTH = N_HEADS * HEAD_DIM
KV_WIDTH = N_KV_HEADS * HEAD_DIM
SG_HEADS = 8
SG_HEAD_DIM = 64
SG_WIDTH = SG_HEADS * SG_HEAD_DIM
MIX_WIDTH = ATTN_WIDTH + SG_WIDTH
IN_WIDTH = ATTN_WIDTH + 2 * KV_WIDTH + 2 * SG_WIDTH
D_FF = 2816
CONV_W = 3
ROPE_THETA = 10000.0
EPS = 1e-6


def rms_norm(x, g):
    xf = x.astype(jnp.float32)
    y = xf * lax.rsqrt(jnp.mean(xf * xf, axis=-1, keepdims=True) + EPS)
    return (y * g.astype(jnp.float32)).astype(x.dtype)

def axial_rope_tables(seq_len):
    rows = seq_len // GRID_W
    row = jnp.repeat(jnp.arange(rows, dtype=jnp.float32), GRID_W)
    col = jnp.tile(jnp.arange(GRID_W, dtype=jnp.float32), rows)
    axis_dim = HEAD_DIM // 2
    inv_freq = 1.0 / (ROPE_THETA ** (jnp.arange(0, axis_dim, 2, dtype=jnp.float32) / axis_dim))
    ang_r = row[:, None] * inv_freq[None, :]
    ang_c = col[:, None] * inv_freq[None, :]
    return jnp.cos(ang_r), jnp.sin(ang_r), jnp.cos(ang_c), jnp.sin(ang_c)

def rotate(x, cos, sin):
    n = x.shape[-1] // 2
    x1, x2 = x[..., :n], x[..., n:]
    c = cos[None, :, None, :].astype(x.dtype)
    s = sin[None, :, None, :].astype(x.dtype)
    return jnp.concatenate([x1 * c - x2 * s, x2 * c + x1 * s], axis=-1)

def axial_rope(x, tables):
    cr, sr, cc, sc = tables
    half = HEAD_DIM // 2
    return jnp.concatenate([rotate(x[..., :half], cr, sr), rotate(x[..., half:], cc, sc)], axis=-1)

def gqa_attention(q, k, v):
    b, s, _, dh = q.shape
    nblk = s // Q_BLOCK
    qb = q.reshape(b, nblk, Q_BLOCK, N_KV_HEADS, GQA_GROUP, dh)
    qb = jnp.moveaxis(qb, 1, 0)
    scale = HEAD_DIM ** -0.5

    def one_block(qblk):
        sc = jnp.einsum('bqkgd,bskd->bkgqs', qblk, k).astype(jnp.float32) * scale
        p = jax.nn.softmax(sc, axis=-1).astype(v.dtype)
        return jnp.einsum('bkgqs,bskd->bqkgd', p, v)

    o = lax.map(one_block, qb)
    return jnp.moveaxis(o, 0, 1).reshape(b, s, ATTN_WIDTH)

def spatial_gating(u, vv, sg_norm_g, sg_w, sg_b):
    b, s, _ = u.shape
    nc = s // CHUNK
    vv = rms_norm(vv.reshape(b, s, SG_HEADS, SG_HEAD_DIM), sg_norm_g)
    vv = vv.reshape(b, nc, CHUNK, SG_HEADS, SG_HEAD_DIM)
    mixed = jnp.einsum('hpq,bnqhd->bnphd', sg_w, vv) + sg_b.T[:, :, None]
    out = u.reshape(b, nc, CHUNK, SG_HEADS, SG_HEAD_DIM) * mixed
    return out.reshape(b, s, SG_WIDTH)

def depthwise_conv(h, w, bias):
    c = h.shape[-1]
    y = lax.conv_general_dilated(h, w[:, None, :].astype(h.dtype), window_strides=(1,),
                                 padding=[(CONV_W // 2, CONV_W // 2)],
                                 dimension_numbers=('NWC', 'WIO', 'NWC'),
                                 feature_group_count=c)
    return y + bias

def first_inputs(seed: int = 0) -> dict:
    key = jax.random.key(seed)
    ks = jax.random.split(key, 17)
    f32 = jnp.float32
    nrm = lambda k, shape, scale: jax.random.normal(k, shape, f32) * scale
    gain = lambda k, shape: 1.0 + 0.05 * jax.random.normal(k, shape, f32)
    return {
        "x": jax.random.normal(ks[0], (BATCH, SEQ, D_MODEL), f32),
        "attn_norm_g": gain(ks[1], (DEPTH, D_MODEL)),
        "w_in": nrm(ks[2], (DEPTH, D_MODEL, IN_WIDTH), D_MODEL ** -0.5),
        "q_norm_g": gain(ks[3], (DEPTH, HEAD_DIM)),
        "k_norm_g": gain(ks[4], (DEPTH, HEAD_DIM)),
        "sg_norm_g": gain(ks[5], (DEPTH, SG_HEADS, SG_HEAD_DIM)),
        "sg_w": nrm(ks[6], (DEPTH, SG_HEADS, CHUNK, CHUNK), 0.5 * CHUNK ** -0.5),
        "sg_b": gain(ks[7], (DEPTH, SG_HEADS, CHUNK)),
        "attn_out_g": gain(ks[8], (DEPTH, ATTN_WIDTH)),
        "sg_out_g": gain(ks[9], (DEPTH, SG_WIDTH)),
        "w_o": nrm(ks[10], (DEPTH, MIX_WIDTH, D_MODEL), MIX_WIDTH ** -0.5),
        "ffn_norm_g": gain(ks[11], (DEPTH, D_MODEL)),
        "w_up": nrm(ks[12], (DEPTH, D_MODEL, 2 * D_FF), D_MODEL ** -0.5),
        "conv_w": nrm(ks[13], (DEPTH, CONV_W, 2 * D_FF), CONV_W ** -0.5),
        "conv_b": nrm(ks[14], (DEPTH, 2 * D_FF), 0.02),
        "w_down": nrm(ks[15], (DEPTH, D_FF, D_MODEL), D_FF ** -0.5),
    }

def first_block(x, attn_norm_g, w_in, q_norm_g, k_norm_g, sg_norm_g, sg_w, sg_b,
              attn_out_g, sg_out_g, w_o, ffn_norm_g, w_up, conv_w, conv_b, w_down):
    b, s, _ = x.shape
    tables = axial_rope_tables(s)
    split_at = [ATTN_WIDTH, ATTN_WIDTH + KV_WIDTH, ATTN_WIDTH + 2 * KV_WIDTH,
                ATTN_WIDTH + 2 * KV_WIDTH + SG_WIDTH]
    for i in range(DEPTH):
        h = rms_norm(x, attn_norm_g[i])
        proj = h @ w_in[i]
        q, k, v, u, vv = jnp.split(proj, split_at, axis=-1)
        q = rms_norm(q.reshape(b, s, N_HEADS, HEAD_DIM), q_norm_g[i])
        k = rms_norm(k.reshape(b, s, N_KV_HEADS, HEAD_DIM), k_norm_g[i])
        v = v.reshape(b, s, N_KV_HEADS, HEAD_DIM)
        q = axial_rope(q, tables)
        k = axial_rope(k, tables)
        attn_o = gqa_attention(q, k, v)
        sg_o = spatial_gating(jax.nn.gelu(u), jax.nn.gelu(vv),
                              sg_norm_g[i], sg_w[i], sg_b[i])
        merged = jnp.concatenate([rms_norm(attn_o, attn_out_g[i]),
                                  rms_norm(sg_o, sg_out_g[i])], axis=-1)
        x = x + merged @ w_o[i]
        h = rms_norm(x, ffn_norm_g[i]) @ w_up[i]
        h = depthwise_conv(h, conv_w[i], conv_b[i])
        gate, up = jnp.split(h, 2, axis=-1)
        x = x + (jax.nn.silu(gate) * up) @ w_down[i]
    return x


MIX_WIDTH_2 = D_MODEL
ATTN_HEAD_DIM = 64
ATTN_WIDTH_2 = MIX_WIDTH_2 // 4
ATTN_HEADS = ATTN_WIDTH_2 // ATTN_HEAD_DIM
DILATED_PATTERNS = ((128, 1), (512, 4), (2048, 16))
CONV_CH = MIX_WIDTH_2 // 4
CONV_WIDTH = 31
GDN_HEAD_DIM = 128
GDN_WIDTH = MIX_WIDTH_2 - ATTN_WIDTH_2 - CONV_CH
GDN_HEADS = GDN_WIDTH // GDN_HEAD_DIM
GDN_CONV_WIDTH = 4
GDN_CHUNK = 64
FFN_HIDDEN = ((8 * D_MODEL + 3 * 256 - 1) // (3 * 256)) * 256
IN_SPLIT_SIZES = (ATTN_WIDTH_2, ATTN_WIDTH_2, ATTN_WIDTH_2, 2 * CONV_CH, 3 * GDN_WIDTH, GDN_WIDTH, GDN_HEADS, GDN_HEADS)
IN_WIDTH_2 = sum(IN_SPLIT_SIZES)
RMS_EPS = 1e-6
LN_EPS = 1e-5
L2_EPS = 1e-6


def rms_norm_2(x, gain):
    x32 = x.astype(jnp.float32)
    y = x32 * lax.rsqrt(jnp.mean(x32 * x32, axis=-1, keepdims=True) + RMS_EPS)
    return (y * gain.astype(jnp.float32)).astype(x.dtype)

def l2_normalize(t):
    return t * lax.rsqrt(jnp.sum(t * t, axis=-1, keepdims=True) + L2_EPS)

def causal_depthwise_conv(x, w):
    K, C = w.shape
    return lax.conv_general_dilated(
        x, w.reshape(K, 1, C).astype(x.dtype), window_strides=(1,), padding=[(K - 1, 0)],
        dimension_numbers=('NWC', 'WIO', 'NWC'), feature_group_count=C)

def rotary(t, positions):
    D = t.shape[-1]
    half = D // 2
    inv_freq = jnp.exp(-math.log(ROPE_THETA) * jnp.arange(half, dtype=jnp.float32) * (2.0 / D))
    ang = positions.astype(jnp.float32)[:, None] * inv_freq[None, :]
    cos = jnp.cos(ang)[None, :, None, :]
    sin = jnp.sin(ang)[None, :, None, :]
    t1, t2 = t[..., :half], t[..., half:]
    return jnp.concatenate([t1 * cos - t2 * sin, t2 * cos + t1 * sin], axis=-1)

def dilated_window_attention(q, k, v, window, dilation):
    Bn, S, H, D = q.shape
    n = window // dilation
    L = S // dilation
    nb = -(-L // n)
    Lp = nb * n

    def residues(t):
        t = t.reshape(Bn, L, dilation, H, D)
        return jnp.pad(t, ((0, 0), (0, Lp - L), (0, 0), (0, 0), (0, 0)))

    def key_blocks(t):
        tp = jnp.pad(residues(t), ((0, 0), (n, 0), (0, 0), (0, 0), (0, 0)))
        tp = tp.reshape(Bn, nb + 1, n, dilation, H, D)
        return jnp.concatenate([tp[:, :-1], tp[:, 1:]], axis=2)

    qb = residues(q).reshape(Bn, nb, n, dilation, H, D)
    kb = key_blocks(k)
    vb = key_blocks(v)
    s = jnp.einsum('bnqrhd,bnkrhd->bnrhqk', qb, kb)
    qi = jnp.arange(n)[None, :, None]
    ki = jnp.arange(2 * n)[None, None, :]
    blk = jnp.arange(nb)[:, None, None]
    valid = (ki >= qi) & (ki <= qi + n) & (blk * n - n + ki >= 0)
    s = jnp.where(valid[None, :, None, None], s, -jnp.inf)
    m = jnp.max(s, axis=-1, keepdims=True)
    p = jnp.exp(s - m)
    l = jnp.sum(p, axis=-1, keepdims=True)
    o = jnp.einsum('bnrhqk,bnkrhd->bnqrhd', p / l, vb)
    o = o.reshape(Bn, Lp, dilation, H, D)[:, :L].reshape(Bn, S, H, D)
    lse = (m + jnp.log(l))[..., 0]
    lse = lse.transpose(0, 1, 4, 2, 3).reshape(Bn, Lp, dilation, H)[:, :L].reshape(Bn, S, H)
    return o, lse

def dilated_attention_mixer(aq, ak, av, positions):
    Bn, S, _ = aq.shape
    shp = (Bn, S, ATTN_HEADS, ATTN_HEAD_DIM)
    q = rotary(aq.reshape(shp).astype(jnp.float32), positions) * (ATTN_HEAD_DIM ** -0.5)
    k = rotary(ak.reshape(shp).astype(jnp.float32), positions)
    v = av.reshape(shp).astype(jnp.float32)
    outs, lses = [], []
    for window, dilation in DILATED_PATTERNS:
        o, lse = dilated_window_attention(q, k, v, window, dilation)
        outs.append(o)
        lses.append(lse)
    wts = jax.nn.softmax(jnp.stack(lses, axis=0), axis=0)
    o = jnp.einsum('pbsh,pbshd->bshd', wts, jnp.stack(outs, axis=0))
    return o.reshape(Bn, S, ATTN_WIDTH_2)

def conformer_conv_mixer(u, dw, dw_bias, norm_gain, norm_bias):
    val, gate = jnp.split(u, 2, axis=-1)
    y = val * jax.nn.sigmoid(gate)
    y = causal_depthwise_conv(y, dw) + dw_bias.astype(y.dtype)
    y32 = y.astype(jnp.float32)
    mu = jnp.mean(y32, axis=-1, keepdims=True)
    var = jnp.mean(jnp.square(y32 - mu), axis=-1, keepdims=True)
    y32 = (y32 - mu) * lax.rsqrt(var + LN_EPS) * norm_gain.astype(jnp.float32) + norm_bias.astype(jnp.float32)
    return jax.nn.silu(y32)

def chunk_gated_delta_rule(q, k, v, g, beta):
    Bn, S, H, Dk = q.shape
    Dv = v.shape[-1]
    C = GDN_CHUNK
    N = S // C
    q = q * (Dk ** -0.5)

    def to_chunks(t):
        return t.reshape(Bn, N, C, H, -1).transpose(0, 3, 1, 2, 4)

    q, k, v = to_chunks(q), to_chunks(k), to_chunks(v)
    g = jnp.cumsum(g.reshape(Bn, N, C, H).transpose(0, 3, 1, 2), axis=-1)
    beta = beta.reshape(Bn, N, C, H).transpose(0, 3, 1, 2)
    idx = jnp.arange(C)
    lower_incl = idx[:, None] >= idx[None, :]
    strict = idx[:, None] > idx[None, :]
    decay = jnp.exp(jnp.where(lower_incl, g[..., :, None] - g[..., None, :], -jnp.inf))
    k_beta = k * beta[..., None]
    v_beta = v * beta[..., None]
    m = jnp.where(strict, jnp.einsum('bhncd,bhnsd->bhncs', k_beta, k) * decay, 0.0)
    rhs = jnp.concatenate([v_beta, k_beta * jnp.exp(g)[..., None]], axis=-1)
    sol = lax.linalg.triangular_solve(m + jnp.eye(C, dtype=jnp.float32), rhs, left_side=True, lower=True,
                                      unit_diagonal=True)
    u = sol[..., :Dv]
    w = sol[..., Dv:]
    intra = jnp.where(lower_incl, jnp.einsum('bhncd,bhnsd->bhncs', q, k) * decay, 0.0)

    def step(state, xs):
        q_c, k_c, u_c, w_c, g_c, intra_c = xs
        v_new = u_c - w_c @ state
        out = (q_c * jnp.exp(g_c)[..., None]) @ state + intra_c @ v_new
        g_last = g_c[..., -1]
        state = state * jnp.exp(g_last)[..., None, None] + jnp.einsum(
            'bhcd,bhce->bhde', k_c * jnp.exp(g_last[..., None] - g_c)[..., None], v_new)
        return state, out

    xs = tuple(jnp.moveaxis(t, 2, 0) for t in (q, k, u, w, g, intra))
    state0 = jnp.zeros((Bn, H, Dk, Dv), jnp.float32)
    _, out = lax.scan(step, state0, xs)
    return out.transpose(1, 0, 3, 2, 4).reshape(Bn, S, H, Dv)

def gated_deltanet_mixer(qkv, gate, a, b, short_conv, a_log, dt_bias, out_norm):
    Bn, S, _ = qkv.shape
    qkv = jax.nn.silu(causal_depthwise_conv(qkv, short_conv).astype(jnp.float32))
    shp = (Bn, S, GDN_HEADS, GDN_HEAD_DIM)
    q, k, v = (t.reshape(shp) for t in jnp.split(qkv, 3, axis=-1))
    q = l2_normalize(q)
    k = l2_normalize(k)
    beta = jax.nn.sigmoid(b.astype(jnp.float32))
    g = -jnp.exp(a_log.astype(jnp.float32)) * jax.nn.softplus(a.astype(jnp.float32) + dt_bias.astype(jnp.float32))
    o = chunk_gated_delta_rule(q, k, v, g, beta)
    o = rms_norm_2(o, out_norm) * jax.nn.silu(gate.astype(jnp.float32).reshape(shp))
    return o.reshape(Bn, S, GDN_WIDTH)

def second_inputs(seed: int = 0) -> dict:
    key = jax.random.key(seed)
    ks = jax.random.split(key, 20)
    f32 = jnp.float32

    def nrm(k, shape, fan_in):
        return jax.random.normal(k, shape, f32) * (fan_in ** -0.5)

    def gain(k, shape):
        return 1.0 + 0.01 * jax.random.normal(k, shape, f32)

    dt = jnp.exp(jax.random.uniform(ks[10], (DEPTH, GDN_HEADS), f32, math.log(1e-3), math.log(1e-1)))
    return {
        'x': jax.random.normal(ks[0], (BATCH, SEQ, D_MODEL), f32),
        'attn_pre_norm': gain(ks[1], (DEPTH, D_MODEL)),
        'w_in': nrm(ks[2], (DEPTH, D_MODEL, IN_WIDTH_2), D_MODEL),
        'conv_dw': nrm(ks[3], (DEPTH, CONV_WIDTH, CONV_CH), CONV_WIDTH),
        'conv_dw_bias': 0.01 * jax.random.normal(ks[4], (DEPTH, CONV_CH), f32),
        'conv_norm_gain': gain(ks[5], (DEPTH, CONV_CH)),
        'conv_norm_bias': 0.01 * jax.random.normal(ks[6], (DEPTH, CONV_CH), f32),
        'gdn_short_conv': nrm(ks[7], (DEPTH, GDN_CONV_WIDTH, 3 * GDN_WIDTH), GDN_CONV_WIDTH),
        'gdn_a_log': jnp.log(jax.random.uniform(ks[8], (DEPTH, GDN_HEADS), f32, 1.0, 16.0)),
        'gdn_dt_bias': dt + jnp.log(-jnp.expm1(-dt)),
        'gdn_out_norm': gain(ks[9], (DEPTH, GDN_HEAD_DIM)),
        'w_out': nrm(ks[11], (DEPTH, MIX_WIDTH_2, D_MODEL), MIX_WIDTH_2),
        'attn_post_norm': gain(ks[12], (DEPTH, D_MODEL)),
        'ffn_pre_norm': gain(ks[13], (DEPTH, D_MODEL)),
        'w_gate': nrm(ks[14], (DEPTH, D_MODEL, FFN_HIDDEN), D_MODEL),
        'w_up': nrm(ks[15], (DEPTH, D_MODEL, FFN_HIDDEN), D_MODEL),
        'w_down': nrm(ks[16], (DEPTH, FFN_HIDDEN, D_MODEL), FFN_HIDDEN),
        'ffn_post_norm': gain(ks[17], (DEPTH, D_MODEL)),
    }

def second_block(x, attn_pre_norm, w_in, conv_dw, conv_dw_bias, conv_norm_gain, conv_norm_bias, gdn_short_conv,
              gdn_a_log, gdn_dt_bias, gdn_out_norm, w_out, attn_post_norm, ffn_pre_norm, w_gate, w_up, w_down,
              ffn_post_norm):
    Bn, S, _ = x.shape
    positions = jnp.arange(S)
    offsets = np.cumsum(IN_SPLIT_SIZES)[:-1].tolist()
    for i in range(DEPTH):
        h = rms_norm_2(x, attn_pre_norm[i])
        z = h @ w_in[i]
        aq, ak, av, conv_u, gdn_qkv, gdn_gate, gdn_a, gdn_b = jnp.split(z, offsets, axis=-1)
        y_attn = dilated_attention_mixer(aq, ak, av, positions)
        y_conv = conformer_conv_mixer(conv_u, conv_dw[i], conv_dw_bias[i], conv_norm_gain[i], conv_norm_bias[i])
        y_gdn = gated_deltanet_mixer(gdn_qkv, gdn_gate, gdn_a, gdn_b, gdn_short_conv[i], gdn_a_log[i],
                                     gdn_dt_bias[i], gdn_out_norm[i])
        mix = jnp.concatenate([y_attn.astype(x.dtype), y_conv.astype(x.dtype), y_gdn.astype(x.dtype)], axis=-1)
        x = x + rms_norm_2(mix @ w_out[i], attn_post_norm[i])
        h = rms_norm_2(x, ffn_pre_norm[i])
        f = (jax.nn.silu(h @ w_gate[i]) * (h @ w_up[i])) @ w_down[i]
        x = x + rms_norm_2(f, ffn_post_norm[i])
    return x


_first_inputs = second_inputs


def second_inputs(seed=0):
    import zlib

    import numpy as np

    out = dict(_first_inputs(seed))
    spreads = {}
    factors = {'attn_pre_norm': 3.012,
     'conv_dw_bias': 18.049,
     'conv_norm_gain': 54.32,
     'conv_norm_bias': 58.912,
     'gdn_out_norm': 19.098,
     'attn_post_norm': 14.958,
     'ffn_pre_norm': 13.945,
     'ffn_post_norm': 30.288}
    for name, (base, spread) in spreads.items():
        noise = np.random.default_rng([zlib.crc32(name.encode()), seed]).standard_normal(out[name].shape)
        drawn = base * np.exp(spread * noise) if base else spread * noise
        out[name] = jnp.asarray(drawn.astype(out[name].dtype))
    for name, factor in factors.items():
        out[name] = (out[name] * factor).astype(out[name].dtype)
    return out


_narrow_inputs = second_inputs


def second_inputs(seed=0):
    out = dict(_narrow_inputs(seed))
    wider = {'conv_norm_gain': 6.29,
     'conv_norm_bias': 5.36,
     'gdn_out_norm': 4.25,
     'attn_post_norm': 3.55,
     'ffn_pre_norm': 3.33,
     'ffn_post_norm': 4.87}
    for name, times in wider.items():
        mean = out[name].mean()
        out[name] = (mean + times * (out[name] - mean)).astype(out[name].dtype)
    return out


def setup_inputs(seed=0):
    out = dict(first_inputs(seed))
    for name, value in second_inputs(seed + 1).items():
        if name != "x":
            out[name + "_2"] = value
    return out


def reference(
    x, attn_norm_g, w_in, q_norm_g, k_norm_g, sg_norm_g, sg_w, sg_b, attn_out_g, sg_out_g, w_o,
    ffn_norm_g, w_up, conv_w, conv_b, w_down, attn_pre_norm_2, w_in_2, conv_dw_2,
    conv_dw_bias_2, conv_norm_gain_2, conv_norm_bias_2, gdn_short_conv_2, gdn_a_log_2,
    gdn_dt_bias_2, gdn_out_norm_2, w_out_2, attn_post_norm_2, ffn_pre_norm_2, w_gate_2, w_up_2,
    w_down_2, ffn_post_norm_2,
):
    x = first_block(
        x, attn_norm_g, w_in, q_norm_g, k_norm_g, sg_norm_g, sg_w, sg_b, attn_out_g, sg_out_g,
        w_o, ffn_norm_g, w_up, conv_w, conv_b, w_down,
    )
    return second_block(
        x, attn_pre_norm_2, w_in_2, conv_dw_2, conv_dw_bias_2, conv_norm_gain_2,
        conv_norm_bias_2, gdn_short_conv_2, gdn_a_log_2, gdn_dt_bias_2, gdn_out_norm_2, w_out_2,
        attn_post_norm_2, ffn_pre_norm_2, w_gate_2, w_up_2, w_down_2, ffn_post_norm_2,
    )


_drawn_inputs = setup_inputs


def setup_inputs(seed=0):
    import zlib

    import numpy as np

    out = dict(_drawn_inputs(seed))
    spreads = {}
    factors = {}
    for name, (base, spread) in spreads.items():
        noise = np.random.default_rng([zlib.crc32(name.encode()), seed]).standard_normal(out[name].shape)
        drawn = base * np.exp(spread * noise) if base else spread * noise
        out[name] = jnp.asarray(drawn.astype(out[name].dtype))
    for name, factor in factors.items():
        out[name] = (out[name] * factor).astype(out[name].dtype)
    return out
```

```python
import math
from contextlib import ExitStack

import concourse.bass as bass
from concourse import mybir

P = 128
F32 = mybir.dt.float32
F32R = mybir.dt.float32r
BF16 = mybir.dt.bfloat16
ALU = mybir.AluOpType
ACT = mybir.ActivationFunctionType
AX = mybir.AxisListType.X
ds = bass.ds


class Signal:

    def __init__(self, sem, per=1, base=0):
        self.sem, self.per, self.base = sem, per, base

    def at(self, layer, i):
        return layer * self.per + (i + (self.base + 1))


class Order:

    def __init__(self, eng, sem, begun):
        self.eng, self.sem, self.n, self.last, self.begun = eng, sem, 0, None, begun

    def step(self, ins):
        self.n += 1
        ins.then_inc(self.sem, 1)
        self.last = (self.sem, self.n)

    def told(self, ins, signal, layer, i):
        ins.then_inc(signal.sem, 1)
        self.last = (signal.sem, signal.at(layer, i))

    def settle(self):
        if self.last is not None:
            self.eng.wait_ge(*self.last)

    def wait_alone(self, sem, value, own=None):
        self.eng.wait_ge(*(own or (self.begun.sem, 1)))
        self.eng.wait_ge(sem, value)

    def restart(self):
        own = (self.sem, self.n) if self.n else (self.begun.sem, 1)
        if self.last is not None and self.last[0] is not self.sem:
            self.wait_alone(*self.last, own)
        else:
            self.eng.wait_ge(*own)
        if self.n:
            self.eng.sem_clear(self.sem)
        self.n, self.last = 0, None


def network(nc, D, out, stop=None):
    SEQ, DM = D["x"].shape[1:]
    DEPTH = D["w_in"].shape[0]
    KD = DM // P
    TB = SEQ // P
    EPS = 1e-6
    LN_EPS = 1e-5

    HD = D["q_norm_g"].shape[1]
    AW = D["attn_out_g"].shape[1]
    SGW = D["sg_out_g"].shape[1]
    SGH = D["sg_w"].shape[1]
    INW = D["w_in"].shape[2]
    KVW = (INW - AW - 2 * SGW) // 2
    NH, NKV = AW // HD, KVW // HD
    GROUP = NH // NKV
    NQ, NS = AW // P, SGW // P
    N_IN = INW // P
    FF = D["w_down"].shape[1]
    NF = FF // P
    HALF = NF // 2
    TAPS = D["conv_w"].shape[1]
    assert (KD, TB, SEQ, N_IN, NQ, NS, KVW, HALF * 2, TAPS) == (8, 4, 512, 14, 4, 4, P, NF, 3)

    PAIRS_IN, PAIRS_O, PAIRS_UP, PAIRS_DOWN = N_IN // 2, KD // 2, HALF, KD // 2
    OFF_O = PAIRS_IN
    OFF_UP = [OFF_O + PAIRS_O + hf * (PAIRS_UP + PAIRS_DOWN) for hf in range(2)]
    OFF_DOWN = [o + PAIRS_UP for o in OFF_UP]
    PAIRS1 = OFF_DOWN[1] + PAIRS_DOWN

    CC = D["conv_dw_2"].shape[2]
    CT = D["conv_dw_2"].shape[1]
    GH = D["gdn_a_log_2"].shape[1]
    GT = D["gdn_short_conv_2"].shape[1]
    GW = D["gdn_short_conv_2"].shape[2] // 3
    AH = (DM - CC - GW) // 64
    CH = 64
    NCH = SEQ // CH
    NC, NA, NG = CC // P, AH // 2, 3 * GH
    LEVELS = 6
    N_IN2 = 3 * NA + 2 * NC + 4 * GH
    assert GW // GH == P and D["w_gate_2"].shape[2] == FF and N_IN2 % 2 == 0 and CH == 2 ** LEVELS == P // 2
    PAIRS_IN2 = N_IN2 // 2
    OFF_O2 = PAIRS_IN2
    OFF_UP2 = [OFF_O2 + PAIRS_O + hf * (PAIRS_UP + PAIRS_DOWN) for hf in range(2)]
    OFF_DOWN2 = [o + PAIRS_UP for o in OFF_UP2]
    PAIRS2 = OFF_DOWN2[1] + PAIRS_DOWN
    BASE2 = DEPTH * PAIRS1
    PAIRS = BASE2 + DEPTH * PAIRS2
    D_DW, D_BIAS = 0, CT * NC
    D_LNG, D_LNB = D_BIAS + NC, D_BIAS + 2 * NC
    D_SC = D_BIAS + 3 * NC
    D_ON = D_SC + GT * NG
    N_PD = D_ON + 1

    with ExitStack() as ctx:
        def sb(name, shape, dt=F32, on=ctx):
            return on.enter_context(nc.sbuf_tensor(name, shape, dt))

        def sem(name, per=1):
            return Signal(ctx.enter_context(nc.semaphore(name)), per)

        def again(signal, per):
            return Signal(signal.sem, per, DEPTH * signal.per)

        ps = ctx.enter_context(nc.psum_tensor("ps", [P, 8, SEQ], F32))
        ACC, STAT, ROT, TRN = (0, 1), (2, 3), (4, 5), (6, 7)

        x = sb("x_sb", [P, KD, SEQ])
        h_hi, h_lo = sb("h_hi", [P, KD, SEQ], F32R), sb("h_lo", [P, KD, SEQ], F32R)
        raw = [sb(f"raw{s}", [P, HALF, P]) for s in range(2)]
        whi = [sb(f"whi{s}", [P, HALF, P], F32R) for s in range(2)]
        wlo = [sb(f"wlo{s}", [P, HALF, P], F32R) for s in range(2)]
        rstd = sb("rstd", [P, SEQ])
        ssq = sb("ssq", [P, SEQ])
        sqt = sb("sqt", [P, 2, SEQ])
        lnt = sb("lnt", [P, SEQ])
        ident = sb("ident", [P, P])
        ones = sb("ones", [P, P])
        blk = sb("blk", [P, P])
        negones = sb("negones", [P, P], F32R)
        eps = sb("eps", [P, 2])
        GENS = 4 * DEPTH + 1
        gains = sb("gains", [P, GENS * KD + 2 * DEPTH * KD])
        pa = sb("pa", [P, DEPTH, 14])
        pb = sb("pb", [P, DEPTH, 2 * 2 * NF])
        pc = sb("pc", [P, DEPTH, 2 * 2 * NF])
        pd = sb("pd", [P, DEPTH, N_PD])
        gate_par = sb("gate_par", [P, 2, DEPTH, GH])

        setup_loaded = sem("setup_loaded")
        consts_made = sem("consts_made")
        params_turned = sem("params_turned")
        params_kept = sem("params_kept")
        x_loaded = sem("x_loaded")
        x_turned = sem("x_turned")
        x_ready = sem("x_ready", KD)
        act_step, dve_step, pool_step = sem("act_step"), sem("dve_step"), sem("pool_step")
        w_loaded = [sem(f"w_loaded{s}") for s in range(2)]
        w_hi_ready = sem("w_hi_ready")
        w_lo_ready = sem("w_lo_ready")
        unit_done = sem("unit_done")
        acc_free = sem("acc_free")
        sq_ready, ssq_done = sem("sq_ready", KD), sem("ssq_done", KD)
        hhi_ready, h_ready = sem("hhi_ready", KD), sem("h_ready", KD)
        stat_ready, rstd_ready = sem("stat_ready"), sem("rstd_ready")
        sgw_loaded, sgb_loaded = sem("sgw_loaded", 1), sem("sgb_loaded", 1)
        wT_ready, wT_kept = sem("wT_ready", 2), sem("wT_kept", 2)
        gelu_ready = sem("gelu_ready", 2 * NS)
        vvsq_ready, vvstat_ready = sem("vvsq_ready", NS), sem("vvstat_ready", NS)
        vvrs_ready, vvn_ready = sem("vvrs_ready", NS), sem("vvn_ready", NS)
        vvT_ready, vvT_kept = sem("vvT_ready", NS), sem("vvT_kept", NS)
        mix_ready, sg_ready = sem("mix_ready", NS), sem("sg_ready", NS)
        mix_used = sem("mix_used", NS)
        qksq_ready, qkstat_ready = sem("qksq_ready", NQ + 1), sem("qkstat_ready", NQ + 1)
        qkrs_ready, qkn_ready = sem("qkrs_ready", NQ + 1), sem("qkn_ready", NQ + 1)
        rot_ready, rot_used, rope_ready = sem("rot_ready", NQ + 1), sem("rot_used", NQ + 1), sem("rope_ready", NQ + 1)
        qr_ready = sem("qr_ready", NQ + 1)
        vT_ready, vaug_ready = sem("vT_ready", 1), sem("vaug_ready", 1)
        vones_ready = sem("vones_ready", 1)
        S_ready, S_used = sem("S_ready", 2 * NH), sem("S_used", 2 * NH)
        diag_ready = sem("diag_ready", NH)
        ST_ready, P_ready = sem("ST_ready", NH * TB), sem("P_ready", NH * TB)
        PV_done, ao_ready = sem("PV_done", NH * TB), sem("ao_ready", NH)
        osq_ready, osq_used = sem("osq_ready", NQ + NS), sem("osq_used", NQ + NS)
        ors_ready = sem("ors_ready", 2)
        mtmp_ready, mhi_ready, merged_ready = (sem(n, NQ + NS) for n in ("mtmp_ready", "mhi_ready", "merged_ready"))
        center_ready, conv_ready = sem("center_ready", 2 * NF), sem("conv_ready", 2 * NF)
        silu_ready, prod_ready = sem("silu_ready", NF), sem("prod_ready", NF)
        ahi_ready, a_ready = sem("ahi_ready", NF), sem("a_ready", NF)
        c2_loaded, c2_cast, wab_loaded, wab_split = sem("c2_loaded"), sem("c2_cast"), sem("wab_loaded"), sem("wab_split", 2)
        zp_clear = sem("zp_clear")
        sc_center, sc_ready, sc_silu = (sem(n, NG) for n in ("sc_center", "sc_ready", "sc_silu"))
        gate_ready, glu_ready, cg_ready = sem("gate_ready", GH), sem("glu_ready", NC), sem("cg_ready", NC)
        rcol_ready, rcol_kept, ab_ready = sem("rcol_ready"), sem("rcol_kept"), sem("ab_ready")
        l2sq, l2stat, l2rs, l2n = (sem(n, 2 * GH) for n in ("l2sq", "l2stat", "l2rs", "l2n"))
        rot2_ready, rot2_used, rope2_ready, qkr2_ready = (again(n, 2 * NA) for n in (rot_ready, rot_used, rope_ready, qr_ready))
        v2T_ready, vaug2_ready, v2ones_ready = again(vT_ready, NA), again(vaug_ready, NA), again(vones_ready, 1)
        S2_ready, S2_used, diag2_ready = again(S_ready, 2 * AH), again(S_used, 2 * AH), again(diag_ready, AH)
        E2_ready = sem("E2_ready", AH * TB)
        ST2_ready, P2_ready, PV2_done = (again(n, AH * TB) for n in (ST_ready, P_ready, PV_done))
        ya_ready = sem("ya_ready", AH)
        dw_ready, mean_ready, mean_kept = sem("dw_ready", NC), sem("mean_ready"), sem("mean_kept")
        centered, lnsq, lnsq_used, ln_scaled, yc_ready = (sem(n, NC) for n in ("centered", "lnsq", "lnsq_used", "ln_scaled", "yc_ready"))
        ln_rs = sem("ln_rs")
        gate_in, gate_e1, gate_e2, g_ready, G_ready, gc_kept, dg_ready, eg_cols = (sem(n) for n in (
            "gate_in", "gate_e1", "gate_e2", "g_ready", "G_ready", "gc_kept", "dg_ready", "eg_cols"))
        beg_ready = sem("beg_ready")
        grow_ready, brow_ready, kT_ready, gvT_ready = (sem(n, GH) for n in ("grow_ready", "brow_ready", "kT_ready", "gvT_ready"))
        kb_ready, gap_ready, decay_ready, eg_ready = (sem(n, GH) for n in ("kb_ready", "gap_ready", "decay_ready", "eg_ready"))
        turned_used, kk_ready, qk_ready, head_ready = (sem(n, GH) for n in ("turned_used", "kk_ready", "qk_ready", "head_ready"))
        lt_ready, p1_ready, p1_kept, xp_ready, xpt_ready, x_new = (sem(n, GH * LEVELS) for n in (
            "lt_ready", "p1_ready", "p1_kept", "xp_ready", "xpt_ready", "x_new"))
        uu_ready, uu_kept, ww_ready, ww_kept = (sem(n, GH) for n in ("uu_ready", "uu_kept", "ww_ready", "ww_kept"))
        state_ready, ws_ready, vn_ready, o_ready, o_kept, ds_ready = (sem(n, NCH) for n in (
            "state_ready", "ws_ready", "vn_ready", "o_ready", "o_kept", "ds_ready"))
        ogsq, ogstat, ogrs, og_ready = (sem(n, GH) for n in ("ogsq", "ogstat", "ogrs", "og_ready"))
        m2hi_ready, merged2_ready = again(mhi_ready, KD), again(merged_ready, KD)
        ysq_ready, yssq_done = sem("ysq_ready", 2 * KD), sem("yssq_done", 2 * KD)
        ystat_ready, yrs_ready = sem("ystat_ready", 2), sem("yrs_ready", 2)
        x2_ready = sem("x2_ready", 2 * KD)
        silu2_ready, prod2_ready, a2hi_ready, a2_ready = (again(n, NF) for n in (silu_ready, prod_ready, ahi_ready, a_ready))
        out_turned, out_kept, out_stored = sem("out_turned"), sem("out_kept"), sem("out_stored")

        def tile(t, n):
            return t[:, n, :] if isinstance(n, int) else t[:, ds(n, 1), :].rearrange("p a n -> p (a n)")

        def gain(i):
            return gains[:, i:i + 1] if isinstance(i, int) else gains[:, ds(i, 1)]

        def param(t, layer, i):
            i = slice(i, i + 1) if isinstance(i, int) else ds(i, 1)
            return t[:, ds(layer, 1), i].rearrange("p a b -> p (a b)")

        with ExitStack() as on:
            xs = sb("xs", [P, TB, DM], on=on)
            rows = sb("rows", [P, 9, P], on=on)
        N_GAINS = GENS * KD + 2 * DEPTH * KD
        ROWS = [N_GAINS] + [14, 4 * NF, 4 * NF, N_PD] * DEPTH
        COLS = [gains[:]] + [t[:, l, :] for l in range(DEPTH) for t in (pa, pb, pc, pd)]
        N_ROWS = len(ROWS)

        with ExitStack() as on:
            zq = sb("zq", [P, NQ, SEQ], on=on)
            zk = sb("zk", [P, SEQ], on=on)
            zv = sb("zv", [P, SEQ], on=on)
            vv = sb("vv", [P, NS, SEQ], on=on)
            kd = [sb(f"kd{g}", [P, SEQ], on=on) for g in range(NKV)]
            qr = sb("qr", [P, NQ, SEQ], F32R, on=on)
            kr = [sb(f"kr{g}", [P, SEQ], F32R, on=on) for g in range(NKV)]
            vaug = sb("vaug", [P, NKV, 2, TB, P], on=on)
            probs = sb("probs", [P, TB, SEQ], on=on)
            diag = sb("diag", [P, TB, P], F32R, on=on)
            vvT = sb("vvT", [P, TB, SGW], on=on)
            wT = sb("wT", [P, SGH, P], on=on)
            mrs = sb("mrs", [P, 2, SEQ], on=on)
            t1 = sb("t1", [P, SEQ], on=on)
            t2 = sb("t2", [P, SEQ], on=on)
            mx = sb("mx", [P, 2, TB], on=on)
            u = sb("u", [P, NS, SEQ], on=on)
            ao = sb("ao", [P, NQ, SEQ], on=on)
            ors = sb("ors", [P, 2, SEQ], on=on)
            mtmp = sb("mtmp", [P, 2, SEQ], on=on)
            rope = sb("rope", [P, 2, SEQ], on=on)
            perm = sb("perm", [P, P], on=on)
            sgb = sb("sgb", [P, NS, P], on=on)
        msq = sqt
        sgw = probs[:, 0:2, :].rearrange("p a (h q) -> p (a h) q", q=P)

        with ExitStack() as on:
            a_hi = sb("a_hi", [P, HALF, SEQ], F32R, on=on)
            a_lo = sb("a_lo", [P, HALF, SEQ], F32R, on=on)
            pad = [sb(f"pad{s}", [P, SEQ + 2], on=on) for s in range(2)]
            cv = [sb(f"cv{s}", [P, SEQ], on=on) for s in range(2)]
            prod = sb("prod", [P, SEQ], on=on)
            y = sb("y_sb", [P, KD, SEQ], on=on)

        with ExitStack() as on:
            gq, gk, gv, gz = (sb(n, [P, GH, SEQ], on=on) for n in ("gq", "gk", "gv", "gz"))
            with ExitStack() as core:
                kbeg, kout, vb = (sb(n, [P, GH, TB, P], on=core) for n in ("kbeg", "kout", "vb"))
                eg, dm, kb = (sb(n, [P, 2, SEQ], on=core) for n in ("eg", "dm", "kb"))
                intraT, xT = sb("intraT", [P, GH, SEQ], on=core), sb("xT", [P, GH, SEQ], on=core)
                after_core = sb("after_core", [P, 1], on=core)
            with ExitStack() as early:
                zp = sb("zp", [P, 2, SEQ + GT - 1], on=early)
                cg = sb("cg", [P, NC, SEQ], on=early)
                za = sb("za", [P, 3 * NA, SEQ], on=early)
                qkr2 = sb("qkr2", [P, 2 * NA, SEQ], F32R, on=early)
                vaug2 = sb("vaug2", [P, AH, TB, P], on=early)
                probs2 = sb("probs2", [P, TB, SEQ], on=early)
                diag2 = sb("diag2", [P, TB, P], F32R, on=early)
                ta, tb2 = sb("ta", [P, SEQ], on=early), sb("tb2", [P, SEQ], on=early)
                mx2 = sb("mx2", [P, 2, TB], on=early)
            on.enter_context(nc.sbuf_tensor("hold_core", [P, 2 * 3 * SEQ + (3 + 2) * GH * SEQ + 1], F32))
            ya = sb("ya", [P, NA, SEQ], on=on)
            yc = sb("yc", [P, NC, SEQ], on=on)
            ypad = sb("ypad", [P, NC, SEQ + CT - 1], on=on)
            rope2 = sb("rope2", [P, 2, SEQ], on=on)
            perm2 = sb("perm2", [P, P], on=on)
            wide = SEQ + SEQ - P
            mask_s, mask_t, times = (sb(n, [P, wide], BF16, on=on) for n in ("mask_s", "mask_t", "times"))
            ident_b = sb("ident_b", [P, P], BF16, on=on)
            tri = sb("tri", [P, P], on=on)
            lev = sb("lev", [P, LEVELS, P], BF16, on=on)
            wab, wab_hi, wab_lo = sb("wab", [P, KD, 2 * GH], on=on), sb("wab_hi", [P, KD, 2 * GH], F32R, on=on), sb("wab_lo", [P, KD, 2 * GH], F32R, on=on)
            cols = {n: sb(f"col_{n}", [P, TB, GH], on=on) for n in
                    ("a", "ax", "e", "l", "g", "beta", "gc", "egc", "dg", "egl", "beg", "b")}
            rcol = sb("rcol", [P, TB], on=on)
            expa = sb("expa", [P, GH], on=on)
            eg_last = sb("eg_last", [P, GH, NCH], on=on)
        lt, p1, mrs2, msq2 = eg, dm, kb, sqt
        vn, state = ypad[:, 0, 0:GH * P].rearrange("p (h d) -> p h d", d=P), ypad[:, 1, 0:GH * P].rearrange("p (h d) -> p h d", d=P)
        og = xT
        gqkv = [t[:, i, :] for t in (gq, gk, gv) for i in range(GH)]

        def by_rows(src):
            return src.rearrange("(r p) -> r p", p=P)

        def setup_rows():
            for dst, name in ((ident, "c_ident"), (blk, "c_blk"), (perm, "c_perm")):
                yield dst[:], D[name]
            yield rope[:], D["c_rope"].rearrange("a p n -> p a n")
            for l in range(DEPTH):
                for b, names in enumerate((("attn_norm_g", "ffn_norm_g"), ("attn_pre_norm_2", "ffn_pre_norm_2"))):
                    for i, name in enumerate(names):
                        g = (b * DEPTH + l) * 2 + i
                        yield rows[g * KD:(g + 1) * KD, 0, :], by_rows(D[name][l])
                for i, name in enumerate(("attn_post_norm_2", "ffn_post_norm_2")):
                    g = GENS + 2 * l + i
                    yield rows[g * KD:(g + 1) * KD, 0, :], by_rows(D[name][l])
                a = 1 + 4 * l
                for i, name in enumerate(("q_norm_g", "k_norm_g")):
                    for r in range(2):
                        yield rows[i:i + 1, a, r * HD:(r + 1) * HD], D[name][l:l + 1, :]
                yield rows[2:2 + NS, a, :], by_rows(D["sg_norm_g"][l].rearrange("h d -> (h d)"))
                yield rows[2 + NS:2 + NS + NQ, a, :], by_rows(D["attn_out_g"][l])
                yield rows[2 + NS + NQ:2 + 2 * NS + NQ, a, :], by_rows(D["sg_out_g"][l])
                yield rows[0:2 * NF, a + 1, :], by_rows(D["conv_w"][l, 0])
                yield rows[2 * NF:4 * NF, a + 1, :], by_rows(D["conv_w"][l, 1])
                yield rows[0:2 * NF, a + 2, :], by_rows(D["conv_w"][l, 2])
                yield rows[2 * NF:4 * NF, a + 2, :], by_rows(D["conv_b"][l])
                yield rows[D_DW:D_BIAS, a + 3, :], by_rows(D["conv_dw_2"][l].rearrange("t c -> (t c)"))
                for at, name in ((D_BIAS, "conv_dw_bias_2"), (D_LNG, "conv_norm_gain_2"), (D_LNB, "conv_norm_bias_2")):
                    yield rows[at:at + NC, a + 3, :], by_rows(D[name][l])
                yield rows[D_SC:D_ON, a + 3, :], by_rows(D["gdn_short_conv_2"][l].rearrange("t c -> (t c)"))
                yield rows[D_ON:N_PD, a + 3, :], by_rows(D["gdn_out_norm_2"][l])
            for i, name in enumerate(("gdn_a_log_2", "gdn_dt_bias_2")):
                yield gate_par[:, i, :, :], D[name].unsqueeze(0).to_broadcast([P, DEPTH, GH])

        SETUP = [16 * sum(1 for _ in setup_rows())]

        wv = {n: D[n].rearrange("l (k p) n -> l p k n", p=P) for n in
              ("w_in", "w_o", "w_up", "w_down", "w_in_2", "w_out_2", "w_gate_2", "w_up_2", "w_down_2")}

        def weight(name, layer, k0, kt, col):
            return wv[name][ds(layer, 1), :, k0:k0 + kt, ds(col, P)].rearrange("l p k n -> p (l k) n")

        def plan1(layer):
            yield 0, NS, KD, lambda j, s: weight("w_in", layer, 0, KD, j * 2 * P + (N_IN - 2 * NS + s) * P)
            yield NS, PAIRS_IN - NS, KD, lambda j, s: weight("w_in", layer, 0, KD, j * 2 * P + s * P)
            yield OFF_O, PAIRS_O, KD, lambda j, s: weight("w_o", layer, 0, KD, j * 2 * P + s * P)
            for hf in range(2):
                yield OFF_UP[hf], PAIRS_UP, KD, lambda j, s, hf=hf: weight(
                    "w_up", layer, 0, KD, j * P + (s * NF + hf * HALF) * P)
                yield OFF_DOWN[hf], PAIRS_DOWN, HALF, lambda j, s, hf=hf: weight(
                    "w_down", layer, hf * HALF, HALF, j * 2 * P + s * P)

        mixed = [t[:, i, :] for t, n in ((ya, NA), (yc, NC), (og, GH)) for i in range(n)]

        def plan2(layer):
            for at, n, tile0 in ((0, 2 * GH, 3 * NA + 2 * NC), (2 * GH, NC, 3 * NA), (2 * GH + NC, 3 * NA // 2, 0)):
                yield at, n, KD, lambda j, s, t=tile0: weight("w_in_2", layer, 0, KD, j * 2 * P + (t + s) * P)
            yield OFF_O2, PAIRS_O, KD, lambda j, s: weight("w_out_2", layer, 0, KD, j * 2 * P + s * P)
            for hf in range(2):
                yield OFF_UP2[hf], PAIRS_UP, KD, lambda j, s, hf=hf: weight(
                    ("w_gate_2", "w_up_2")[s], layer, 0, KD, j * P + hf * HALF * P)
                yield OFF_DOWN2[hf], PAIRS_DOWN, HALF, lambda j, s, hf=hf: weight(
                    "w_down_2", layer, hf * HALF, HALF, j * 2 * P + s * P)

        block = ctx.enter_context(nc.Block())

        @block.sync
        def _(sp):
            def load(v, s, kt, src):
                sp.wait_ge(w_lo_ready.sem, v * 2 + (s + 1))
                sp.wait_ge(consts_made.sem, 1)
                sp.dma_start(raw[s][:, 0:kt, :], src).then_inc(w_loaded[s].sem, 16)

            sp.dma_start(xs[:], D["x"][0].rearrange("(t p) d -> p t d", p=P)).then_inc(x_loaded.sem, 16)
            with sp.Fori(0, DEPTH) as L:
                for off, n, kt, src in plan1(L):
                    with sp.Fori(0, n) as j:
                        for s in range(2):
                            load(L * PAIRS1 + off + j, s, kt, src(j, s))
            with sp.Fori(0, DEPTH) as L:
                for off, n, kt, src in plan2(L):
                    with sp.Fori(0, n) as j:
                        for s in range(2):
                            load(BASE2 + L * PAIRS2 + off + j, s, kt, src(j, s))
            for s in range(2):
                load(PAIRS, s, KD, weight("w_in", 0, 0, KD, s * P))
            for tb in range(TB):
                for hf in range(2):
                    sp.wait_ge(out_kept.sem, tb * 2 + hf + 1)
                    sp.dma_start(out[0, tb * P:(tb + 1) * P, hf * SEQ:(hf + 1) * SEQ],
                                 xs[:, tb, hf * SEQ:(hf + 1) * SEQ]).then_inc(out_stored.sem, 16)
            sp.wait_ge(out_stored.sem, TB * 2 * 16)
            for s in range(2):
                sp.wait_ge(w_loaded[s].sem, 16 * (PAIRS + 1))

        @block.gpsimd
        def _(pool):
            pool.sem_inc(w_lo_ready.sem, 2)

            def low(v, s, kt):
                pool.wait_ge(w_hi_ready.sem, v * 2 + (s + 1))
                nc.gpsimd.tensor_tensor(wlo[s][:, 0:kt, :], raw[s][:, 0:kt, :], whi[s][:, 0:kt, :].bitcast(F32),
                                        ALU.subtract).then_inc(w_lo_ready.sem, 1)

            with pool.Fori(0, DEPTH) as L:
                for off, n, kt, _src in plan1(L):
                    with pool.Fori(0, n) as j:
                        for s in range(2):
                            low(L * PAIRS1 + off + j, s, kt)

            pool.wait_ge(h_ready.sem, h_ready.at(2 * DEPTH, KD - 1))
            for dst, name in ((mask_s, "c_mask_s"), (mask_t, "c_mask_t"), (times, "c_times"), (ident_b, "c_ident")):
                pool.dma_start(dst[:], D[name]).then_inc(c2_cast.sem, 16)
            pool.dma_start(lev[:], D["c_lev"].rearrange("a p n -> p a n")).then_inc(c2_cast.sem, 16)
            with pool.Fori(0, DEPTH) as L:
                for off, n, kt, _src in plan2(L):
                    with pool.Fori(0, n) as j:
                        for s in range(2):
                            low(BASE2 + L * PAIRS2 + off + j, s, kt)
            pool.wait_ge(c2_cast.sem, 5 * 16)

        @block.tensor
        def _(pe):
            pe.sem_inc(unit_done.sem, 2)

            def unit(v, s, kt, rhs_hi, rhs_lo, wait_rhs):
                pe.wait_ge(w_lo_ready.sem, v * 2 + (s + 3))
                pe.wait_ge(acc_free.sem, v * 2 + (s + 1))
                for k in range(kt):
                    wait_rhs(k, s)
                    for n, (w, r) in enumerate(((whi, rhs_hi), (whi, rhs_lo), (wlo, rhs_hi))):
                        mm = pe.matmul(ps[:, ACC[s], :], w[s][:, k, :], r[:, k, :],
                                       start=(k == 0 and n == 0), stop=(k == kt - 1 and n == 2))
                mm.then_inc(unit_done.sem, 1)

            def norm_sum(gen):
                pe.wait_ge(ssq_done.sem, ssq_done.at(gen, KD - 1))
                pe.matmul(ps[:, STAT[0], :], ones[:], ssq[:], start=True, stop=True).then_inc(stat_ready.sem, 1)

            def need_h(gen):
                def wait(k, s):
                    if s == 0:
                        pe.wait_ge(h_ready.sem, h_ready.at(gen, k))
                return wait

            pe.wait_ge(setup_loaded.sem, SETUP[0])
            pe.wait_ge(consts_made.sem, 1)
            for i, r in enumerate(ROWS):
                bank = TRN[i % 2]
                if i >= 2:
                    pe.wait_ge(params_kept.sem, i - 1)
                pe.transpose(ps[:, bank, 0:r], rows[0:r, i, :], ident[0:r, 0:r]).then_inc(params_turned.sem, 1)
            pe.wait_ge(x_loaded.sem, 16)
            for n in range(KD):
                if n >= 2:
                    pe.wait_ge(x_ready.sem, n - 1)
                for tb in range(TB):
                    mm = pe.transpose(ps[:, ROT[n % 2], tb * P:(tb + 1) * P], xs[:, tb, n * P:(n + 1) * P], ident[:])
                mm.then_inc(x_turned.sem, 1)

            with pe.Fori(0, DEPTH) as L:
                V = L * PAIRS1
                norm_sum(L * 2)
                with pe.Fori(0, PAIRS_IN) as j:
                    for s in range(2):
                        unit(V + j, s, KD, h_hi, h_lo, need_h(L * 2))

                pe.wait_ge(sgw_loaded.sem, L * 16 + 16)
                for b in range(2):
                    for i in range(4):
                        mm = pe.transpose(ps[:, TRN[b], i * P:(i + 1) * P], sgw[:, 4 * b + i, :], ident[:])
                    mm.then_inc(wT_ready.sem, 1)
                for t in range(NS):
                    pe.wait_ge(vvsq_ready.sem, vvsq_ready.at(L, t))
                    if t == 0:
                        pe.wait_ge(rstd_ready.sem, rstd_ready.at(L * 2, 0))
                    if t >= 2:
                        pe.wait_ge(vvrs_ready.sem, vvrs_ready.at(L, t - 2))
                    pe.matmul(ps[:, STAT[t % 2], :], blk[:], msq[:, t % 2, :], start=True, stop=True)\
                        .then_inc(vvstat_ready.sem, 1)
                for t in range(NS):
                    pe.wait_ge(vvn_ready.sem, vvn_ready.at(L, t))
                    if t < 2:
                        pe.wait_ge(wT_kept.sem, wT_kept.at(L, t))
                    else:
                        pe.wait_ge(vvT_kept.sem, vvT_kept.at(L, t - 2))
                    for c in range(TB):
                        mm = pe.transpose(ps[:, TRN[t % 2], c * P:(c + 1) * P], vv[:, t, c * P:(c + 1) * P], ident[:])
                    mm.then_inc(vvT_ready.sem, 1)
                    pe.wait_ge(vvT_kept.sem, vvT_kept.at(L, t))
                    if t == 0:
                        pe.wait_ge(wT_kept.sem, wT_kept.at(L, 1))
                    if t >= 2:
                        pe.wait_ge(mix_used.sem, mix_used.at(L, t - 2))
                    for c in range(TB):
                        for r in range(2):
                            mm = pe.matmul(ps[64 * r:64 * r + 64, ROT[t % 2], c * P:(c + 1) * P],
                                           vvT[:, c, t * P + 64 * r:t * P + 64 * r + 64], wT[:, 2 * t + r, :],
                                           start=True, stop=True)
                    mm.then_inc(mix_ready.sem, 1)
                for i in range(NQ + 1):
                    pe.wait_ge(qksq_ready.sem, qksq_ready.at(L, i))
                    if i < 2:
                        pe.wait_ge(vvrs_ready.sem, vvrs_ready.at(L, NS - 2 + i))
                    else:
                        pe.wait_ge(qkrs_ready.sem, qkrs_ready.at(L, i - 2))
                    pe.matmul(ps[:, STAT[i % 2], :], blk[:], msq[:, i % 2, :], start=True, stop=True)\
                        .then_inc(qkstat_ready.sem, 1)
                for i in range(NQ + 1):
                    pe.wait_ge(qkn_ready.sem, qkn_ready.at(L, i))
                    if i < 2:
                        pe.wait_ge(mix_used.sem, mix_used.at(L, NS - 2 + i))
                    else:
                        pe.wait_ge(rot_used.sem, rot_used.at(L, i - 2))
                    pe.matmul(ps[:, ROT[i % 2], :], perm[:], zk[:] if i == 0 else zq[:, i - 1, :],
                              start=True, stop=True).then_inc(rot_ready.sem, 1)
                pe.wait_ge(acc_free.sem, V * 2 + 2 * PAIRS_IN + 2)
                pe.wait_ge(vvT_kept.sem, vvT_kept.at(L, NS - 1))
                for kt in range(TB):
                    mm = pe.transpose(ps[:, TRN[0], kt * P:(kt + 1) * P], zv[:, kt * P:(kt + 1) * P], ident[:])
                mm.then_inc(vT_ready.sem, 1)

                def scores(h):
                    t, r, g = h // 2, 64 * (h % 2), h // GROUP
                    for b in range(2):
                        if h == 0:
                            pe.wait_ge(qr_ready.sem, qr_ready.at(L, NQ))
                            pe.wait_ge(qkrs_ready.sem, qkrs_ready.at(L, NQ))
                        if h or b:
                            pe.wait_ge(S_used.sem, S_used.at(L, 2 * h + b - 1))
                        for i in range(2):
                            qb = 2 * b + i
                            mm = pe.matmul(ps[:, STAT[i], :], qr[r:r + 64, t, qb * P:(qb + 1) * P],
                                           kr[g][r:r + 64, :], start=True, stop=True)
                        mm.then_inc(S_ready.sem, 1)

                def probs_values(h, kt):
                    pe.wait_ge(P_ready.sem, P_ready.at(L, h * TB + kt))
                    if kt == 0 and h >= 2:
                        pe.wait_ge(ao_ready.sem, ao_ready.at(L, h - 2))
                    if kt == 0 and h == 0:
                        pe.wait_ge(vaug_ready.sem, vaug_ready.at(L, 0))
                    pe.matmul(ps[:, TRN[h % 2], :], vaug[:, h // GROUP, h % 2, kt, :], probs[:, kt, :],
                              start=(kt == 0), stop=(kt == TB - 1)).then_inc(PV_done.sem, 1)

                scores(0)
                for h in range(NH):
                    t, r, g = h // 2, 64 * (h % 2), h // GROUP
                    if h + 1 < NH:
                        scores(h + 1)
                    for kt in range(TB):
                        if kt == 0:
                            pe.wait_ge(diag_ready.sem, diag_ready.at(L, h))
                        n = h * TB + kt
                        if n >= 2:
                            pe.wait_ge(P_ready.sem, P_ready.at(L, n - 2))
                        else:
                            pe.wait_ge(rope_ready.sem, rope_ready.at(L, NQ))
                        pe.matmul(ps[:, ROT[kt % 2], :], kd[g][r:r + 64, kt * P:(kt + 1) * P], zq[r:r + 64, t, :],
                                  start=True, stop=False)
                        pe.matmul(ps[:, ROT[kt % 2], :], negones[:], diag[:].rearrange("p b q -> p (b q)"),
                                  start=False, stop=True).then_inc(ST_ready.sem, 1)
                        if kt >= 1:
                            probs_values(h, kt - 1)
                    probs_values(h, TB - 1)

                for i in range(NQ + NS):
                    pe.wait_ge(osq_ready.sem, osq_ready.at(L, i))
                    if i == 0:
                        pe.wait_ge(S_used.sem, S_used.at(L, 2 * NH - 1))
                    pe.matmul(ps[:, STAT[i // NQ], :], ones[:], msq[:, i % 2, :],
                              start=(i % NQ == 0), stop=(i % NQ == NQ - 1)).then_inc(osq_used.sem, 1)

                def need_merged(k, s):
                    if s == 0:
                        pe.wait_ge(merged_ready.sem, merged_ready.at(L, k))

                with pe.Fori(0, PAIRS_O) as j:
                    for s in range(2):
                        unit(V + OFF_O + j, s, KD, a_hi, a_lo, need_merged)
                norm_sum(L * 2 + 1)
                for hf in range(2):
                    with pe.Fori(0, PAIRS_UP) as j:
                        for s in range(2):
                            unit(V + OFF_UP[hf] + j, s, KD, h_hi, h_lo, need_h(L * 2 + 1))

                    def need_a(k, s, hf=hf):
                        if s == 0:
                            pe.wait_ge(a_ready.sem, a_ready.at(L, hf * HALF + k))

                    with pe.Fori(0, PAIRS_DOWN) as j:
                        for s in range(2):
                            unit(V + OFF_DOWN[hf] + j, s, HALF, a_hi, a_lo, need_a)

            with pe.Fori(0, DEPTH) as L:
                V = BASE2 + L * PAIRS2
                G = L * 2 + 2 * DEPTH
                norm_sum(G)
                with pe.Fori(0, PAIRS_IN2) as j:
                    for s in range(2):
                        unit(V + j, s, KD, h_hi, h_lo, need_h(G))
                pe.wait_ge(rstd_ready.sem, rstd_ready.at(G, 0))
                for tb in range(TB):
                    mm = pe.transpose(ps[:, TRN[0], tb * P:(tb + 1) * P], rstd[:, tb * P:(tb + 1) * P], ident[:])
                mm.then_inc(rcol_ready.sem, 1)
                pe.wait_ge(wab_split.sem, wab_split.at(L, 1))
                for tb in range(TB):
                    for k in range(KD):
                        for n, (r, w) in enumerate(((h_hi, wab_hi), (h_hi, wab_lo), (h_lo, wab_hi))):
                            mm = pe.matmul(ps[:, TRN[1], tb * 2 * GH:(tb + 1) * 2 * GH], r[:, k, tb * P:(tb + 1) * P],
                                           w[:, k, :], start=(k == 0 and n == 0), stop=(k == KD - 1 and n == 2))
                mm.then_inc(ab_ready.sem, 1)
                pe.wait_ge(acc_free.sem, V * 2 + 2 * PAIRS_IN2 + 2)
                pe.wait_ge(c2_loaded.sem, 3 * 16)
                for i in range(2 * NA):
                    if i >= 2:
                        pe.wait_ge(rot2_used.sem, rot2_used.at(L, i - 2))
                    pe.matmul(ps[:, ROT[i % 2], :], perm2[:], za[:, i, :], start=True, stop=True).then_inc(rot2_ready.sem, 1)
                pe.wait_ge(rcol_kept.sem, rcol_kept.at(L, 0))
                pe.wait_ge(gate_in.sem, gate_in.at(L, 0))
                for i in range(NA):
                    for kt in range(TB):
                        mm = pe.transpose(ps[:, TRN[i], kt * P:(kt + 1) * P], za[:, 2 * NA + i, kt * P:(kt + 1) * P], ident[:])
                    mm.then_inc(v2T_ready.sem, 1)

                pe.wait_ge(c2_cast.sem, 5 * 16)

                def scores(h):
                    t, r = h // 2, 64 * (h % 2)
                    for b in range(2):
                        if h == 0:
                            pe.wait_ge(qkr2_ready.sem, qkr2_ready.at(L, 2 * NA - 1))
                        if h or b:
                            pe.wait_ge(S2_used.sem, S2_used.at(L, 2 * h + b - 1))
                        for i in range(2):
                            qb = 2 * b + i
                            pe.matmul(ps[:, STAT[i], :], qkr2[r:r + 64, t, qb * P:(qb + 1) * P], qkr2[r:r + 64, NA + t, :],
                                      start=True, stop=False)
                            mm = pe.matmul(ps[:, STAT[i], :], ident_b[:], mask_s[:, (TB - 1 - qb) * P:(TB - 1 - qb) * P + SEQ],
                                           start=False, stop=True)
                        mm.then_inc(S2_ready.sem, 1)

                def probs_values(h, kt):
                    pe.wait_ge(P2_ready.sem, P2_ready.at(L, h * TB + kt))
                    if kt == 0 and h >= 2:
                        pe.wait_ge(ya_ready.sem, ya_ready.at(L, h - 2))
                    if kt == 0 and h == 0:
                        pe.wait_ge(vaug2_ready.sem, vaug2_ready.at(L, NA - 1))
                    pe.matmul(ps[:, TRN[h % 2], :], vaug2[:, h, kt, :], probs2[:, kt, :],
                              start=(kt == 0), stop=(kt == TB - 1)).then_inc(PV2_done.sem, 1)

                scores(0)
                for h in range(AH):
                    t, r = h // 2, 64 * (h % 2)
                    if h + 1 < AH:
                        scores(h + 1)
                    for kt in range(TB):
                        n = h * TB + kt
                        if kt == 0:
                            pe.wait_ge(diag2_ready.sem, diag2_ready.at(L, h))
                        if n >= 2:
                            pe.wait_ge(E2_ready.sem, E2_ready.at(L, n - 2))
                        pe.matmul(ps[:, ROT[kt % 2], :], za[r:r + 64, NA + t, kt * P:(kt + 1) * P], za[r:r + 64, t, :],
                                  start=True, stop=False)
                        pe.matmul(ps[:, ROT[kt % 2], :], negones[:], diag2[:].rearrange("p b q -> p (b q)"),
                                  start=False, stop=False)
                        pe.matmul(ps[:, ROT[kt % 2], :], ident_b[:], mask_t[:, (TB - 1 - kt) * P:(TB - 1 - kt) * P + SEQ],
                                  start=False, stop=True).then_inc(ST2_ready.sem, 1)
                        if kt >= 1:
                            probs_values(h, kt - 1)
                    probs_values(h, TB - 1)

                for i in range(NC):
                    pe.wait_ge(dw_ready.sem, dw_ready.at(L, i))
                    if i == 0:
                        pe.wait_ge(S2_used.sem, S2_used.at(L, 2 * AH - 1))
                    mm = pe.matmul(ps[:, STAT[0], :], ones[:], yc[:, i, :], start=(i == 0), stop=(i == NC - 1))
                mm.then_inc(mean_ready.sem, 1)
                for i in range(NC):
                    pe.wait_ge(lnsq.sem, lnsq.at(L, i))
                    pe.matmul(ps[:, STAT[1], :], ones[:], msq2[:, i % 2, :], start=(i == 0), stop=(i == NC - 1))\
                        .then_inc(lnsq_used.sem, 1)

                for i in range(2 * GH):
                    pe.wait_ge(l2sq.sem, l2sq.at(L, i))
                    if i < 2:
                        pe.wait_ge(ln_rs.sem, ln_rs.at(L, 0))
                    else:
                        pe.wait_ge(l2rs.sem, l2rs.at(L, i - 2))
                    pe.matmul(ps[:, STAT[i % 2], :], ones[:], msq2[:, i % 2, :], start=True, stop=True).then_inc(l2stat.sem, 1)
                pe.wait_ge(g_ready.sem, g_ready.at(L, 0))
                pe.wait_ge(ya_ready.sem, ya_ready.at(L, AH - 1))
                pe.wait_ge(c2_loaded.sem, 3 * 16)
                NCOL = TB * GH
                gflat = cols["g"][:].rearrange("p t h -> p (t h)")
                pe.matmul(ps[:, TRN[0], 0:NCOL], tri[:], gflat, start=True, stop=True)
                pe.matmul(ps[:, TRN[0], NCOL:2 * NCOL], blk[:], gflat, start=True, stop=True).then_inc(G_ready.sem, 1)
                pe.wait_ge(l2n.sem, l2n.at(L, 2 * GH - 1))
                pe.wait_ge(beg_ready.sem, beg_ready.at(L, 0))

                def head_in(h):
                    if h >= 2:
                        pe.wait_ge(head_ready.sem, head_ready.at(L, h - 2))
                    for tb in range(TB):
                        mm = pe.matmul(ps[:, ROT[h % 2], tb * P:(tb + 1) * P], cols["g"][:, tb, h:h + 1].to_broadcast([P, P]),
                                       tri[:], start=True, stop=True)
                    mm.then_inc(grow_ready.sem, 1)
                    for tb in range(TB):
                        mm = pe.matmul(ps[:, STAT[h % 2], tb * P:(tb + 1) * P], cols["beta"][:, tb, h:h + 1].to_broadcast([P, P]),
                                       ident[:], start=True, stop=True)
                    mm.then_inc(brow_ready.sem, 1)
                    if h >= 1:
                        pe.wait_ge(turned_used.sem, turned_used.at(L, h - 1))
                    for tb in range(TB):
                        mm = pe.transpose(ps[:, TRN[0], tb * P:(tb + 1) * P], gk[:, h, tb * P:(tb + 1) * P], ident[:])
                    mm.then_inc(kT_ready.sem, 1)
                    for tb in range(TB):
                        mm = pe.transpose(ps[:, TRN[1], tb * P:(tb + 1) * P], gv[:, h, tb * P:(tb + 1) * P], ident[:])
                    mm.then_inc(gvT_ready.sem, 1)

                def head_products(h):
                    pe.wait_ge(kb_ready.sem, kb_ready.at(L, h))
                    if h >= 1:
                        pe.wait_ge(head_ready.sem, head_ready.at(L, h - 1))
                    for tb in range(TB):
                        mm = pe.matmul(ps[:, ACC[0], tb * P:(tb + 1) * P], gk[:, h, tb * P:(tb + 1) * P],
                                       kb[:, h % 2, tb * P:(tb + 1) * P], start=True, stop=True)
                    mm.then_inc(kk_ready.sem, 1)
                    for tb in range(TB):
                        mm = pe.matmul(ps[:, ACC[1], tb * P:(tb + 1) * P], gk[:, h, tb * P:(tb + 1) * P],
                                       gq[:, h, tb * P:(tb + 1) * P], start=True, stop=True)
                    mm.then_inc(qk_ready.sem, 1)

                head_in(0)
                for h in range(GH):
                    if h + 1 < GH:
                        head_in(h + 1)
                    head_products(h)

                def level_first(n):
                    h = n % GH
                    pe.wait_ge(lt_ready.sem, lt_ready.at(L, n))
                    if n >= 2:
                        pe.wait_ge(p1_kept.sem, p1_kept.at(L, n - 2))
                    for tb in range(TB):
                        c = slice(tb * P, (tb + 1) * P)
                        mm = pe.matmul(ps[:, ROT[n % 2], c], lt[:, n % 2, c], gk[:, h, c], start=True, stop=True)
                    mm.then_inc(p1_ready.sem, 1)

                def level_second(n):
                    h = n % GH
                    pe.wait_ge(p1_kept.sem, p1_kept.at(L, n))
                    if n >= 2:
                        pe.wait_ge(x_new.sem, x_new.at(L, n - 2))
                    for tb in range(TB):
                        c = slice(tb * P, (tb + 1) * P)
                        mm = pe.matmul(ps[:, STAT[n % 2], c], xT[:, h, c], p1[:, n % 2, c], start=True, stop=True)
                    mm.then_inc(xp_ready.sem, 1)
                    for tb in range(TB):
                        c = slice(tb * P, (tb + 1) * P)
                        mm = pe.matmul(ps[:, TRN[n % 2], c], p1[:, n % 2, c], xT[:, h, c], start=True, stop=True)
                    mm.then_inc(xpt_ready.sem, 1)

                pe.wait_ge(head_ready.sem, head_ready.at(L, GH - 1))
                for n in range(GH * LEVELS + 1):
                    if n < GH * LEVELS:
                        level_first(n)
                    if n >= 1:
                        level_second(n - 1)
                for h in range(GH):
                    pe.wait_ge(x_new.sem, x_new.at(L, GH * (LEVELS - 1) + h))
                    if h == 0:
                        pe.wait_ge(x_new.sem, x_new.at(L, GH * LEVELS - 1))
                    if h >= 2:
                        pe.wait_ge(uu_kept.sem, uu_kept.at(L, h - 2))
                    for tb in range(TB):
                        mm = pe.matmul(ps[:, ROT[h % 2], tb * P:(tb + 1) * P], xT[:, h, tb * P:(tb + 1) * P], vb[:, h, tb, :],
                                       start=True, stop=True)
                    mm.then_inc(uu_ready.sem, 1)
                    if h >= 2:
                        pe.wait_ge(ww_kept.sem, ww_kept.at(L, h - 2))
                    for tb in range(TB):
                        mm = pe.matmul(ps[:, STAT[h % 2], tb * P:(tb + 1) * P], kbeg[:, h, tb, :], xT[:, h, tb * P:(tb + 1) * P],
                                       start=True, stop=True)
                    mm.then_inc(ww_ready.sem, 1)
                pe.wait_ge(uu_kept.sem, uu_kept.at(L, GH - 1))
                pe.wait_ge(ww_kept.sem, ww_kept.at(L, GH - 1))
                for c in range(NCH):
                    tb, r = c // 2, CH * (c % 2)
                    at = slice(c * CH, (c + 1) * CH)
                    pe.wait_ge(state_ready.sem, state_ready.at(L, c))
                    wTf = kbeg[:].rearrange("p h t d -> p h (t d)")
                    for h in range(GH):
                        mm = pe.matmul(ps[r:r + CH, ROT[c % 2], h * P:(h + 1) * P], wTf[:, h, at], state[:, h, :],
                                       start=True, stop=True)
                    mm.then_inc(ws_ready.sem, 1)
                    if c >= 2:
                        pe.wait_ge(o_kept.sem, o_kept.at(L, c - 2))
                    pe.wait_ge(vn_ready.sem, vn_ready.at(L, c))
                    for h in range(GH):
                        pe.matmul(ps[:, STAT[c % 2], h * CH:(h + 1) * CH], state[:, h, :], gq[:, h, at], start=True, stop=False)
                        mm = pe.matmul(ps[:, STAT[c % 2], h * CH:(h + 1) * CH], vn[r:r + CH, h, :], intraT[r:r + CH, h, at],
                                       start=False, stop=True)
                    mm.then_inc(o_ready.sem, 1)
                    for h in range(GH):
                        mm = pe.matmul(ps[:, TRN[c % 2], h * P:(h + 1) * P], kout[r:r + CH, h, tb, :], vn[r:r + CH, h, :],
                                       start=True, stop=True)
                    mm.then_inc(ds_ready.sem, 1)
                for h in range(GH):
                    pe.wait_ge(ogsq.sem, ogsq.at(L, h))
                    if h >= 2:
                        pe.wait_ge(ogrs.sem, ogrs.at(L, h - 2))
                    pe.matmul(ps[:, STAT[h % 2], :], ones[:], msq2[:, h % 2, :], start=True, stop=True).then_inc(ogstat.sem, 1)

                def need_merged2(k, s):
                    if s == 0:
                        pe.wait_ge(merged2_ready.sem, merged2_ready.at(L, k))

                def post_sum(i):
                    pe.wait_ge(yssq_done.sem, yssq_done.at(L, i * KD + KD - 1))
                    pe.matmul(ps[:, STAT[1], :], ones[:], prod[:], start=True, stop=True).then_inc(ystat_ready.sem, 1)

                with pe.Fori(0, PAIRS_O) as j:
                    for s in range(2):
                        unit(V + OFF_O2 + j, s, KD, a_hi, a_lo, need_merged2)
                post_sum(0)
                norm_sum(G + 1)
                for hf in range(2):
                    with pe.Fori(0, PAIRS_UP) as j:
                        for s in range(2):
                            unit(V + OFF_UP2[hf] + j, s, KD, h_hi, h_lo, need_h(G + 1))

                    def need_a2(k, s, hf=hf):
                        if s == 0:
                            pe.wait_ge(a2_ready.sem, a2_ready.at(L, hf * HALF + k))

                    with pe.Fori(0, PAIRS_DOWN) as j:
                        for s in range(2):
                            unit(V + OFF_DOWN2[hf] + j, s, HALF, a_hi, a_lo, need_a2)
                post_sum(1)

            pe.wait_ge(h_ready.sem, h_ready.at(4 * DEPTH, KD - 1))
            for tb in range(TB):
                for hf in range(2):
                    i = tb * 2 + hf
                    if i >= 2:
                        pe.wait_ge(out_kept.sem, i - 1)
                    for n in range(4):
                        mm = pe.transpose(ps[:, ROT[i % 2], n * P:(n + 1) * P],
                                          x[:, 4 * hf + n, tb * P:(tb + 1) * P], ident[:])
                    mm.then_inc(out_turned.sem, 1)

        @block.scalar
        def _(act):
            order = Order(act, act_step.sem, consts_made)

            act.wait_ge(consts_made.sem, 1)
            count = 0
            for dst, src in setup_rows():
                act.dma_start(dst, src).then_inc(setup_loaded.sem, 16)
                count += 16
            assert count == SETUP[0]

            def hi_next(v, s, kt):
                act.wait_ge(w_loaded[s].sem, v * 16 + 16)
                act.wait_ge(unit_done.sem, v * 2 + (s + 1))
                act.activation(whi[s][:, 0:kt, :], raw[s][:, 0:kt, :], ACT.Copy).then_inc(w_hi_ready.sem, 1)

            def rs(dst, src, width, e=0):
                act.activation(lnt[:], src, ACT.Ln, bias=eps[:, e:e + 1], scale=1.0 / width).then_inc(act_step.sem, 1)
                order.n += 1
                act.wait_ge(act_step.sem, order.n)
                return act.activation(dst, lnt[:], ACT.Exp, scale=-0.5)

            def norm_rstd(gen):
                act.wait_ge(stat_ready.sem, stat_ready.at(gen, 0))
                order.settle()
                order.told(rs(rstd[:], ps[:, STAT[0], :], DM), rstd_ready, gen, 0)

            def split_h(gen, n, s, wait_x):
                wait_x()
                if not (isinstance(gen, int) and n < 2):
                    act.wait_ge(ssq_done.sem, ssq_done.at(gen, n - 2))
                act.activation(sqt[:, s, :], tile(x, n), ACT.Square).then_inc(sq_ready.sem, 1)
                act.activation(tile(h_hi, n), tile(x, n), ACT.Identity, scale=gain(gen * KD + n))\
                    .then_inc(hhi_ready.sem, 1)

            for s in range(2):
                hi_next(0, s, KD)
            act.wait_ge(consts_made.sem, 1)
            act.wait_ge(params_kept.sem, N_ROWS)
            for n in range(KD):
                split_h(0, n, n % 2, lambda n=n: act.wait_ge(x_ready.sem, n + 1))

            with act.Fori(0, DEPTH) as L:
                V = L * PAIRS1
                act.wait_ge(unit_done.sem, V * 2 + 2)
                act.wait_ge(params_kept.sem, N_ROWS)
                act.dma_start(sgw, D["sg_w"][ds(L, 1)].rearrange("l h p q -> p (l h) q")).then_inc(sgw_loaded.sem, 16)
                for r in range(2):
                    act.dma_start(sgb[64 * r:64 * r + 64, :, :],
                                  D["sg_b"][ds(L, 1), r::2, :].to_broadcast([64, NS, P])).then_inc(sgb_loaded.sem, 16)
                norm_rstd(L * 2)
                for i in range(N_IN):
                    hi_next(V + (i // 2 + 1), i % 2, KD)
                    if i < 2 * NS:
                        z = u[:, i, :] if i < NS else vv[:, i - NS, :]
                        act.wait_ge(acc_free.sem, V * 2 + i + 3)
                        order.told(act.activation(z, z, ACT.Gelu_apprx_tanh), gelu_ready, L, i)
                for b in range(2):
                    act.wait_ge(wT_ready.sem, wT_ready.at(L, b))
                    order.told(act.activation(wT[:, 4 * b:4 * b + 4, :].rearrange("q h p -> q (h p)"),
                                              ps[:, TRN[b], :], ACT.Copy), wT_kept, L, b)
                order.settle()

                def head_rs(i, sq, stat, rsig):
                    act.wait_ge(stat.sem, stat.at(L, i))
                    order.settle()
                    order.told(rs(mrs[:, i % 2, :], ps[:, STAT[i % 2], :], HD), rsig, L, i)

                for t in range(NS + 1):
                    if t < NS:
                        if t >= 2:
                            act.wait_ge(vvstat_ready.sem, vvstat_ready.at(L, t - 2))
                        order.told(act.activation(msq[:, t % 2, :], vv[:, t, :], ACT.Square), vvsq_ready, L, t)
                    if t >= 1:
                        if t - 1 >= 2:
                            act.wait_ge(vvn_ready.sem, vvn_ready.at(L, t - 3))
                        head_rs(t - 1, vvsq_ready, vvstat_ready, vvrs_ready)
                for t in range(NS):
                    act.wait_ge(vvT_ready.sem, vvT_ready.at(L, t))
                    order.told(act.activation(vvT[:, :, t * P:(t + 1) * P],
                                              ps[:, TRN[t % 2], :].rearrange("q (c f) -> q c f", f=P), ACT.Copy),
                               vvT_kept, L, t)
                act.wait_ge(acc_free.sem, V * 2 + 2 * PAIRS_IN + 2)
                for i in range(NQ + 2):
                    if i < NQ + 1:
                        if i < 2:
                            act.wait_ge(vvstat_ready.sem, vvstat_ready.at(L, NS - 2 + i))
                        else:
                            act.wait_ge(qkstat_ready.sem, qkstat_ready.at(L, i - 2))
                        z = zk[:] if i == 0 else zq[:, i - 1, :]
                        order.told(act.activation(msq[:, i % 2, :], z, ACT.Square), qksq_ready, L, i)
                    if i >= 1:
                        if i - 1 < 2:
                            act.wait_ge(vvn_ready.sem, vvn_ready.at(L, NS - 3 + i))
                        else:
                            act.wait_ge(qkn_ready.sem, qkn_ready.at(L, i - 3))
                        head_rs(i - 1, qksq_ready, qkstat_ready, qkrs_ready)
                act.wait_ge(rope_ready.sem, rope_ready.at(L, 0))
                for g in range(NKV):
                    for r in range(2):
                        for to in (kd, kr):
                            ins = act.activation(to[g][64 * r:64 * r + 64, :], zk[64 * g:64 * g + 64, :], ACT.Copy)
                            if (g, r) == (NKV - 1, 1) and to is kr:
                                order.told(ins, qr_ready, L, 0)
                            else:
                                order.step(ins)
                for t in range(NQ):
                    act.wait_ge(rope_ready.sem, rope_ready.at(L, t + 1))
                    order.told(act.activation(qr[:, t, :], zq[:, t, :], ACT.Copy), qr_ready, L, t + 1)
                act.wait_ge(vT_ready.sem, vT_ready.at(L, 0))
                for g in range(NKV):
                    for r in range(2):
                        ins = act.activation(vaug[:, g, r, :, 64 * r:64 * r + 64],
                                             ps[:, TRN[0], :].rearrange("q (k f) -> q k f", f=P)[:, :, 64 * g:64 * g + 64],
                                             ACT.Copy)
                        if (g, r) == (NKV - 1, 1):
                            act.wait_ge(vones_ready.sem, vones_ready.at(L, 0))
                            order.told(ins, vaug_ready, L, 0)
                        else:
                            order.step(ins)
                for h in range(NH):
                    r = 64 * (h % 2)
                    for kt in range(TB):
                        n = h * TB + kt
                        act.wait_ge(ST_ready.sem, ST_ready.at(L, n))
                        if n >= TB:
                            act.wait_ge(PV_done.sem, PV_done.at(L, n - TB))
                        else:
                            act.wait_ge(wT_ready.sem, wT_ready.at(L, 1))
                        order.told(act.activation(probs[:, kt, :], ps[:, ROT[kt % 2], :], ACT.Exp, scale=HD ** -0.5),
                                   P_ready, L, n)
                for i in range(NQ + NS):
                    if i < NQ:
                        act.wait_ge(ao_ready.sem, ao_ready.at(L, 2 * i + 1))
                        z = ao[:, i, :]
                    else:
                        act.wait_ge(sg_ready.sem, sg_ready.at(L, i - NQ))
                        z = u[:, i - NQ, :]
                    if i >= 2:
                        act.wait_ge(osq_used.sem, osq_used.at(L, i - 2))
                    else:
                        act.wait_ge(qkstat_ready.sem, qkstat_ready.at(L, NQ))
                    order.told(act.activation(msq[:, i % 2, :], z, ACT.Square), osq_ready, L, i)
                for b in range(2):
                    act.wait_ge(osq_used.sem, osq_used.at(L, b * NQ + NQ - 1))
                    order.settle()
                    order.told(rs(ors[:, b, :], ps[:, STAT[b], :], AW), ors_ready, L, b)
                for i in range(NQ + NS):
                    act.wait_ge(mtmp_ready.sem, mtmp_ready.at(L, i))
                    order.told(act.activation(a_hi[:, i, :], mtmp[:, i % 2, :], ACT.Copy), mhi_ready, L, i)

                order.restart()
                with act.Fori(0, PAIRS_O) as j:
                    for s in range(2):
                        hi_next(V + OFF_O + 1 + j, s, KD)
                        split_h(L * 2 + 1, j * 2 + s, s, lambda: act.wait_ge(acc_free.sem, (V + OFF_O + j) * 2 + (s + 3)))
                norm_rstd(L * 2 + 1)
                order.restart()
                for hf in range(2):
                    def feed(j, kt, hf=hf):
                        v = V + OFF_UP[hf] + j
                        for s in range(2):
                            hi_next(v + 1, s, kt)
                            act.wait_ge(acc_free.sem, v * 2 + (s + 3))
                            col = s * NF + hf * HALF + j
                            act.activation(cv[s][:], pad[s][:, 1:SEQ + 1], ACT.Identity,
                                           scale=param(pb, L, 2 * NF + col), bias=param(pc, L, 2 * NF + col))\
                                .then_inc(center_ready.sem, 1)
                        t = hf * HALF + j
                        act.wait_ge(conv_ready.sem, L * 2 * NF + 2 * t + 1)
                        act.activation(cv[0][:], cv[0][:], ACT.Silu).then_inc(silu_ready.sem, 1)
                        act.wait_ge(prod_ready.sem, prod_ready.at(L, t))
                        act.activation(tile(a_hi, j), prod[:], ACT.Copy).then_inc(ahi_ready.sem, 1)

                    with act.Fori(0, PAIRS_UP - 1) as j:
                        feed(j, KD)
                    feed(PAIRS_UP - 1, HALF)

                    def drain(j, kt, hf=hf):
                        v = V + OFF_DOWN[hf] + j
                        for s in range(2):
                            hi_next(v + 1, s, kt)
                            if hf == 1:
                                split_h(L * 2 + 2, j * 2 + s, s, lambda: act.wait_ge(acc_free.sem, v * 2 + (s + 3)))

                    with act.Fori(0, PAIRS_DOWN - 1) as j:
                        drain(j, HALF)
                    drain(PAIRS_DOWN - 1, KD)

            act.wait_ge(consts_made.sem, 1)
            act.wait_ge(h_ready.sem, h_ready.at(2 * DEPTH, KD - 1))
            act.dma_start(rope2[:], D["c_rope2"].rearrange("a p n -> p a n")).then_inc(c2_loaded.sem, 16)
            act.dma_start(perm2[:], D["c_perm2"]).then_inc(c2_loaded.sem, 16)
            act.dma_start(tri[:], D["c_tri"]).then_inc(c2_loaded.sem, 16)
            with act.Fori(0, DEPTH) as L:
                V = BASE2 + L * PAIRS2
                G = L * 2 + 2 * DEPTH
                act.wait_ge(consts_made.sem, 1)
                act.wait_ge(h_ready.sem, h_ready.at(G, KD - 1))
                act.dma_start(wab[:], D["w_in_2"].rearrange("l (k p) n -> l p k n", p=P)[ds(L, 1), :, :, N_IN2 * P:N_IN2 * P + 2 * GH]
                              .rearrange("l p k n -> p (l k) n")).then_inc(wab_loaded.sem, 16)
                norm_rstd(G)
                for i in range(N_IN2):
                    hi_next(V + (i // 2 + 1), i % 2, KD)
                    act.wait_ge(acc_free.sem, V * 2 + i + 3)
                    if i < NG:
                        order.told(act.activation(gqkv[i], zp[:, i % 2, GT - 1:GT - 1 + SEQ], ACT.Copy,
                                                  scale=param(pd, L, D_SC + (GT - 1) * NG + i)), sc_center, L, i)
                        act.wait_ge(sc_ready.sem, sc_ready.at(L, i))
                        order.told(act.activation(gqkv[i], gqkv[i], ACT.Silu), sc_silu, L, i)
                    elif i < NG + GH:
                        h = i - NG
                        order.told(act.activation(gz[:, h, :], gz[:, h, :], ACT.Silu), gate_ready, L, h)
                    elif NG + GH + NC <= i < NG + GH + 2 * NC:
                        t = i - NG - GH - NC
                        order.told(act.activation(cg[:, t, :], cg[:, t, :], ACT.Sigmoid), cg_ready, L, t)
                act.wait_ge(gate_in.sem, gate_in.at(L, 0))
                order.settle()
                order.step(act.activation(expa[:], gate_par[:, 0, ds(L, 1), :].rearrange("p l h -> p (l h)"), ACT.Exp))
                order.step(act.activation(cols["e"][:], cols["ax"][:], ACT.Exp, scale=-1.0))
                order.told(act.activation(cols["beta"][:], cols["b"][:], ACT.Exp, scale=-1.0), gate_e1, L, 0)
                order.settle()
                order.told(act.activation(cols["l"][:], cols["e"][:], ACT.Ln, bias=ones[:, 0:1]), gate_e2, L, 0)
                for i in range(2 * NA):
                    act.wait_ge(rope2_ready.sem, rope2_ready.at(L, i))
                    order.told(act.activation(qkr2[:, i, :], za[:, i, :], ACT.Copy), qkr2_ready, L, i)
                act.wait_ge(v2ones_ready.sem, v2ones_ready.at(L, 0))
                for i in range(NA):
                    act.wait_ge(v2T_ready.sem, v2T_ready.at(L, i))
                    for r in range(2):
                        ins = act.activation(vaug2[:, 2 * i + r, :, 64 * r:64 * r + 64],
                                             ps[:, TRN[i], :].rearrange("q (k f) -> q k f", f=P)[:, :, 64 * r:64 * r + 64], ACT.Copy)
                        if r:
                            order.told(ins, vaug2_ready, L, i)
                        else:
                            order.step(ins)
                for n in range(AH * TB):
                    act.wait_ge(ST2_ready.sem, ST2_ready.at(L, n))
                    if n >= TB:
                        act.wait_ge(PV2_done.sem, PV2_done.at(L, n - TB))
                    order.told(act.activation(probs2[:, n % TB, :], ps[:, ROT[n % 2], :], ACT.Exp, scale=64 ** -0.5), E2_ready, L, n)
                act.wait_ge(mean_ready.sem, mean_ready.at(L, 0))
                order.told(act.activation(lnt[:], ps[:, STAT[0], :], ACT.Copy, scale=1.0 / CC), mean_kept, L, 0)
                for i in range(NC):
                    act.wait_ge(centered.sem, centered.at(L, i))
                    order.told(act.activation(msq2[:, i % 2, :], yc[:, i, :], ACT.Square), lnsq, L, i)
                act.wait_ge(lnsq_used.sem, lnsq_used.at(L, NC - 1))
                order.settle()
                order.told(rs(mrs2[:, 0, :], ps[:, STAT[1], :], CC, 1), ln_rs, L, 0)
                for i in range(NC):
                    act.wait_ge(ln_scaled.sem, ln_scaled.at(L, i))
                    order.told(act.activation(yc[:, i, :], yc[:, i, :], ACT.Silu, bias=param(pd, L, D_LNB + i)), yc_ready, L, i)
                for i in range(2 * GH + 1):
                    if i < 2 * GH:
                        if i >= 2:
                            act.wait_ge(l2stat.sem, l2stat.at(L, i - 2))
                        order.told(act.activation(msq2[:, i % 2, :], gqkv[i], ACT.Square), l2sq, L, i)
                    if i >= 1:
                        act.wait_ge(l2stat.sem, l2stat.at(L, i - 1))
                        if i >= 3:
                            act.wait_ge(l2n.sem, l2n.at(L, i - 3))
                        else:
                            act.wait_ge(ln_scaled.sem, ln_scaled.at(L, NC - 1))
                        order.settle()
                        order.told(rs(mrs2[:, (i - 1) % 2, :], ps[:, STAT[(i - 1) % 2], :], 1), l2rs, L, i - 1)
                NCOL = TB * GH
                flat = lambda n: cols[n][:].rearrange("p t h -> p (t h)")
                act.wait_ge(gc_kept.sem, gc_kept.at(L, 0))
                order.step(act.activation(flat("egc"), flat("gc"), ACT.Exp))
                act.wait_ge(dg_ready.sem, dg_ready.at(L, 0))
                order.told(act.activation(flat("egl"), flat("dg"), ACT.Exp), eg_cols, L, 0)
                for h in range(GH):
                    act.wait_ge(gap_ready.sem, gap_ready.at(L, h))
                    if h >= 2:
                        act.wait_ge(head_ready.sem, head_ready.at(L, h - 2))
                    order.told(act.activation(eg[:, h % 2, :], ps[:, ROT[h % 2], :], ACT.Exp), eg_ready, L, h)
                    order.told(act.activation(dm[:, h % 2, :], dm[:, h % 2, :], ACT.Exp), decay_ready, L, h)
                for n in range(GH * LEVELS):
                    act.wait_ge(p1_ready.sem, p1_ready.at(L, n))
                    if n >= 2:
                        act.wait_ge(xpt_ready.sem, xpt_ready.at(L, n - 2))
                    else:
                        act.wait_ge(head_ready.sem, head_ready.at(L, GH - 1))
                    order.told(act.activation(p1[:, n % 2, :], ps[:, ROT[n % 2], :], ACT.Copy), p1_kept, L, n)
                for h in range(GH):
                    act.wait_ge(uu_ready.sem, uu_ready.at(L, h))
                    order.told(act.activation(vb[:, h, :, :].rearrange("p t d -> p (t d)"), ps[:, ROT[h % 2], :], ACT.Copy), uu_kept, L, h)
                act.wait_ge(ww_ready.sem, ww_ready.at(L, GH - 1))
                for c in range(NCH):
                    act.wait_ge(o_ready.sem, o_ready.at(L, c))
                    order.told(act.activation(og[:, :, c * CH:(c + 1) * CH],
                                              ps[:, STAT[c % 2], 0:GH * CH].rearrange("p (h t) -> p h t", t=CH), ACT.Copy), o_kept, L, c)
                order.settle()
                for i in range(GH + 1):
                    if i < GH:
                        if i >= 2:
                            act.wait_ge(ogstat.sem, ogstat.at(L, i - 2))
                        order.told(act.activation(msq2[:, i % 2, :], og[:, i, :], ACT.Square), ogsq, L, i)
                    if i >= 1:
                        act.wait_ge(ogstat.sem, ogstat.at(L, i - 1))
                        if i >= 3:
                            act.wait_ge(og_ready.sem, og_ready.at(L, i - 3))
                        order.settle()
                        order.told(rs(mrs2[:, (i - 1) % 2, :], ps[:, STAT[(i - 1) % 2], :], P), ogrs, L, i - 1)
                act.wait_ge(og_ready.sem, og_ready.at(L, GH - 1))
                for n, src in enumerate(mixed):
                    order.told(act.activation(a_hi[:, n, :], src, ACT.Copy), m2hi_ready, L, n)

                order.settle()
                order.step(act.activation(after_core[:], ones[:, 0:1], ACT.Copy))
                order.restart()

                def post_squares(i, v, j, hi_kt):
                    for s in range(2):
                        hi_next(v + 1, s, hi_kt)
                        act.wait_ge(acc_free.sem, v * 2 + (s + 3))
                        n = j * 2 + s
                        if not (isinstance(j, int) and j == 0):
                            act.wait_ge(yssq_done.sem, yssq_done.at(L, i * KD + n - 2))
                        act.activation(cv[s][:], tile(y, n), ACT.Square).then_inc(ysq_ready.sem, 1)

                def post_norm(i, gen):
                    act.wait_ge(ystat_ready.sem, ystat_ready.at(L, i))
                    order.settle()
                    order.told(rs(cv[0][:], ps[:, STAT[1], :], DM), yrs_ready, L, i)
                    order.restart()
                    with act.Fori(0, PAIRS_O) as j:
                        for s in range(2):
                            split_h(gen, j * 2 + s, s, lambda: act.wait_ge(x2_ready.sem, x2_ready.at(L, i * KD + j * 2 + s)))

                post_squares(0, V + OFF_O2, 0, KD)
                with act.Fori(1, PAIRS_O) as j:
                    post_squares(0, V + OFF_O2 + j, j, KD)
                post_norm(0, G + 1)
                norm_rstd(G + 1)
                order.restart()
                for hf in range(2):
                    def feed2(j, kt, hf=hf):
                        v = V + OFF_UP2[hf] + j
                        t = hf * HALF + j
                        hi_next(v + 1, 0, kt)
                        act.wait_ge(acc_free.sem, v * 2 + 3)
                        act.activation(cv[0][:], cv[0][:], ACT.Silu).then_inc(silu2_ready.sem, 1)
                        hi_next(v + 1, 1, kt)
                        act.wait_ge(prod2_ready.sem, prod2_ready.at(L, t))
                        act.activation(tile(a_hi, j), prod[:], ACT.Copy).then_inc(a2hi_ready.sem, 1)

                    with act.Fori(0, PAIRS_UP - 1) as j:
                        feed2(j, KD)
                    feed2(PAIRS_UP - 1, HALF)
                    if hf == 0:
                        with act.Fori(0, PAIRS_DOWN - 1) as j:
                            for s in range(2):
                                hi_next(V + OFF_DOWN2[hf] + 1 + j, s, HALF)
                        for s in range(2):
                            hi_next(V + OFF_DOWN2[hf] + PAIRS_DOWN, s, KD)
                    else:
                        post_squares(1, V + OFF_DOWN2[hf], 0, HALF)
                        with act.Fori(1, PAIRS_DOWN - 1) as j:
                            post_squares(1, V + OFF_DOWN2[hf] + j, j, HALF)
                        post_squares(1, V + OFF_DOWN2[hf] + PAIRS_DOWN - 1, PAIRS_DOWN - 1, KD)
                post_norm(1, G + 2)

        @block.vector
        def _(dve):
            order = Order(dve, dve_step.sem, consts_made)
            dve.memset(ones[:], 1.0).then_inc(dve_step.sem, 1)
            dve.memset(eps[:, 0:1], EPS).then_inc(dve_step.sem, 1)
            dve.memset(eps[:, 1:2], LN_EPS).then_inc(dve_step.sem, 1)
            dve.memset(rows[:], 1.0).then_inc(dve_step.sem, 1)
            order.n, order.last = 4, (dve_step.sem, 4)
            order.settle()
            dve.tensor_scalar(negones[:], ones[:], -1.0, None, ALU.mult).then_inc(consts_made.sem, 1)
            dve.wait_ge(consts_made.sem, 1)
            dve.sem_inc(acc_free.sem, 2)
            for i, r in enumerate(ROWS):
                dve.wait_ge(params_turned.sem, i + 1)
                dve.tensor_copy(COLS[i], ps[:, TRN[i % 2], 0:r]).then_inc(params_kept.sem, 1)

            def tail(gen, n, s, first):
                dve.wait_ge(sq_ready.sem, sq_ready.at(gen, n))
                if not first:
                    dve.wait_ge(ssq_done.sem, ssq_done.at(gen, n - 1))
                if first:
                    ins = dve.tensor_copy(ssq[:], sqt[:, s, :])
                else:
                    ins = dve.tensor_tensor(ssq[:], ssq[:], sqt[:, s, :], ALU.add)
                order.told(ins, ssq_done, gen, n)
                dve.wait_ge(hhi_ready.sem, hhi_ready.at(gen, n))
                ins = dve.scalar_tensor_tensor(tile(h_lo, n), tile(x, n), gain(gen * KD + n),
                                               tile(h_hi, n).bitcast(F32), ALU.mult, ALU.subtract)
                order.told(ins, h_ready, gen, n)

            def evac(v, s, wait=True):
                dve.wait_ge(unit_done.sem, v * 2 + (s + 3))

            for n in range(KD):
                dve.wait_ge(x_turned.sem, n + 1)
                order.told(dve.tensor_copy(x[:, n, :], ps[:, ROT[n % 2], :]), x_ready, 0, n)
                tail(0, n, n % 2, n == 0)

            order.restart()
            with dve.Fori(0, DEPTH) as L:
                V = L * PAIRS1
                dve.wait_ge(rstd_ready.sem, rstd_ready.at(L * 2, 0))
                dests = [t[:, i, :] for t in (u, vv) for i in range(NS)] + [zq[:, i, :] for i in range(NQ)] + [zk[:], zv[:]]
                for i, z in enumerate(dests):
                    dve.wait_ge(unit_done.sem, V * 2 + i + 3)
                    dve.tensor_tensor(z, ps[:, ACC[i % 2], :], rstd[:], ALU.mult).then_inc(acc_free.sem, 1)
                    order.last = (acc_free.sem, V * 2 + i + 3)
                for g in range(NKV):
                    for r in range(2):
                        ins = dve.memset(vaug[:, g, r, :, 64 - 64 * r:128 - 64 * r], 1.0)
                        if (g, r) == (NKV - 1, 1):
                            order.told(ins, vones_ready, L, 0)
                        else:
                            order.step(ins)
                for t in range(NS):
                    dve.wait_ge(vvrs_ready.sem, vvrs_ready.at(L, t))
                    order.told(dve.scalar_tensor_tensor(vv[:, t, :], vv[:, t, :], param(pa, L, 2 + t), mrs[:, t % 2, :],
                                                        ALU.mult, ALU.mult), vvn_ready, L, t)
                dve.wait_ge(sgb_loaded.sem, L * 32 + 32)
                for t in range(NS):
                    dve.wait_ge(mix_ready.sem, mix_ready.at(L, t))
                    order.settle()
                    order.told(dve.tensor_tensor(
                        t1[:].rearrange("p (c q) -> p c q", q=P), ps[:, ROT[t % 2], :].rearrange("p (c q) -> p c q", q=P),
                        sgb[:, t, :].unsqueeze(1).to_broadcast([P, TB, P]), ALU.add), mix_used, L, t)
                    order.settle()
                    order.told(dve.tensor_tensor(u[:, t, :], u[:, t, :], t1[:], ALU.mult), sg_ready, L, t)
                for i in range(NQ + 1):
                    z = zk[:] if i == 0 else zq[:, i - 1, :]
                    dve.wait_ge(qkrs_ready.sem, qkrs_ready.at(L, i))
                    order.told(dve.scalar_tensor_tensor(z, z, param(pa, L, 1 if i == 0 else 0), mrs[:, i % 2, :],
                                                        ALU.mult, ALU.mult), qkn_ready, L, i)
                for i in range(NQ + 1):
                    z = zk[:] if i == 0 else zq[:, i - 1, :]
                    dve.wait_ge(rot_ready.sem, rot_ready.at(L, i))
                    order.settle()
                    order.told(dve.tensor_tensor(t2[:], ps[:, ROT[i % 2], :], rope[:, 1, :], ALU.mult), rot_used, L, i)
                    order.step(dve.tensor_tensor(t1[:], z, rope[:, 0, :], ALU.mult))
                    order.settle()
                    order.told(dve.tensor_tensor(z, t1[:], t2[:], ALU.add), rope_ready, L, i)
                for h in range(NH + 1):
                    if h < NH:
                        for b in range(2):
                            dve.wait_ge(S_ready.sem, S_ready.at(L, 2 * h + b))
                            order.settle()
                            order.told(dve.tensor_reduce(mx[:, h % 2, 2 * b:2 * b + 2], ps[:, STAT[0]:STAT[1] + 1, :], AX, ALU.max),
                                       S_used, L, 2 * h + b)
                        if h >= 1:
                            dve.wait_ge(ST_ready.sem, ST_ready.at(L, h * TB - 1))
                        order.settle()
                        order.told(dve.tensor_tensor(diag[:], ident[:].unsqueeze(1).to_broadcast([P, TB, P]),
                                                     mx[:, h % 2, :].unsqueeze(2).to_broadcast([P, TB, P]), ALU.mult),
                                   diag_ready, L, h)
                    if h >= 1:
                        t, r = (h - 1) // 2, 64 * ((h - 1) % 2)
                        dve.wait_ge(PV_done.sem, PV_done.at(L, h * TB - 1))
                        order.step(dve.reciprocal(mrs[r:r + 64, 0, :], ps[64 - r:128 - r, TRN[(h - 1) % 2], :]))
                        order.settle()
                        order.told(dve.tensor_tensor(ao[r:r + 64, t, :], ps[r:r + 64, TRN[(h - 1) % 2], :],
                                                     mrs[r:r + 64, 0, :], ALU.mult), ao_ready, L, h - 1)
                for i in range(NQ + NS + 1):
                    if i < NQ + NS:
                        if i % NQ == 0:
                            dve.wait_ge(ors_ready.sem, ors_ready.at(L, i // NQ))
                        z = ao[:, i, :] if i < NQ else u[:, i - NQ, :]
                        order.settle()
                        order.told(dve.scalar_tensor_tensor(mtmp[:, i % 2, :], z, param(pa, L, 6 + i), ors[:, i // NQ, :],
                                                            ALU.mult, ALU.mult), mtmp_ready, L, i)
                    if i >= 1:
                        dve.wait_ge(mhi_ready.sem, mhi_ready.at(L, i - 1))
                        order.told(dve.tensor_tensor(a_lo[:, i - 1, :], mtmp[:, (i - 1) % 2, :],
                                                     a_hi[:, i - 1, :].bitcast(F32), ALU.subtract), merged_ready, L, i - 1)

                def residual(v, s, n):
                    dve.wait_ge(unit_done.sem, v * 2 + (s + 3))
                    dve.tensor_tensor(tile(x, n), tile(x, n), ps[:, ACC[s], :], ALU.add).then_inc(acc_free.sem, 1)
                    order.last = (acc_free.sem, v * 2 + (s + 3))

                def residual_norm(gen, v, j, first):
                    for s in range(2):
                        residual(v, s, j * 2 + s)
                        tail(gen, j * 2 + s, s, first and s == 0)

                order.restart()
                residual_norm(L * 2 + 1, V + OFF_O, 0, True)
                order.restart()
                with dve.Fori(1, PAIRS_O) as j:
                    residual_norm(L * 2 + 1, V + OFF_O + j, j, False)
                    order.restart()
                order.settle()
                for s in range(2):
                    for e in (0, SEQ + 1):
                        order.step(dve.memset(pad[s][:, e:e + 1], 0.0))
                order.restart()
                order.wait_alone(rstd_ready.sem, rstd_ready.at(L * 2 + 1, 0))
                for hf in range(2):
                    with dve.Fori(0, PAIRS_UP) as j:
                        v = V + OFF_UP[hf] + j
                        for s in range(2):
                            dve.wait_ge(unit_done.sem, v * 2 + (s + 3))
                            if s == 0:
                                order.settle()
                            dve.tensor_tensor(pad[s][:, 1:SEQ + 1], ps[:, ACC[s], :], rstd[:], ALU.mult)\
                                .then_inc(acc_free.sem, 1)
                            col = s * NF + hf * HALF + j
                            i = 2 * (hf * HALF + j) + s
                            dve.wait_ge(center_ready.sem, L * 2 * NF + i + 1)
                            order.step(dve.scalar_tensor_tensor(cv[s][:], pad[s][:, 0:SEQ], param(pb, L, col), cv[s][:],
                                                                ALU.mult, ALU.add))
                            order.settle()
                            order.told(dve.scalar_tensor_tensor(cv[s][:], pad[s][:, 2:SEQ + 2], param(pc, L, col), cv[s][:],
                                                                ALU.mult, ALU.add), conv_ready, L, i)
                        t = hf * HALF + j
                        dve.wait_ge(silu_ready.sem, silu_ready.at(L, t))
                        order.settle()
                        order.told(dve.tensor_tensor(prod[:], cv[0][:], cv[1][:], ALU.mult), prod_ready, L, t)
                        dve.wait_ge(ahi_ready.sem, ahi_ready.at(L, t))
                        order.told(dve.tensor_tensor(tile(a_lo, j), prod[:], tile(a_hi, j).bitcast(F32), ALU.subtract),
                                   a_ready, L, t)
                        order.restart()
                    if hf == 0:
                        with dve.Fori(0, PAIRS_DOWN) as j:
                            for s in range(2):
                                residual(V + OFF_DOWN[hf] + j, s, j * 2 + s)
                            order.restart()
                    else:
                        residual_norm(L * 2 + 2, V + OFF_DOWN[hf], 0, True)
                        order.restart()
                        with dve.Fori(1, PAIRS_DOWN) as j:
                            residual_norm(L * 2 + 2, V + OFF_DOWN[hf] + j, j, False)
                            order.restart()

            with dve.Fori(0, DEPTH) as L:
                V = BASE2 + L * PAIRS2
                G = L * 2 + 2 * DEPTH
                dve.wait_ge(rstd_ready.sem, rstd_ready.at(G, 0))
                order.step(dve.memset(zp[:, :, 0:GT - 1], 0.0))
                order.step(dve.memset(ypad[:, :, 0:CT - 1], 0.0))
                for i in range(NA):
                    order.step(dve.memset(vaug2[:, 2 * i, :, 64:128], 1.0))
                    ins = dve.memset(vaug2[:, 2 * i + 1, :, 0:64], 1.0)
                    if i == NA - 1:
                        order.told(ins, v2ones_ready, L, 0)
                    else:
                        order.step(ins)
                dve.wait_ge(wab_loaded.sem, L * 16 + 16)
                order.settle()
                order.told(dve.tensor_copy(wab_hi[:], wab[:]), wab_split, L, 0)
                order.settle()
                order.told(dve.tensor_tensor(wab_lo[:], wab[:], wab_hi[:].bitcast(F32), ALU.subtract), wab_split, L, 1)

                def project(i, dst):
                    dve.wait_ge(unit_done.sem, V * 2 + i + 3)
                    order.settle()
                    dve.tensor_tensor(dst, ps[:, ACC[i % 2], :], rstd[:], ALU.mult).then_inc(acc_free.sem, 1)
                    order.last = (acc_free.sem, V * 2 + i + 3)

                for i in range(NG):
                    project(i, zp[:, i % 2, GT - 1:GT - 1 + SEQ])
                    dve.wait_ge(sc_center.sem, sc_center.at(L, i))
                    for k in range(GT - 1):
                        order.settle()
                        ins = dve.scalar_tensor_tensor(gqkv[i], zp[:, i % 2, k:k + SEQ], param(pd, L, D_SC + k * NG + i), gqkv[i],
                                                       ALU.mult, ALU.add)
                        if k == GT - 2:
                            order.told(ins, sc_ready, L, i)
                        else:
                            order.step(ins)
                for h in range(GH):
                    project(NG + h, gz[:, h, :])
                at = NG + GH
                for t in range(NC):
                    project(at + t, ypad[:, t, CT - 1:])
                for t in range(NC):
                    project(at + NC + t, cg[:, t, :])
                at += 2 * NC

                def taps(k0, k1):
                    for k in range(k0, k1):
                        for t in range(NC):
                            w = param(pd, L, D_DW + k * NC + t)
                            src = ypad[:, t, k:k + SEQ]
                            if k == 0:
                                ins = dve.tensor_scalar(yc[:, t, :], src, w, param(pd, L, D_BIAS + t), ALU.mult, ALU.add)
                            else:
                                ins = dve.scalar_tensor_tensor(yc[:, t, :], src, w, yc[:, t, :], ALU.mult, ALU.add)
                            if k == CT - 1:
                                order.told(ins, dw_ready, L, t)
                            else:
                                order.step(ins)
                        order.settle()

                n_att = 3 * NA
                for i in range(n_att):
                    project(at + i, za[:, i, :])
                    if i == 0:
                        for t in range(NC):
                            dve.wait_ge(cg_ready.sem, cg_ready.at(L, t))
                            order.step(dve.tensor_tensor(ypad[:, t, CT - 1:], ypad[:, t, CT - 1:], cg[:, t, :], ALU.mult))
                        order.settle()
                    taps(CT * i // n_att, CT * (i + 1) // n_att)

                dve.wait_ge(rcol_ready.sem, rcol_ready.at(L, 0))
                order.told(dve.tensor_copy(rcol[:], ps[:, TRN[0], :].rearrange("p (t q) -> p t q", q=P)[:, :, 0:1]
                                           .rearrange("p t q -> p (t q)")), rcol_kept, L, 0)
                order.settle()
                dve.wait_ge(ab_ready.sem, ab_ready.at(L, 0))
                abp = ps[:, TRN[1], 0:TB * 2 * GH].rearrange("p (t c) -> p t c", c=2 * GH)
                rb = rcol[:].unsqueeze(2).to_broadcast([P, TB, GH])
                dtb = gate_par[:, 1, ds(L, 1), :].to_broadcast([P, TB, GH])
                order.step(dve.tensor_tensor(cols["a"][:], abp[:, :, 0:GH], rb, ALU.mult))
                order.step(dve.tensor_tensor(cols["b"][:], abp[:, :, GH:2 * GH], rb, ALU.mult))
                order.settle()
                order.step(dve.tensor_tensor(cols["a"][:], cols["a"][:], dtb, ALU.add))
                order.settle()
                order.step(dve.tensor_scalar(cols["ax"][:], cols["a"][:], -1.0, None, ALU.mult))
                order.settle()
                order.told(dve.tensor_tensor(cols["ax"][:], cols["ax"][:], cols["a"][:], ALU.max), gate_in, L, 0)
                dve.wait_ge(gate_e1.sem, gate_e1.at(L, 0))
                order.step(dve.tensor_scalar(cols["beta"][:], cols["beta"][:], 1.0, None, ALU.add))
                order.settle()
                order.step(dve.reciprocal(cols["beta"][:], cols["beta"][:]))
                dve.wait_ge(gate_e2.sem, gate_e2.at(L, 0))
                order.step(dve.scalar_tensor_tensor(cols["a"][:], cols["a"][:], 0.0, cols["l"][:], ALU.max, ALU.add))
                order.settle()
                order.told(dve.scalar_tensor_tensor(cols["g"][:], cols["a"][:], -1.0,
                                                    expa[:].unsqueeze(1).to_broadcast([P, TB, GH]), ALU.mult, ALU.mult), g_ready, L, 0)
                dve.wait_ge(c2_loaded.sem, 3 * 16)
                for i in range(2 * NA):
                    z = za[:, i, :]
                    dve.wait_ge(rot2_ready.sem, rot2_ready.at(L, i))
                    order.settle()
                    order.told(dve.tensor_tensor(ta[:], ps[:, ROT[i % 2], :], rope2[:, 1, :], ALU.mult), rot2_used, L, i)
                    order.step(dve.tensor_tensor(tb2[:], z, rope2[:, 0, :], ALU.mult))
                    order.settle()
                    order.told(dve.tensor_tensor(z, ta[:], tb2[:], ALU.add), rope2_ready, L, i)
                dve.wait_ge(c2_cast.sem, 5 * 16)

                def row_max(h):
                    for b in range(2):
                        dve.wait_ge(S2_ready.sem, S2_ready.at(L, 2 * h + b))
                        order.settle()
                        order.told(dve.tensor_reduce(mx2[:, h % 2, 2 * b:2 * b + 2], ps[:, STAT[0]:STAT[1] + 1, :], AX, ALU.max),
                                   S2_used, L, 2 * h + b)

                row_max(0)
                for h in range(AH):
                    if h >= 1:
                        dve.wait_ge(ST2_ready.sem, ST2_ready.at(L, h * TB - 1))
                    order.settle()
                    order.told(dve.tensor_tensor(diag2[:], ident[:].unsqueeze(1).to_broadcast([P, TB, P]),
                                                 mx2[:, h % 2, :].unsqueeze(2).to_broadcast([P, TB, P]), ALU.mult), diag2_ready, L, h)
                    if h + 1 < AH:
                        row_max(h + 1)
                    for kt in range(TB):
                        n = h * TB + kt
                        dve.wait_ge(E2_ready.sem, E2_ready.at(L, n))
                        o = (TB - 1 - kt) * P
                        order.told(dve.tensor_tensor(probs2[:, kt, :], probs2[:, kt, :], times[:, o:o + SEQ], ALU.mult), P2_ready, L, n)
                    t, r = h // 2, 64 * (h % 2)
                    dve.wait_ge(PV2_done.sem, PV2_done.at(L, h * TB + TB - 1))
                    order.settle()
                    order.step(dve.reciprocal(ta[r:r + 64, :], ps[64 - r:128 - r, TRN[h % 2], :]))
                    order.settle()
                    order.told(dve.tensor_tensor(ya[r:r + 64, t, :], ps[r:r + 64, TRN[h % 2], :], ta[r:r + 64, :], ALU.mult), ya_ready, L, h)
                dve.wait_ge(mean_kept.sem, mean_kept.at(L, 0))
                for i in range(NC):
                    order.told(dve.tensor_tensor(yc[:, i, :], yc[:, i, :], lnt[:], ALU.subtract), centered, L, i)
                dve.wait_ge(ln_rs.sem, ln_rs.at(L, 0))
                for i in range(NC):
                    order.settle()
                    order.told(dve.scalar_tensor_tensor(yc[:, i, :], yc[:, i, :], param(pd, L, D_LNG + i), mrs2[:, 0, :],
                                                        ALU.mult, ALU.mult), ln_scaled, L, i)
                for i in range(2 * GH):
                    dve.wait_ge(l2rs.sem, l2rs.at(L, i))
                    order.told(dve.scalar_tensor_tensor(gqkv[i], gqkv[i], float(P) ** -0.5 if i < GH else 1.0, mrs2[:, i % 2, :],
                                                        ALU.mult, ALU.mult), l2n, L, i)
                NCOL = TB * GH
                flat = lambda n: cols[n][:].rearrange("p t h -> p (t h)")
                dve.wait_ge(G_ready.sem, G_ready.at(L, 0))
                order.told(dve.tensor_copy(flat("gc"), ps[:, TRN[0], 0:NCOL]), gc_kept, L, 0)
                order.settle()
                order.told(dve.tensor_tensor(flat("dg"), ps[:, TRN[0], NCOL:2 * NCOL], flat("gc"), ALU.subtract), dg_ready, L, 0)
                dve.wait_ge(eg_cols.sem, eg_cols.at(L, 0))
                order.told(dve.tensor_tensor(flat("beg"), flat("beta"), flat("egc"), ALU.mult), beg_ready, L, 0)
                order.settle()

                def by_token(t):
                    return t.rearrange("p (t d) -> p t d", d=P)

                def column(n, h):
                    return cols[n][:, :, h:h + 1].to_broadcast([P, TB, P])

                for h in range(GH):
                    s = h % 2
                    dve.wait_ge(grow_ready.sem, grow_ready.at(L, h))
                    order.settle()
                    order.step(dve.tensor_tensor(by_token(dm[:, s, :]), by_token(ps[:, ROT[s], :]), column("gc", h), ALU.subtract))
                    order.settle()
                    order.told(dve.tensor_scalar(dm[:, s, :], dm[:, s, :], 0.0, None, ALU.min), gap_ready, L, h)
                    dve.wait_ge(brow_ready.sem, brow_ready.at(L, h))
                    order.told(dve.tensor_tensor(kb[:, s, :], ps[:, STAT[s], :], gk[:, h, :], ALU.mult), kb_ready, L, h)
                    dve.wait_ge(kT_ready.sem, kT_ready.at(L, h))
                    order.step(dve.tensor_tensor(kbeg[:, h, :, :], by_token(ps[:, TRN[0], :]), column("beg", h), ALU.mult))
                    order.step(dve.tensor_tensor(kout[:, h, :, :], by_token(ps[:, TRN[0], :]), column("egl", h), ALU.mult))
                    dve.wait_ge(gvT_ready.sem, gvT_ready.at(L, h))
                    order.told(dve.tensor_tensor(vb[:, h, :, :], by_token(ps[:, TRN[1], :]), column("beta", h), ALU.mult), turned_used, L, h)
                    dve.wait_ge(decay_ready.sem, decay_ready.at(L, h))
                    dve.wait_ge(kk_ready.sem, kk_ready.at(L, h))
                    order.settle()
                    order.step(dve.tensor_tensor(gv[:, h, :], ps[:, ACC[0], :], dm[:, s, :], ALU.mult))
                    dve.wait_ge(qk_ready.sem, qk_ready.at(L, h))
                    order.step(dve.tensor_tensor(intraT[:, h, :], ps[:, ACC[1], :], dm[:, s, :], ALU.mult))
                    order.settle()
                    order.step(dve.tensor_tensor(by_token(intraT[:, h, :]), by_token(intraT[:, h, :]),
                                                 tri[:].unsqueeze(1).to_broadcast([P, TB, P]), ALU.mult))
                    dve.wait_ge(eg_ready.sem, eg_ready.at(L, h))
                    order.step(dve.tensor_tensor(gq[:, h, :], gq[:, h, :], eg[:, s, :], ALU.mult))
                    order.step(dve.tensor_copy(eg_last[:, h, :], eg[:, s, CH - 1::CH]))
                    for t in (gk, xT):
                        ins = dve.tensor_copy(by_token(t[:, h, :]), ident[:].unsqueeze(1).to_broadcast([P, TB, P]))
                        if t is xT:
                            order.told(ins, head_ready, L, h)
                        else:
                            order.step(ins)
                for n in range(GH * LEVELS + 2):
                    if n < GH * LEVELS:
                        if n >= 2:
                            dve.wait_ge(p1_ready.sem, p1_ready.at(L, n - 2))
                        order.settle()
                        order.told(dve.tensor_tensor(by_token(lt[:, n % 2, :]), by_token(gv[:, n % GH, :]),
                                                     lev[:, n // GH, :].unsqueeze(1).to_broadcast([P, TB, P]), ALU.mult), lt_ready, L, n)
                    m = n - 2
                    if m >= 0:
                        h = m % GH
                        dve.wait_ge(xp_ready.sem, xp_ready.at(L, m))
                        dve.wait_ge(xpt_ready.sem, xpt_ready.at(L, m))
                        order.step(dve.tensor_tensor(gk[:, h, :], gk[:, h, :], ps[:, STAT[m % 2], :], ALU.subtract))
                        order.told(dve.tensor_tensor(xT[:, h, :], xT[:, h, :], ps[:, TRN[m % 2], :], ALU.subtract), x_new, L, m)
                for h in range(GH):
                    dve.wait_ge(ww_ready.sem, ww_ready.at(L, h))
                    order.told(dve.tensor_copy(kbeg[:, h, :, :].rearrange("p t d -> p (t d)"), ps[:, STAT[h % 2], :]), ww_kept, L, h)
                order.told(dve.memset(state, 0.0), state_ready, L, 0)
                for c in range(NCH):
                    tb, r = c // 2, CH * (c % 2)
                    dve.wait_ge(ws_ready.sem, ws_ready.at(L, c))
                    if c == 0:
                        dve.wait_ge(uu_kept.sem, uu_kept.at(L, GH - 1))
                    order.told(dve.tensor_tensor(vn[r:r + CH, :, :], vb[r:r + CH, :, tb, :],
                                                 ps[r:r + CH, ROT[c % 2], :].rearrange("p (h d) -> p h d", d=P), ALU.subtract), vn_ready, L, c)
                    if c < NCH - 1:
                        dve.wait_ge(ds_ready.sem, ds_ready.at(L, c))
                        order.settle()
                        for h in range(GH):
                            ins = dve.scalar_tensor_tensor(state[:, h, :], state[:, h, :], eg_last[:, h, c:c + 1],
                                                           ps[:, TRN[c % 2], h * P:(h + 1) * P], ALU.mult, ALU.add)
                            if h == GH - 1:
                                order.told(ins, state_ready, L, c + 1)
                            else:
                                order.step(ins)
                for h in range(GH):
                    dve.wait_ge(ogrs.sem, ogrs.at(L, h))
                    order.step(dve.scalar_tensor_tensor(og[:, h, :], og[:, h, :], param(pd, L, D_ON), mrs2[:, h % 2, :], ALU.mult, ALU.mult))
                    order.settle()
                    order.told(dve.tensor_tensor(og[:, h, :], og[:, h, :], gz[:, h, :], ALU.mult), og_ready, L, h)
                for n, src in enumerate(mixed):
                    dve.wait_ge(m2hi_ready.sem, m2hi_ready.at(L, n))
                    order.settle()
                    order.told(dve.tensor_tensor(a_lo[:, n, :], src, a_hi[:, n, :].bitcast(F32), ALU.subtract), merged2_ready, L, n)
                order.restart()

                def branch(i, v, j, more):
                    for s in range(2):
                        n = j * 2 + s
                        dve.wait_ge(unit_done.sem, v * 2 + (s + 3))
                        if more:
                            ins = dve.tensor_tensor(tile(y, n), tile(y, n), ps[:, ACC[s], :], ALU.add)
                        else:
                            ins = dve.tensor_copy(tile(y, n), ps[:, ACC[s], :])
                        ins.then_inc(acc_free.sem, 1)
                        order.last = (acc_free.sem, v * 2 + (s + 3))
                        if i is None:
                            continue
                        dve.wait_ge(ysq_ready.sem, ysq_ready.at(L, i * KD + n))
                        if isinstance(n, int) and n == 0:
                            ins = dve.tensor_copy(prod[:], cv[s][:])
                        else:
                            dve.wait_ge(yssq_done.sem, yssq_done.at(L, i * KD + n - 1))
                            ins = dve.tensor_tensor(prod[:], prod[:], cv[s][:], ALU.add)
                        order.told(ins, yssq_done, L, i * KD + n)
                    order.restart()

                def post_norm(i, gen):
                    dve.wait_ge(yrs_ready.sem, yrs_ready.at(L, i))

                    def pair(j):
                        for s in range(2):
                            n = j * 2 + s
                            order.step(dve.scalar_tensor_tensor(cv[1][:], tile(y, n), gain(L * 2 * KD + (GENS + i) * KD + n), cv[0][:],
                                                                ALU.mult, ALU.mult))
                            order.settle()
                            order.told(dve.tensor_tensor(tile(x, n), tile(x, n), cv[1][:], ALU.add), x2_ready, L, i * KD + n)
                            tail(gen, n, s, isinstance(n, int) and n == 0)
                        order.restart()

                    pair(0)
                    with dve.Fori(1, PAIRS_O) as j:
                        pair(j)

                branch(0, V + OFF_O2, 0, False)
                with dve.Fori(1, PAIRS_O) as j:
                    branch(0, V + OFF_O2 + j, j, False)
                post_norm(0, G + 1)
                for hf in range(2):
                    with dve.Fori(0, PAIRS_UP) as j:
                        v = V + OFF_UP2[hf] + j
                        t = hf * HALF + j
                        dve.wait_ge(rstd_ready.sem, rstd_ready.at(G + 1, 0))
                        for s in range(2):
                            dve.wait_ge(unit_done.sem, v * 2 + (s + 3))
                            dve.tensor_tensor(cv[s][:], ps[:, ACC[s], :], rstd[:], ALU.mult).then_inc(acc_free.sem, 1)
                            order.last = (acc_free.sem, v * 2 + (s + 3))
                        dve.wait_ge(silu2_ready.sem, silu2_ready.at(L, t))
                        order.settle()
                        order.told(dve.tensor_tensor(prod[:], cv[0][:], cv[1][:], ALU.mult), prod2_ready, L, t)
                        dve.wait_ge(a2hi_ready.sem, a2hi_ready.at(L, t))
                        order.told(dve.tensor_tensor(tile(a_lo, j), prod[:], tile(a_hi, j).bitcast(F32), ALU.subtract), a2_ready, L, t)
                        order.restart()
                    if hf == 0:
                        with dve.Fori(0, PAIRS_DOWN) as j:
                            branch(None, V + OFF_DOWN2[hf] + j, j, False)
                    else:
                        branch(1, V + OFF_DOWN2[hf], 0, True)
                        with dve.Fori(1, PAIRS_DOWN) as j:
                            branch(1, V + OFF_DOWN2[hf] + j, j, True)
                post_norm(1, G + 2)

            for i in range(TB * 2):
                tb, hf = i // 2, i % 2
                dve.wait_ge(out_turned.sem, i + 1)
                dve.tensor_copy(xs[:, tb, hf * SEQ:(hf + 1) * SEQ], ps[:, ROT[i % 2], :]).then_inc(out_kept.sem, 1)


def constants(seq, head_dim, grid_w, theta, patterns):
    import numpy as np

    f = np.float32
    ident = np.eye(P, dtype=f)
    blk = np.kron(np.eye(2, dtype=f), np.ones((64, 64), f))
    half = head_dim // 2
    inv = f(1) / (f(theta) ** (np.arange(0, half, 2, dtype=f) / f(half)))
    pos = np.arange(seq)
    rope, perm = np.zeros((2, P, seq), f), np.zeros((P, P), f)
    for p in range(P):
        d = p % head_dim
        axis = (pos // grid_w if d < half else pos % grid_w).astype(f)
        i = d % half
        ang = axis * inv[i % (half // 2)]
        rope[0, p], rope[1, p] = np.cos(ang), np.sin(ang) * (f(-1) if i < half // 2 else f(1))
        perm[p ^ (half // 2), p] = 1
    half = head_dim // 2
    inv = np.exp(f(-math.log(theta)) * np.arange(half, dtype=f) * f(2.0 / head_dim))
    rope2, perm2 = np.zeros((2, P, seq), f), np.zeros((P, P), f)
    for p in range(P):
        d = p % head_dim
        ang = pos.astype(f) * inv[d % half]
        rope2[0, p], rope2[1, p] = np.cos(ang), np.sin(ang) * (f(-1) if d < half else f(1))
        perm2[p ^ half, p] = 1
    def held(d):
        return sum((d >= 0) & (d <= window) & (d % dilation == 0) for window, dilation in patterns).astype(f)

    p, c = np.arange(P)[:, None], np.arange(2 * seq - P)[None, :]
    by_query, by_key = held(p + (seq - P) - c), held(c - (seq - P) - p)
    low = lambda n: np.where(n > 0, f(0), f(-1e30))
    j, i = np.arange(P)[:, None], np.arange(P)[None, :]
    tri = ((j // 64 == i // 64) & (j <= i)).astype(f)
    lev = np.stack([((j // (2 << s) == i // (2 << s)) & (j // (1 << s) < i // (1 << s))).astype(f) for s in range(6)])
    return {"c_ident": ident, "c_blk": blk, "c_rope": rope, "c_perm": perm, "c_rope2": rope2, "c_perm2": perm2,
            "c_mask_s": low(by_query), "c_mask_t": low(by_key), "c_times": by_key, "c_tri": tri, "c_lev": lev}


def kernel(**inputs):
    import numpy as np
    import concourse.bacc as bacc
    from concourse.bass_utils import run_bass_kernel_spmd

    nc = bacc.Bacc("TRN2", target_bir_lowering=False, num_devices=1)
    arrays = {f"in_{n}": np.ascontiguousarray(a) for n, a in inputs.items()}
    arrays |= {f"in_{n}": a for n, a in constants(inputs["x"].shape[1], inputs["q_norm_g"].shape[1], 64, 10000.0,
                                                        ((128, 1), (512, 4), (2048, 16))).items()}
    D = {n[3:]: nc.dram_tensor(n, a.shape, mybir.dt.from_np(a.dtype), kind="ExternalInput").ap() for n, a in arrays.items()}
    out = nc.dram_tensor("out", inputs["x"].shape, F32, kind="ExternalOutput").ap()
    network(nc, D, out)
    r = run_bass_kernel_spmd(nc, [arrays], core_ids=[0])
    return r.results[0]["out"]
```

```python
import math
from contextlib import ExitStack

import concourse.bass as bass
from concourse import mybir

P = 128
F32 = mybir.dt.float32
F32R = mybir.dt.float32r
BF16 = mybir.dt.bfloat16
ALU = mybir.AluOpType
ACT = mybir.ActivationFunctionType
AX = mybir.AxisListType.X
ds = bass.ds


class Signal:

    def __init__(self, sem, per=1, base=0):
        self.sem, self.per, self.base = sem, per, base

    def at(self, layer, i):
        return layer * self.per + (i + (self.base + 1))


class Order:

    def __init__(self, eng, sem, begun):
        self.eng, self.sem, self.n, self.last, self.begun = eng, sem, 0, None, begun

    def step(self, ins):
        self.n += 1
        ins.then_inc(self.sem, 1)
        self.last = (self.sem, self.n)

    def told(self, ins, signal, layer, i):
        ins.then_inc(signal.sem, 1)
        self.last = (signal.sem, signal.at(layer, i))

    def settle(self):
        if self.last is not None:
            self.eng.wait_ge(*self.last)

    def wait_alone(self, sem, value, own=None):
        self.eng.wait_ge(*(own or (self.begun.sem, 1)))
        self.eng.wait_ge(sem, value)

    def restart(self):
        own = (self.sem, self.n) if self.n else (self.begun.sem, 1)
        if self.last is not None and self.last[0] is not self.sem:
            self.wait_alone(*self.last, own)
        else:
            self.eng.wait_ge(*own)
        if self.n:
            self.eng.sem_clear(self.sem)
        self.n, self.last = 0, None


def network(nc, D, out, stop=None):
    SEQ, DM = D["x"].shape[1:]
    DEPTH = D["w_in"].shape[0]
    KD = DM // P
    TB = SEQ // P
    EPS = 1e-6
    LN_EPS = 1e-5

    HD = D["q_norm_g"].shape[1]
    AW = D["attn_out_g"].shape[1]
    SGW = D["sg_out_g"].shape[1]
    SGH = D["sg_w"].shape[1]
    INW = D["w_in"].shape[2]
    KVW = (INW - AW - 2 * SGW) // 2
    NH, NKV = AW // HD, KVW // HD
    GROUP = NH // NKV
    NQ, NS = AW // P, SGW // P
    N_IN = INW // P
    FF = D["w_down"].shape[1]
    NF = FF // P
    HALF = NF // 2
    TAPS = D["conv_w"].shape[1]
    assert (KD, TB, SEQ, N_IN, NQ, NS, KVW, HALF * 2, TAPS) == (8, 4, 512, 14, 4, 4, P, NF, 3)

    PAIRS_IN, PAIRS_O, PAIRS_UP, PAIRS_DOWN = N_IN // 2, KD // 2, HALF, KD // 2
    OFF_O = PAIRS_IN
    OFF_UP = [OFF_O + PAIRS_O + hf * (PAIRS_UP + PAIRS_DOWN) for hf in range(2)]
    OFF_DOWN = [o + PAIRS_UP for o in OFF_UP]
    PAIRS1 = OFF_DOWN[1] + PAIRS_DOWN

    CC = D["conv_dw_2"].shape[2]
    CT = D["conv_dw_2"].shape[1]
    GH = D["gdn_a_log_2"].shape[1]
    GT = D["gdn_short_conv_2"].shape[1]
    GW = D["gdn_short_conv_2"].shape[2] // 3
    AH = (DM - CC - GW) // 64
    CH = 64
    NCH = SEQ // CH
    NC, NA, NG = CC // P, AH // 2, 3 * GH
    LEVELS = 6
    N_IN2 = 3 * NA + 2 * NC + 4 * GH
    assert GW // GH == P and D["w_gate_2"].shape[2] == FF and N_IN2 % 2 == 0 and CH == 2 ** LEVELS == P // 2
    PAIRS_IN2 = N_IN2 // 2
    OFF_O2 = PAIRS_IN2
    OFF_UP2 = [OFF_O2 + PAIRS_O + hf * (PAIRS_UP + PAIRS_DOWN) for hf in range(2)]
    OFF_DOWN2 = [o + PAIRS_UP for o in OFF_UP2]
    PAIRS2 = OFF_DOWN2[1] + PAIRS_DOWN
    BASE2 = DEPTH * PAIRS1
    PAIRS = BASE2 + DEPTH * PAIRS2
    D_DW, D_BIAS = 0, CT * NC
    D_LNG, D_LNB = D_BIAS + NC, D_BIAS + 2 * NC
    D_SC = D_BIAS + 3 * NC
    D_ON = D_SC + GT * NG
    N_PD = D_ON + 1

    with ExitStack() as ctx:
        def sb(name, shape, dt=F32, on=ctx):
            return on.enter_context(nc.sbuf_tensor(name, shape, dt))

        def sem(name, per=1):
            return Signal(ctx.enter_context(nc.semaphore(name)), per)

        def again(signal, per):
            return Signal(signal.sem, per, DEPTH * signal.per)

        ps = ctx.enter_context(nc.psum_tensor("ps", [P, 8, SEQ], F32))
        ACC, STAT, ROT, TRN = (0, 1), (2, 3), (4, 5), (6, 7)

        x = sb("x_sb", [P, KD, SEQ])
        h_hi, h_lo = sb("h_hi", [P, KD, SEQ], F32R), sb("h_lo", [P, KD, SEQ], F32R)
        raw = [sb(f"raw{s}", [P, HALF, P]) for s in range(2)]
        whi = [sb(f"whi{s}", [P, HALF, P], F32R) for s in range(2)]
        wlo = [sb(f"wlo{s}", [P, HALF, P], F32R) for s in range(2)]
        rstd = sb("rstd", [P, SEQ])
        ssq = sb("ssq", [P, SEQ])
        sqt = sb("sqt", [P, 2, SEQ])
        lnt = sb("lnt", [P, SEQ])
        ident = sb("ident", [P, P])
        ones = sb("ones", [P, P])
        blk = sb("blk", [P, P])
        negones = sb("negones", [P, P], F32R)
        eps = sb("eps", [P, 2])
        GENS = 4 * DEPTH + 1
        gains = sb("gains", [P, GENS * KD + 2 * DEPTH * KD])
        pa = sb("pa", [P, DEPTH, 14])
        pb = sb("pb", [P, DEPTH, 2 * 2 * NF])
        pc = sb("pc", [P, DEPTH, 2 * 2 * NF])
        pd = sb("pd", [P, DEPTH, N_PD])
        gate_par = sb("gate_par", [P, 2, DEPTH, GH])

        setup_loaded = sem("setup_loaded")
        consts_made = sem("consts_made")
        params_turned = sem("params_turned")
        params_kept = sem("params_kept")
        x_loaded = sem("x_loaded")
        x_turned = sem("x_turned")
        x_ready = sem("x_ready", KD)
        act_step, dve_step, pool_step = sem("act_step"), sem("dve_step"), sem("pool_step")
        w_loaded = [sem(f"w_loaded{s}") for s in range(2)]
        w_hi_ready = sem("w_hi_ready")
        w_lo_ready = sem("w_lo_ready")
        unit_done = sem("unit_done")
        acc_free = sem("acc_free")
        sq_ready, ssq_done = sem("sq_ready", KD), sem("ssq_done", KD)
        hhi_ready, h_ready = sem("hhi_ready", KD), sem("h_ready", KD)
        stat_ready, rstd_ready = sem("stat_ready"), sem("rstd_ready")
        sgw_loaded, sgb_loaded = sem("sgw_loaded", 1), sem("sgb_loaded", 1)
        wT_ready, wT_kept = sem("wT_ready", 2), sem("wT_kept", 2)
        gelu_ready = sem("gelu_ready", 2 * NS)
        vvsq_ready, vvstat_ready = sem("vvsq_ready", NS), sem("vvstat_ready", NS)
        vvrs_ready, vvn_ready = sem("vvrs_ready", NS), sem("vvn_ready", NS)
        vvT_ready, vvT_kept = sem("vvT_ready", NS), sem("vvT_kept", NS)
        mix_ready, sg_ready = sem("mix_ready", NS), sem("sg_ready", NS)
        mix_used = sem("mix_used", NS)
        qksq_ready, qkstat_ready = sem("qksq_ready", NQ + 1), sem("qkstat_ready", NQ + 1)
        qkrs_ready, qkn_ready = sem("qkrs_ready", NQ + 1), sem("qkn_ready", NQ + 1)
        rot_ready, rot_used, rope_ready = sem("rot_ready", NQ + 1), sem("rot_used", NQ + 1), sem("rope_ready", NQ + 1)
        qr_ready, ql_ready = sem("qr_ready", NQ + 1), sem("ql_ready", NQ + 1)
        rl_ready = sem("rl_ready", NH)
        vT_ready, vaug_ready = sem("vT_ready", 1), sem("vaug_ready", 1)
        vones_ready = sem("vones_ready", 1)
        S_ready, S_used = sem("S_ready", 2 * NH), sem("S_used", 2 * NH)
        diag_ready = sem("diag_ready", NH)
        ST_ready, P_ready = sem("ST_ready", NH * TB), sem("P_ready", NH * TB)
        PV_done, ao_ready = sem("PV_done", NH * TB), sem("ao_ready", NH)
        osq_ready, osq_used = sem("osq_ready", NQ + NS), sem("osq_used", NQ + NS)
        ors_ready = sem("ors_ready", 2)
        mtmp_ready, mhi_ready, merged_ready = (sem(n, NQ + NS) for n in ("mtmp_ready", "mhi_ready", "merged_ready"))
        center_ready, conv_ready = sem("center_ready", 2 * NF), sem("conv_ready", 2 * NF)
        silu_ready, prod_ready = sem("silu_ready", NF), sem("prod_ready", NF)
        ahi_ready, a_ready = sem("ahi_ready", NF), sem("a_ready", NF)
        c2_loaded, c2_cast, wab_loaded, wab_split = sem("c2_loaded"), sem("c2_cast"), sem("wab_loaded"), sem("wab_split", 2)
        zp_clear = sem("zp_clear")
        sc_center, sc_ready, sc_silu = (sem(n, NG) for n in ("sc_center", "sc_ready", "sc_silu"))
        gate_ready, glu_ready, cg_ready = sem("gate_ready", GH), sem("glu_ready", NC), sem("cg_ready", NC)
        rcol_ready, rcol_kept, ab_ready = sem("rcol_ready"), sem("rcol_kept"), sem("ab_ready")
        l2sq, l2stat, l2rs, l2n = (sem(n, 2 * GH) for n in ("l2sq", "l2stat", "l2rs", "l2n"))
        rot2_ready, rot2_used, rope2_ready, qkr2_ready = (again(n, 2 * NA) for n in (rot_ready, rot_used, rope_ready, qr_ready))
        v2T_ready, vaug2_ready, v2ones_ready = again(vT_ready, NA), again(vaug_ready, NA), again(vones_ready, 1)
        S2_ready, S2_used, diag2_ready = again(S_ready, 2 * AH), again(S_used, 2 * AH), again(diag_ready, AH)
        E2_ready = sem("E2_ready", AH * TB)
        ST2_ready, P2_ready, PV2_done = (again(n, AH * TB) for n in (ST_ready, P_ready, PV_done))
        ya_ready = sem("ya_ready", AH)
        dw_ready, mean_ready, mean_kept = sem("dw_ready", NC), sem("mean_ready"), sem("mean_kept")
        centered, lnsq, lnsq_used, ln_scaled, yc_ready = (sem(n, NC) for n in ("centered", "lnsq", "lnsq_used", "ln_scaled", "yc_ready"))
        ln_rs = sem("ln_rs")
        gate_in, gate_e1, gate_e2, g_ready, G_ready, gc_kept, dg_ready, eg_cols = (sem(n) for n in (
            "gate_in", "gate_e1", "gate_e2", "g_ready", "G_ready", "gc_kept", "dg_ready", "eg_cols"))
        beg_ready = sem("beg_ready")
        grow_ready, brow_ready, kT_ready, gvT_ready = (sem(n, GH) for n in ("grow_ready", "brow_ready", "kT_ready", "gvT_ready"))
        kb_ready, gap_ready, decay_ready, eg_ready = (sem(n, GH) for n in ("kb_ready", "gap_ready", "decay_ready", "eg_ready"))
        turned_used, kk_ready, qk_ready, head_ready = (sem(n, GH) for n in ("turned_used", "kk_ready", "qk_ready", "head_ready"))
        lt_ready, p1_ready, p1_kept, xp_ready, xpt_ready, x_new = (sem(n, GH * LEVELS) for n in (
            "lt_ready", "p1_ready", "p1_kept", "xp_ready", "xpt_ready", "x_new"))
        uu_ready, uu_kept, ww_ready, ww_kept = (sem(n, GH) for n in ("uu_ready", "uu_kept", "ww_ready", "ww_kept"))
        state_ready, ws_ready, vn_ready, o_ready, o_kept, ds_ready = (sem(n, NCH) for n in (
            "state_ready", "ws_ready", "vn_ready", "o_ready", "o_kept", "ds_ready"))
        ogsq, ogstat, ogrs, og_ready = (sem(n, GH) for n in ("ogsq", "ogstat", "ogrs", "og_ready"))
        m2hi_ready, merged2_ready = again(mhi_ready, KD), again(merged_ready, KD)
        ysq_ready, yssq_done = sem("ysq_ready", 2 * KD), sem("yssq_done", 2 * KD)
        ystat_ready, yrs_ready = sem("ystat_ready", 2), sem("yrs_ready", 2)
        x2_ready = sem("x2_ready", 2 * KD)
        silu2_ready, prod2_ready, a2hi_ready, a2_ready = (again(n, NF) for n in (silu_ready, prod_ready, ahi_ready, a_ready))
        out_turned, out_kept, out_stored = sem("out_turned"), sem("out_kept"), sem("out_stored")

        def tile(t, n):
            return t[:, n, :] if isinstance(n, int) else t[:, ds(n, 1), :].rearrange("p a n -> p (a n)")

        def gain(i):
            return gains[:, i:i + 1] if isinstance(i, int) else gains[:, ds(i, 1)]

        def param(t, layer, i):
            i = slice(i, i + 1) if isinstance(i, int) else ds(i, 1)
            return t[:, ds(layer, 1), i].rearrange("p a b -> p (a b)")

        with ExitStack() as on:
            xs = sb("xs", [P, TB, DM], on=on)
            rows = sb("rows", [P, 9, P], on=on)
        N_GAINS = GENS * KD + 2 * DEPTH * KD
        ROWS = [N_GAINS] + [14, 4 * NF, 4 * NF, N_PD] * DEPTH
        COLS = [gains[:]] + [t[:, l, :] for l in range(DEPTH) for t in (pa, pb, pc, pd)]
        N_ROWS = len(ROWS)

        with ExitStack() as on:
            zq = sb("zq", [P, NQ, SEQ], on=on)
            vv = sb("vv", [P, NS, SEQ], on=on)
            kd2 = sb("kd", [P, NKV, SEQ], on=on)
            kd = [kd2[:, g, :] for g in range(NKV)]
            zk = sb("zk", [P, SEQ], on=on)
            zv = sb("zv", [P, SEQ], on=on)
            t1 = sb("t1", [P, SEQ], on=on)
            t2 = sb("t2", [P, SEQ], on=on)
            kr = [sb("kr0", [P, SEQ], F32R, on=on)]
            vvT = sb("vvT", [P, TB, SGW], on=on)
            kr.append(sb("kr1", [P, SEQ], F32R, on=on))
            kl = [sb(f"kl{g}", [P, SEQ], F32R, on=on) for g in range(NKV)]
            qab = sb("qab", [P, NQ, 2, SEQ], F32R, on=on)
            vaug = sb("vaug", [P, NKV, 2, TB, P], on=on)
            probs = sb("probs", [P, TB, SEQ], on=on)
            diag = sb("diag", [P, 2, TB, P], F32R, on=on)
            wT = sb("wT", [P, SGH, P], on=on)
            mrs = sb("mrs", [P, 2, SEQ], on=on)
            mx = sb("mx", [P, 2, TB], on=on)
            u = sb("u", [P, NS, SEQ], on=on)
            ao = sb("ao", [P, NQ, SEQ], on=on)
            rope = sb("rope", [P, 2, SEQ], on=on)
            perm = sb("perm", [P, P], on=on)
            sgb = sb("sgb", [P, NS, P], on=on)
        msq = sqt
        ors, mtmp = kd2, wT[:].rearrange("p h q -> p (h q)").rearrange("p (a n) -> p a n", n=SEQ)
        sgw = probs[:, 0:2, :].rearrange("p a (h q) -> p (a h) q", q=P)

        with ExitStack() as on:
            a_hi = sb("a_hi", [P, HALF, SEQ], F32R, on=on)
            a_lo = sb("a_lo", [P, HALF, SEQ], F32R, on=on)
            pad = [sb(f"pad{s}", [P, SEQ + 2], on=on) for s in range(2)]
            cv = [sb(f"cv{s}", [P, SEQ], on=on) for s in range(2)]
            prod = sb("prod", [P, SEQ], on=on)
            y = sb("y_sb", [P, KD, SEQ], on=on)

        with ExitStack() as on:
            gq, gk, gv, gz = (sb(n, [P, GH, SEQ], on=on) for n in ("gq", "gk", "gv", "gz"))
            with ExitStack() as core:
                kbeg, kout, vb = (sb(n, [P, GH, TB, P], on=core) for n in ("kbeg", "kout", "vb"))
                eg, dm, kb = (sb(n, [P, 2, SEQ], on=core) for n in ("eg", "dm", "kb"))
                intraT, xT = sb("intraT", [P, GH, SEQ], on=core), sb("xT", [P, GH, SEQ], on=core)
                after_core = sb("after_core", [P, 1], on=core)
            with ExitStack() as early:
                zp = sb("zp", [P, 2, SEQ + GT - 1], on=early)
                cg = sb("cg", [P, NC, SEQ], on=early)
                za = sb("za", [P, 3 * NA, SEQ], on=early)
                qkr2 = sb("qkr2", [P, 2 * NA, SEQ], F32R, on=early)
                vaug2 = sb("vaug2", [P, AH, TB, P], on=early)
                probs2 = sb("probs2", [P, TB, SEQ], on=early)
                diag2 = sb("diag2", [P, TB, P], F32R, on=early)
                ta, tb2 = sb("ta", [P, SEQ], on=early), sb("tb2", [P, SEQ], on=early)
                mx2 = sb("mx2", [P, 2, TB], on=early)
            on.enter_context(nc.sbuf_tensor("hold_core", [P, 2 * 3 * SEQ + (3 + 2) * GH * SEQ + 1], F32))
            ya = sb("ya", [P, NA, SEQ], on=on)
            yc = sb("yc", [P, NC, SEQ], on=on)
            ypad = sb("ypad", [P, NC, SEQ + CT - 1], on=on)
            rope2 = sb("rope2", [P, 2, SEQ], on=on)
            perm2 = sb("perm2", [P, P], on=on)
            wide = SEQ + SEQ - P
            mask_s, mask_t, times = (sb(n, [P, wide], BF16, on=on) for n in ("mask_s", "mask_t", "times"))
            ident_b = sb("ident_b", [P, P], BF16, on=on)
            tri = sb("tri", [P, P], on=on)
            lev = sb("lev", [P, LEVELS, P], BF16, on=on)
            wab, wab_hi, wab_lo = sb("wab", [P, KD, 2 * GH], on=on), sb("wab_hi", [P, KD, 2 * GH], F32R, on=on), sb("wab_lo", [P, KD, 2 * GH], F32R, on=on)
            cols = {n: sb(f"col_{n}", [P, TB, GH], on=on) for n in
                    ("a", "ax", "e", "l", "g", "beta", "gc", "egc", "dg", "egl", "beg", "b")}
            rcol = sb("rcol", [P, TB], on=on)
            expa = sb("expa", [P, GH], on=on)
            eg_last = sb("eg_last", [P, GH, NCH], on=on)
        lt, p1, mrs2, msq2 = eg, dm, kb, sqt
        vn, state = ypad[:, 0, 0:GH * P].rearrange("p (h d) -> p h d", d=P), ypad[:, 1, 0:GH * P].rearrange("p (h d) -> p h d", d=P)
        og = xT
        gqkv = [t[:, i, :] for t in (gq, gk, gv) for i in range(GH)]

        def by_rows(src):
            return src.rearrange("(r p) -> r p", p=P)

        def setup_rows():
            for dst, name in ((ident, "c_ident"), (blk, "c_blk"), (perm, "c_perm")):
                yield dst[:], D[name]
            yield rope[:], D["c_rope"].rearrange("a p n -> p a n")
            for l in range(DEPTH):
                for b, names in enumerate((("attn_norm_g", "ffn_norm_g"), ("attn_pre_norm_2", "ffn_pre_norm_2"))):
                    for i, name in enumerate(names):
                        g = (b * DEPTH + l) * 2 + i
                        yield rows[g * KD:(g + 1) * KD, 0, :], by_rows(D[name][l])
                for i, name in enumerate(("attn_post_norm_2", "ffn_post_norm_2")):
                    g = GENS + 2 * l + i
                    yield rows[g * KD:(g + 1) * KD, 0, :], by_rows(D[name][l])
                a = 1 + 4 * l
                for i, name in enumerate(("q_norm_g", "k_norm_g")):
                    for r in range(2):
                        yield rows[i:i + 1, a, r * HD:(r + 1) * HD], D[name][l:l + 1, :]
                yield rows[2:2 + NS, a, :], by_rows(D["sg_norm_g"][l].rearrange("h d -> (h d)"))
                yield rows[2 + NS:2 + NS + NQ, a, :], by_rows(D["attn_out_g"][l])
                yield rows[2 + NS + NQ:2 + 2 * NS + NQ, a, :], by_rows(D["sg_out_g"][l])
                yield rows[0:2 * NF, a + 1, :], by_rows(D["conv_w"][l, 0])
                yield rows[2 * NF:4 * NF, a + 1, :], by_rows(D["conv_w"][l, 1])
                yield rows[0:2 * NF, a + 2, :], by_rows(D["conv_w"][l, 2])
                yield rows[2 * NF:4 * NF, a + 2, :], by_rows(D["conv_b"][l])
                yield rows[D_DW:D_BIAS, a + 3, :], by_rows(D["conv_dw_2"][l].rearrange("t c -> (t c)"))
                for at, name in ((D_BIAS, "conv_dw_bias_2"), (D_LNG, "conv_norm_gain_2"), (D_LNB, "conv_norm_bias_2")):
                    yield rows[at:at + NC, a + 3, :], by_rows(D[name][l])
                yield rows[D_SC:D_ON, a + 3, :], by_rows(D["gdn_short_conv_2"][l].rearrange("t c -> (t c)"))
                yield rows[D_ON:N_PD, a + 3, :], by_rows(D["gdn_out_norm_2"][l])
            for i, name in enumerate(("gdn_a_log_2", "gdn_dt_bias_2")):
                yield gate_par[:, i, :, :], D[name].unsqueeze(0).to_broadcast([P, DEPTH, GH])

        SETUP = [16 * sum(1 for _ in setup_rows())]

        wv = {n: D[n].rearrange("l (k p) n -> l p k n", p=P) for n in
              ("w_in", "w_o", "w_up", "w_down", "w_in_2", "w_out_2", "w_gate_2", "w_up_2", "w_down_2")}

        def weight(name, layer, k0, kt, col):
            return wv[name][ds(layer, 1), :, k0:k0 + kt, ds(col, P)].rearrange("l p k n -> p (l k) n")

        def plan1(layer):
            yield 0, 1, KD, lambda j, s: weight("w_in", layer, 0, KD, j * 2 * P + (NQ + 1 - s) * P)
            for at, tile0 in ((1, 0), (1 + NQ // 2, NQ + 2 + NS), (1 + NQ // 2 + NS // 2, NQ + 2)):
                yield at, 2, KD, lambda j, s, t=tile0: weight("w_in", layer, 0, KD, j * 2 * P + (t + s) * P)
            yield OFF_O, PAIRS_O, KD, lambda j, s: weight("w_o", layer, 0, KD, j * 2 * P + s * P)
            for hf in range(2):
                yield OFF_UP[hf], PAIRS_UP, KD, lambda j, s, hf=hf: weight(
                    "w_up", layer, 0, KD, j * P + (s * NF + hf * HALF) * P)
                yield OFF_DOWN[hf], PAIRS_DOWN, HALF, lambda j, s, hf=hf: weight(
                    "w_down", layer, hf * HALF, HALF, j * 2 * P + s * P)

        mixed = [t[:, i, :] for t, n in ((ya, NA), (yc, NC), (og, GH)) for i in range(n)]

        def plan2(layer):
            for at, n, tile0 in ((0, 2 * GH, 3 * NA + 2 * NC), (2 * GH, NC, 3 * NA), (2 * GH + NC, 3 * NA // 2, 0)):
                yield at, n, KD, lambda j, s, t=tile0: weight("w_in_2", layer, 0, KD, j * 2 * P + (t + s) * P)
            yield OFF_O2, PAIRS_O, KD, lambda j, s: weight("w_out_2", layer, 0, KD, j * 2 * P + s * P)
            for hf in range(2):
                yield OFF_UP2[hf], PAIRS_UP, KD, lambda j, s, hf=hf: weight(
                    ("w_gate_2", "w_up_2")[s], layer, 0, KD, j * P + hf * HALF * P)
                yield OFF_DOWN2[hf], PAIRS_DOWN, HALF, lambda j, s, hf=hf: weight(
                    "w_down_2", layer, hf * HALF, HALF, j * 2 * P + s * P)

        block = ctx.enter_context(nc.Block())

        @block.sync
        def _(sp):
            def load(v, s, kt, src):
                sp.wait_ge(w_lo_ready.sem, v * 2 + (s + 1))
                sp.wait_ge(consts_made.sem, 1)
                sp.dma_start(raw[s][:, 0:kt, :], src).then_inc(w_loaded[s].sem, 16)

            sp.dma_start(xs[:], D["x"][0].rearrange("(t p) d -> p t d", p=P)).then_inc(x_loaded.sem, 16)
            with sp.Fori(0, DEPTH) as L:
                for off, n, kt, src in plan1(L):
                    with sp.Fori(0, n) as j:
                        for s in range(2):
                            load(L * PAIRS1 + off + j, s, kt, src(j, s))
            with sp.Fori(0, DEPTH) as L:
                for off, n, kt, src in plan2(L):
                    with sp.Fori(0, n) as j:
                        for s in range(2):
                            load(BASE2 + L * PAIRS2 + off + j, s, kt, src(j, s))
            for s in range(2):
                load(PAIRS, s, KD, weight("w_in", 0, 0, KD, s * P))
            for tb in range(TB):
                for hf in range(2):
                    sp.wait_ge(out_kept.sem, tb * 2 + hf + 1)
                    sp.dma_start(out[0, tb * P:(tb + 1) * P, hf * SEQ:(hf + 1) * SEQ],
                                 xs[:, tb, hf * SEQ:(hf + 1) * SEQ]).then_inc(out_stored.sem, 16)
            sp.wait_ge(out_stored.sem, TB * 2 * 16)
            for s in range(2):
                sp.wait_ge(w_loaded[s].sem, 16 * (PAIRS + 1))

        @block.gpsimd
        def _(pool):
            pool.sem_inc(w_lo_ready.sem, 2)

            def low(v, s, kt):
                pool.wait_ge(w_hi_ready.sem, v * 2 + (s + 1))
                nc.gpsimd.tensor_tensor(wlo[s][:, 0:kt, :], raw[s][:, 0:kt, :], whi[s][:, 0:kt, :].bitcast(F32),
                                        ALU.subtract).then_inc(w_lo_ready.sem, 1)

            with pool.Fori(0, DEPTH) as L:
                for off, n, kt, _src in plan1(L):
                    with pool.Fori(0, n) as j:
                        for s in range(2):
                            low(L * PAIRS1 + off + j, s, kt)

            pool.wait_ge(h_ready.sem, h_ready.at(2 * DEPTH, KD - 1))
            for dst, name in ((mask_s, "c_mask_s"), (mask_t, "c_mask_t"), (times, "c_times"), (ident_b, "c_ident")):
                pool.dma_start(dst[:], D[name]).then_inc(c2_cast.sem, 16)
            pool.dma_start(lev[:], D["c_lev"].rearrange("a p n -> p a n")).then_inc(c2_cast.sem, 16)

            def squares(gen):
                for n in range(1, KD):
                    pool.wait_ge(sq_ready.sem, sq_ready.at(gen, n))
                    pool.wait_ge(ssq_done.sem, ssq_done.at(gen, n - 1))
                    nc.gpsimd.tensor_tensor(ssq[:], ssq[:], sqt[:, n % 2, :], ALU.add).then_inc(ssq_done.sem, 1)

            for s in range(2):
                low(BASE2, s, KD)
            with pool.Fori(0, DEPTH) as L:
                for off, n, kt, _src in plan2(L):
                    first = 1 if off == 0 else 0
                    if off == OFF_UP2[0]:
                        first = 1
                        for s in range(2):
                            low(BASE2 + L * PAIRS2 + off, s, kt)
                        squares(L * 2 + (2 * DEPTH + 1))
                    with pool.Fori(first, n) as j:
                        for s in range(2):
                            low(BASE2 + L * PAIRS2 + off + j, s, kt)
                for s in range(2):
                    low(BASE2 + L * PAIRS2 + PAIRS2, s, KD)
                squares(L * 2 + (2 * DEPTH + 2))
            pool.wait_ge(c2_cast.sem, 5 * 16)

        @block.tensor
        def _(pe):
            pe.sem_inc(unit_done.sem, 2)

            def unit(v, s, kt, rhs_hi, rhs_lo, wait_rhs):
                pe.wait_ge(w_lo_ready.sem, v * 2 + (s + 3))
                pe.wait_ge(acc_free.sem, v * 2 + (s + 1))
                for k in range(kt):
                    wait_rhs(k, s)
                    for n, (w, r) in enumerate(((whi, rhs_hi), (whi, rhs_lo), (wlo, rhs_hi))):
                        mm = pe.matmul(ps[:, ACC[s], :], w[s][:, k, :], r[:, k, :],
                                       start=(k == 0 and n == 0), stop=(k == kt - 1 and n == 2))
                mm.then_inc(unit_done.sem, 1)

            def first_pair(v, kt, rhs_hi, rhs_lo, wait_rhs, before, ks=None):
                ks = list(ks or range(kt))
                for s in range(2):
                    pe.wait_ge(w_lo_ready.sem, v * 2 + (s + 3))
                    pe.wait_ge(acc_free.sem, v * 2 + (s + 1))
                for k in ks:
                    if k == before[0]:
                        before[1]()
                    wait_rhs(k, 0)
                    for s in range(2):
                        for n, (w, r) in enumerate(((whi, rhs_hi), (whi, rhs_lo), (wlo, rhs_hi))):
                            mm = pe.matmul(ps[:, ACC[s], :], w[s][:, k, :], r[:, k, :],
                                           start=(k == ks[0] and n == 0), stop=(k == ks[-1] and n == 2))
                        if k == ks[-1]:
                            mm.then_inc(unit_done.sem, 1)

            def norm_sum(gen):
                pe.wait_ge(ssq_done.sem, ssq_done.at(gen, KD - 1))
                pe.matmul(ps[:, STAT[0], :], ones[:], ssq[:], start=True, stop=True).then_inc(stat_ready.sem, 1)

            def need_h(gen):
                def wait(k, s):
                    if s == 0:
                        pe.wait_ge(h_ready.sem, h_ready.at(gen, k))
                return wait

            pe.wait_ge(setup_loaded.sem, SETUP[0])
            pe.wait_ge(consts_made.sem, 1)
            for i, r in enumerate(ROWS):
                bank = TRN[i % 2]
                if i >= 2:
                    pe.wait_ge(params_kept.sem, i - 1)
                pe.transpose(ps[:, bank, 0:r], rows[0:r, i, :], ident[0:r, 0:r]).then_inc(params_turned.sem, 1)
            pe.wait_ge(x_loaded.sem, 16)
            for n in range(KD):
                if n >= 2:
                    pe.wait_ge(x_ready.sem, n - 1)
                for tb in range(TB):
                    mm = pe.transpose(ps[:, ROT[n % 2], tb * P:(tb + 1) * P], xs[:, tb, n * P:(n + 1) * P], ident[:])
                mm.then_inc(x_turned.sem, 1)

            with pe.Fori(0, DEPTH) as L:
                V = L * PAIRS1
                first_pair(V, KD, h_hi, h_lo, need_h(L * 2), (KD - 1, lambda: norm_sum(L * 2)))

                def head_sums(i):
                    pe.wait_ge(qksq_ready.sem, qksq_ready.at(L, i))
                    if i == 0:
                        pe.wait_ge(rstd_ready.sem, rstd_ready.at(L * 2, 0))
                    if i >= 2:
                        pe.wait_ge(qkrs_ready.sem, qkrs_ready.at(L, i - 2))
                    pe.matmul(ps[:, STAT[i % 2], :], blk[:], msq[:, i % 2, :], start=True, stop=True).then_inc(qkstat_ready.sem, 1)

                def partners(i):
                    pe.wait_ge(qkn_ready.sem, qkn_ready.at(L, i))
                    if i >= 2:
                        pe.wait_ge(rot_used.sem, rot_used.at(L, i - 2))
                    pe.matmul(ps[:, ROT[i % 2], :], perm[:], zk[:] if i == 0 else zq[:, i - 1, :],
                              start=True, stop=True).then_inc(rot_ready.sem, 1)

                def gated_sums(t):
                    pe.wait_ge(vvsq_ready.sem, vvsq_ready.at(L, t))
                    if t < 2:
                        pe.wait_ge(qkrs_ready.sem, qkrs_ready.at(L, NQ))
                    else:
                        pe.wait_ge(vvrs_ready.sem, vvrs_ready.at(L, t - 2))
                    pe.matmul(ps[:, STAT[t % 2], :], blk[:], msq[:, t % 2, :], start=True, stop=True).then_inc(vvstat_ready.sem, 1)

                def turn_spatial():
                    pe.wait_ge(sgw_loaded.sem, L * 16 + 16)
                    for b in range(2):
                        for i in range(4):
                            mm = pe.transpose(ps[:, TRN[b], i * P:(i + 1) * P], sgw[:, 4 * b + i, :], ident[:])
                        mm.then_inc(wT_ready.sem, 1)

                def turn_values():
                    pe.wait_ge(acc_free.sem, V * 2 + 3)
                    pe.wait_ge(wT_kept.sem, wT_kept.at(L, 0))
                    for kt in range(TB):
                        mm = pe.transpose(ps[:, TRN[0], kt * P:(kt + 1) * P], zv[:, kt * P:(kt + 1) * P], ident[:])
                    mm.then_inc(vT_ready.sem, 1)

                def turn_gated(t):
                    pe.wait_ge(vvn_ready.sem, vvn_ready.at(L, t))
                    if t == 0:
                        pe.wait_ge(vaug_ready.sem, vaug_ready.at(L, 0))
                    elif t == 1:
                        pe.wait_ge(wT_kept.sem, wT_kept.at(L, 1))
                    else:
                        pe.wait_ge(vvT_kept.sem, vvT_kept.at(L, t - 2))
                    for c in range(TB):
                        mm = pe.transpose(ps[:, TRN[t % 2], c * P:(c + 1) * P], vv[:, t, c * P:(c + 1) * P], ident[:])
                    mm.then_inc(vvT_ready.sem, 1)

                def mix(t):
                    pe.wait_ge(vvT_kept.sem, vvT_kept.at(L, t))
                    if t == 0:
                        pe.wait_ge(wT_kept.sem, wT_kept.at(L, 1))
                    if t < 2:
                        pe.wait_ge(acc_free.sem, V * 2 + N_IN + 2)
                    else:
                        pe.wait_ge(mix_used.sem, mix_used.at(L, t - 2))
                    for c in range(TB):
                        for r in range(2):
                            mm = pe.matmul(ps[64 * r:64 * r + 64, ACC[t % 2], c * P:(c + 1) * P],
                                           vvT[:, c, t * P + 64 * r:t * P + 64 * r + 64], wT[:, 2 * t + r, :],
                                           start=True, stop=True)
                    mm.then_inc(mix_ready.sem, 1)

                for i in range(2, N_IN):
                    unit(V + i // 2, i % 2, KD, h_hi, h_lo, need_h(L * 2))
                    if i - 2 <= NQ:
                        head_sums(i - 2)
                    if 0 <= i - 3 <= NQ:
                        partners(i - 3)
                    if i == 4:
                        turn_spatial()
                    if i == 6:
                        turn_values()
                    if i in (10, 12):
                        gated_sums(i - 10)
                        gated_sums(i - 9)
                    if i == 12:
                        turn_gated(0)
                        turn_gated(1)

                def scores(h, b):
                    t, e, g = h // 2, h % 2, h // GROUP
                    if h == 0 and b == 0:
                        pe.wait_ge(qr_ready.sem, qr_ready.at(L, NQ))
                        pe.wait_ge(vvrs_ready.sem, vvrs_ready.at(L, NS - 1))
                    else:
                        pe.wait_ge(S_used.sem, S_used.at(L, 2 * h + b - 1))
                    for i in range(2):
                        qb = 2 * b + i
                        mm = pe.matmul(ps[:, STAT[i], :], qab[64 * e:64 * e + 64, t, e, qb * P:(qb + 1) * P],
                                       kr[g][64 * e:64 * e + 64, :], start=True, stop=True)
                    mm.then_inc(S_ready.sem, 1)

                def scores_turned(h, kt):
                    t, e, g = h // 2, h % 2, h // GROUP
                    n = h * TB + kt
                    if n == 0:
                        pe.wait_ge(ql_ready.sem, ql_ready.at(L, NQ))
                    if kt == 0:
                        pe.wait_ge(diag_ready.sem, diag_ready.at(L, h))
                    if n >= 2:
                        pe.wait_ge(P_ready.sem, P_ready.at(L, n - 2))
                    cols_k = slice(kt * P, (kt + 1) * P)
                    pe.matmul(ps[:, ROT[kt % 2], :], kr[g][:, cols_k], qab[:, t, e, :], start=True, stop=False)
                    pe.matmul(ps[:, ROT[kt % 2], :], kl[g][64 * e:64 * e + 64, cols_k], qab[64 * e:64 * e + 64, t, e, :],
                              start=False, stop=False)
                    pe.matmul(ps[:, ROT[kt % 2], :], negones[:], diag[:, h % 2, :, :].rearrange("p b q -> p (b q)"),
                              start=False, stop=True).then_inc(ST_ready.sem, 1)

                def probs_values(h, kt):
                    pe.wait_ge(P_ready.sem, P_ready.at(L, h * TB + kt))
                    if kt == 0 and h >= 2:
                        pe.wait_ge(ao_ready.sem, ao_ready.at(L, h - 2))
                    if kt == 0 and h < 2:
                        pe.wait_ge(vvT_kept.sem, vvT_kept.at(L, NS - 2 + h))
                    pe.matmul(ps[:, TRN[h % 2], :], vaug[:, h // GROUP, h % 2, kt, :], probs[:, kt, :],
                              start=(kt == 0), stop=(kt == TB - 1)).then_inc(PV_done.sem, 1)

                def mixer_sum(i):
                    pe.wait_ge(osq_ready.sem, osq_ready.at(L, i))
                    if i == 0:
                        pe.wait_ge(mix_used.sem, mix_used.at(L, NS - 1))
                    if i == NS:
                        pe.wait_ge(S_used.sem, S_used.at(L, 2 * NH - 1))
                    pe.matmul(ps[:, (ACC[0], STAT[1])[i // NS], :], ones[:], msq[:, i % 2, :],
                              start=(i % NS == 0), stop=(i % NS == NS - 1)).then_inc(osq_used.sem, 1)

                scores(0, 0)
                mix(0)
                mix(1)
                scores(0, 1)
                turn_gated(2)
                turn_gated(3)
                for h in range(NH):
                    for kt in range(TB):
                        scores_turned(h, kt)
                        if kt in (0, 2) and h + 1 < NH:
                            scores(h + 1, kt // 2)
                        if kt >= 1:
                            probs_values(h, kt - 1)
                        if h == NH - 1 and kt == 1:
                            mixer_sum(NS)
                            mixer_sum(NS + 1)
                    probs_values(h, TB - 1)
                    if h == 0:
                        mix(2)
                        mix(3)
                    if h in (2, 3):
                        mixer_sum(2 * h - 4)
                        mixer_sum(2 * h - 3)
                mixer_sum(NS + 2)

                def need_merged(k, s):
                    if s == 0:
                        pe.wait_ge(merged_ready.sem, merged_ready.at(L, (k + NS) % (NQ + NS)))

                first_pair(V + OFF_O, KD, a_hi, a_lo, need_merged, (0, lambda: mixer_sum(NS + 3)),
                           [*range(NQ, NQ + NS), *range(NQ)])
                with pe.Fori(1, PAIRS_O) as j:
                    for s in range(2):
                        unit(V + OFF_O + j, s, KD, a_hi, a_lo, need_merged)
                first_pair(V + OFF_UP[0], KD, h_hi, h_lo, need_h(L * 2 + 1), (KD - 1, lambda: norm_sum(L * 2 + 1)))
                for hf in range(2):
                    with pe.Fori(1 - hf, PAIRS_UP) as j:
                        for s in range(2):
                            unit(V + OFF_UP[hf] + j, s, KD, h_hi, h_lo, need_h(L * 2 + 1))

                    def need_a(k, s, hf=hf):
                        if s == 0:
                            pe.wait_ge(a_ready.sem, a_ready.at(L, hf * HALF + k))

                    with pe.Fori(0, PAIRS_DOWN) as j:
                        for s in range(2):
                            unit(V + OFF_DOWN[hf] + j, s, HALF, a_hi, a_lo, need_a)

            with pe.Fori(0, DEPTH) as L:
                V = BASE2 + L * PAIRS2
                G = L * 2 + 2 * DEPTH
                first_pair(V, KD, h_hi, h_lo, need_h(G), (KD - 1, lambda: norm_sum(G)))
                with pe.Fori(1, PAIRS_IN2) as j:
                    for s in range(2):
                        unit(V + j, s, KD, h_hi, h_lo, need_h(G))
                pe.wait_ge(rstd_ready.sem, rstd_ready.at(G, 0))
                for tb in range(TB):
                    mm = pe.transpose(ps[:, TRN[0], tb * P:(tb + 1) * P], rstd[:, tb * P:(tb + 1) * P], ident[:])
                mm.then_inc(rcol_ready.sem, 1)
                pe.wait_ge(wab_split.sem, wab_split.at(L, 1))
                for tb in range(TB):
                    for k in range(KD):
                        for n, (r, w) in enumerate(((h_hi, wab_hi), (h_hi, wab_lo), (h_lo, wab_hi))):
                            mm = pe.matmul(ps[:, TRN[1], tb * 2 * GH:(tb + 1) * 2 * GH], r[:, k, tb * P:(tb + 1) * P],
                                           w[:, k, :], start=(k == 0 and n == 0), stop=(k == KD - 1 and n == 2))
                mm.then_inc(ab_ready.sem, 1)
                pe.wait_ge(acc_free.sem, V * 2 + 2 * PAIRS_IN2 + 2)
                pe.wait_ge(c2_loaded.sem, 3 * 16)
                for i in range(2 * NA):
                    if i >= 2:
                        pe.wait_ge(rot2_used.sem, rot2_used.at(L, i - 2))
                    pe.matmul(ps[:, ROT[i % 2], :], perm2[:], za[:, i, :], start=True, stop=True).then_inc(rot2_ready.sem, 1)
                pe.wait_ge(rcol_kept.sem, rcol_kept.at(L, 0))
                pe.wait_ge(gate_in.sem, gate_in.at(L, 0))
                for i in range(NA):
                    for kt in range(TB):
                        mm = pe.transpose(ps[:, TRN[i], kt * P:(kt + 1) * P], za[:, 2 * NA + i, kt * P:(kt + 1) * P], ident[:])
                    mm.then_inc(v2T_ready.sem, 1)

                pe.wait_ge(c2_cast.sem, 5 * 16)

                def scores(h):
                    t, r = h // 2, 64 * (h % 2)
                    for b in range(2):
                        if h == 0:
                            pe.wait_ge(qkr2_ready.sem, qkr2_ready.at(L, 2 * NA - 1))
                        if h or b:
                            pe.wait_ge(S2_used.sem, S2_used.at(L, 2 * h + b - 1))
                        for i in range(2):
                            qb = 2 * b + i
                            pe.matmul(ps[:, STAT[i], :], qkr2[r:r + 64, t, qb * P:(qb + 1) * P], qkr2[r:r + 64, NA + t, :],
                                      start=True, stop=False)
                            mm = pe.matmul(ps[:, STAT[i], :], ident_b[:], mask_s[:, (TB - 1 - qb) * P:(TB - 1 - qb) * P + SEQ],
                                           start=False, stop=True)
                        mm.then_inc(S2_ready.sem, 1)

                def probs_values(h, kt):
                    pe.wait_ge(P2_ready.sem, P2_ready.at(L, h * TB + kt))
                    if kt == 0 and h >= 2:
                        pe.wait_ge(ya_ready.sem, ya_ready.at(L, h - 2))
                    if kt == 0 and h == 0:
                        pe.wait_ge(vaug2_ready.sem, vaug2_ready.at(L, NA - 1))
                    pe.matmul(ps[:, TRN[h % 2], :], vaug2[:, h, kt, :], probs2[:, kt, :],
                              start=(kt == 0), stop=(kt == TB - 1)).then_inc(PV2_done.sem, 1)

                scores(0)
                for h in range(AH):
                    t, r = h // 2, 64 * (h % 2)
                    if h + 1 < AH:
                        scores(h + 1)
                    for kt in range(TB):
                        n = h * TB + kt
                        if kt == 0:
                            pe.wait_ge(diag2_ready.sem, diag2_ready.at(L, h))
                        if n >= 2:
                            pe.wait_ge(E2_ready.sem, E2_ready.at(L, n - 2))
                        pe.matmul(ps[:, ROT[kt % 2], :], za[r:r + 64, NA + t, kt * P:(kt + 1) * P], za[r:r + 64, t, :],
                                  start=True, stop=False)
                        pe.matmul(ps[:, ROT[kt % 2], :], negones[:], diag2[:].rearrange("p b q -> p (b q)"),
                                  start=False, stop=False)
                        pe.matmul(ps[:, ROT[kt % 2], :], ident_b[:], mask_t[:, (TB - 1 - kt) * P:(TB - 1 - kt) * P + SEQ],
                                  start=False, stop=True).then_inc(ST2_ready.sem, 1)
                        if kt >= 1:
                            probs_values(h, kt - 1)
                    probs_values(h, TB - 1)

                for i in range(NC):
                    pe.wait_ge(dw_ready.sem, dw_ready.at(L, i))
                    if i == 0:
                        pe.wait_ge(S2_used.sem, S2_used.at(L, 2 * AH - 1))
                    mm = pe.matmul(ps[:, STAT[0], :], ones[:], yc[:, i, :], start=(i == 0), stop=(i == NC - 1))
                mm.then_inc(mean_ready.sem, 1)
                for i in range(NC):
                    pe.wait_ge(lnsq.sem, lnsq.at(L, i))
                    pe.matmul(ps[:, STAT[1], :], ones[:], msq2[:, i % 2, :], start=(i == 0), stop=(i == NC - 1))\
                        .then_inc(lnsq_used.sem, 1)

                for i in range(2 * GH):
                    pe.wait_ge(l2sq.sem, l2sq.at(L, i))
                    if i < 2:
                        pe.wait_ge(ln_rs.sem, ln_rs.at(L, 0))
                    else:
                        pe.wait_ge(l2rs.sem, l2rs.at(L, i - 2))
                    pe.matmul(ps[:, STAT[i % 2], :], ones[:], msq2[:, i % 2, :], start=True, stop=True).then_inc(l2stat.sem, 1)
                pe.wait_ge(g_ready.sem, g_ready.at(L, 0))
                pe.wait_ge(ya_ready.sem, ya_ready.at(L, AH - 1))
                pe.wait_ge(c2_loaded.sem, 3 * 16)
                NCOL = TB * GH
                gflat = cols["g"][:].rearrange("p t h -> p (t h)")
                pe.matmul(ps[:, TRN[0], 0:NCOL], tri[:], gflat, start=True, stop=True)
                pe.matmul(ps[:, TRN[0], NCOL:2 * NCOL], blk[:], gflat, start=True, stop=True).then_inc(G_ready.sem, 1)
                pe.wait_ge(l2n.sem, l2n.at(L, 2 * GH - 1))
                pe.wait_ge(beg_ready.sem, beg_ready.at(L, 0))

                def head_in(h):
                    if h >= 2:
                        pe.wait_ge(head_ready.sem, head_ready.at(L, h - 2))
                    for tb in range(TB):
                        mm = pe.matmul(ps[:, ROT[h % 2], tb * P:(tb + 1) * P], cols["g"][:, tb, h:h + 1].to_broadcast([P, P]),
                                       tri[:], start=True, stop=True)
                    mm.then_inc(grow_ready.sem, 1)
                    for tb in range(TB):
                        mm = pe.matmul(ps[:, STAT[h % 2], tb * P:(tb + 1) * P], cols["beta"][:, tb, h:h + 1].to_broadcast([P, P]),
                                       ident[:], start=True, stop=True)
                    mm.then_inc(brow_ready.sem, 1)
                    if h >= 1:
                        pe.wait_ge(turned_used.sem, turned_used.at(L, h - 1))
                    for tb in range(TB):
                        mm = pe.transpose(ps[:, TRN[0], tb * P:(tb + 1) * P], gk[:, h, tb * P:(tb + 1) * P], ident[:])
                    mm.then_inc(kT_ready.sem, 1)
                    for tb in range(TB):
                        mm = pe.transpose(ps[:, TRN[1], tb * P:(tb + 1) * P], gv[:, h, tb * P:(tb + 1) * P], ident[:])
                    mm.then_inc(gvT_ready.sem, 1)

                def head_products(h):
                    pe.wait_ge(kb_ready.sem, kb_ready.at(L, h))
                    if h >= 1:
                        pe.wait_ge(head_ready.sem, head_ready.at(L, h - 1))
                    for tb in range(TB):
                        mm = pe.matmul(ps[:, ACC[0], tb * P:(tb + 1) * P], gk[:, h, tb * P:(tb + 1) * P],
                                       kb[:, h % 2, tb * P:(tb + 1) * P], start=True, stop=True)
                    mm.then_inc(kk_ready.sem, 1)
                    for tb in range(TB):
                        mm = pe.matmul(ps[:, ACC[1], tb * P:(tb + 1) * P], gk[:, h, tb * P:(tb + 1) * P],
                                       gq[:, h, tb * P:(tb + 1) * P], start=True, stop=True)
                    mm.then_inc(qk_ready.sem, 1)

                head_in(0)
                for h in range(GH):
                    if h + 1 < GH:
                        head_in(h + 1)
                    head_products(h)

                def level_first(n):
                    h = n % GH
                    pe.wait_ge(lt_ready.sem, lt_ready.at(L, n))
                    if n >= 2:
                        pe.wait_ge(p1_kept.sem, p1_kept.at(L, n - 2))
                    for tb in range(TB):
                        c = slice(tb * P, (tb + 1) * P)
                        mm = pe.matmul(ps[:, ROT[n % 2], c], lt[:, n % 2, c], gk[:, h, c], start=True, stop=True)
                    mm.then_inc(p1_ready.sem, 1)

                def level_second(n):
                    h = n % GH
                    pe.wait_ge(p1_kept.sem, p1_kept.at(L, n))
                    if n >= 2:
                        pe.wait_ge(x_new.sem, x_new.at(L, n - 2))
                    for tb in range(TB):
                        c = slice(tb * P, (tb + 1) * P)
                        mm = pe.matmul(ps[:, STAT[n % 2], c], xT[:, h, c], p1[:, n % 2, c], start=True, stop=True)
                    mm.then_inc(xp_ready.sem, 1)
                    for tb in range(TB):
                        c = slice(tb * P, (tb + 1) * P)
                        mm = pe.matmul(ps[:, TRN[n % 2], c], p1[:, n % 2, c], xT[:, h, c], start=True, stop=True)
                    mm.then_inc(xpt_ready.sem, 1)

                pe.wait_ge(head_ready.sem, head_ready.at(L, GH - 1))
                for n in range(GH * LEVELS + 1):
                    if n < GH * LEVELS:
                        level_first(n)
                    if n >= 1:
                        level_second(n - 1)
                for h in range(GH):
                    pe.wait_ge(x_new.sem, x_new.at(L, GH * (LEVELS - 1) + h))
                    if h == 0:
                        pe.wait_ge(x_new.sem, x_new.at(L, GH * LEVELS - 1))
                    if h >= 2:
                        pe.wait_ge(uu_kept.sem, uu_kept.at(L, h - 2))
                    for tb in range(TB):
                        mm = pe.matmul(ps[:, ROT[h % 2], tb * P:(tb + 1) * P], xT[:, h, tb * P:(tb + 1) * P], vb[:, h, tb, :],
                                       start=True, stop=True)
                    mm.then_inc(uu_ready.sem, 1)
                    if h >= 2:
                        pe.wait_ge(ww_kept.sem, ww_kept.at(L, h - 2))
                    for tb in range(TB):
                        mm = pe.matmul(ps[:, STAT[h % 2], tb * P:(tb + 1) * P], kbeg[:, h, tb, :], xT[:, h, tb * P:(tb + 1) * P],
                                       start=True, stop=True)
                    mm.then_inc(ww_ready.sem, 1)
                pe.wait_ge(uu_kept.sem, uu_kept.at(L, GH - 1))
                pe.wait_ge(ww_kept.sem, ww_kept.at(L, GH - 1))
                for c in range(NCH):
                    tb, r = c // 2, CH * (c % 2)
                    at = slice(c * CH, (c + 1) * CH)
                    pe.wait_ge(state_ready.sem, state_ready.at(L, c))
                    wTf = kbeg[:].rearrange("p h t d -> p h (t d)")
                    for h in range(GH):
                        mm = pe.matmul(ps[r:r + CH, ROT[c % 2], h * P:(h + 1) * P], wTf[:, h, at], state[:, h, :],
                                       start=True, stop=True)
                    mm.then_inc(ws_ready.sem, 1)
                    if c >= 2:
                        pe.wait_ge(o_kept.sem, o_kept.at(L, c - 2))
                    pe.wait_ge(vn_ready.sem, vn_ready.at(L, c))
                    for h in range(GH):
                        pe.matmul(ps[:, STAT[c % 2], h * CH:(h + 1) * CH], state[:, h, :], gq[:, h, at], start=True, stop=False)
                        mm = pe.matmul(ps[:, STAT[c % 2], h * CH:(h + 1) * CH], vn[r:r + CH, h, :], intraT[r:r + CH, h, at],
                                       start=False, stop=True)
                    mm.then_inc(o_ready.sem, 1)
                    for h in range(GH):
                        mm = pe.matmul(ps[:, TRN[c % 2], h * P:(h + 1) * P], kout[r:r + CH, h, tb, :], vn[r:r + CH, h, :],
                                       start=True, stop=True)
                    mm.then_inc(ds_ready.sem, 1)
                for h in range(GH):
                    pe.wait_ge(ogsq.sem, ogsq.at(L, h))
                    if h >= 2:
                        pe.wait_ge(ogrs.sem, ogrs.at(L, h - 2))
                    pe.matmul(ps[:, STAT[h % 2], :], ones[:], msq2[:, h % 2, :], start=True, stop=True).then_inc(ogstat.sem, 1)

                def need_merged2(k, s):
                    if s == 0:
                        pe.wait_ge(merged2_ready.sem, merged2_ready.at(L, k))

                def post_sum(i):
                    pe.wait_ge(yssq_done.sem, yssq_done.at(L, i * KD + KD - 1))
                    pe.matmul(ps[:, STAT[1], :], ones[:], prod[:], start=True, stop=True).then_inc(ystat_ready.sem, 1)

                with pe.Fori(0, PAIRS_O) as j:
                    for s in range(2):
                        unit(V + OFF_O2 + j, s, KD, a_hi, a_lo, need_merged2)
                post_sum(0)
                first_pair(V + OFF_UP2[0], KD, h_hi, h_lo, need_h(G + 1), (KD - 1, lambda: norm_sum(G + 1)))
                for hf in range(2):
                    with pe.Fori(1 - hf, PAIRS_UP) as j:
                        for s in range(2):
                            unit(V + OFF_UP2[hf] + j, s, KD, h_hi, h_lo, need_h(G + 1))

                    def need_a2(k, s, hf=hf):
                        if s == 0:
                            pe.wait_ge(a2_ready.sem, a2_ready.at(L, hf * HALF + k))

                    with pe.Fori(0, PAIRS_DOWN) as j:
                        for s in range(2):
                            unit(V + OFF_DOWN2[hf] + j, s, HALF, a_hi, a_lo, need_a2)
                post_sum(1)

            pe.wait_ge(h_ready.sem, h_ready.at(4 * DEPTH, KD - 1))
            for tb in range(TB):
                for hf in range(2):
                    i = tb * 2 + hf
                    if i >= 2:
                        pe.wait_ge(out_kept.sem, i - 1)
                    for n in range(4):
                        mm = pe.transpose(ps[:, ROT[i % 2], n * P:(n + 1) * P],
                                          x[:, 4 * hf + n, tb * P:(tb + 1) * P], ident[:])
                    mm.then_inc(out_turned.sem, 1)

        @block.scalar
        def _(act):
            order = Order(act, act_step.sem, consts_made)

            act.wait_ge(consts_made.sem, 1)
            count = 0
            for dst, src in setup_rows():
                act.dma_start(dst, src).then_inc(setup_loaded.sem, 16)
                count += 16
            assert count == SETUP[0]

            def hi_next(v, s, kt):
                act.wait_ge(w_loaded[s].sem, v * 16 + 16)
                act.wait_ge(unit_done.sem, v * 2 + (s + 1))
                act.activation(whi[s][:, 0:kt, :], raw[s][:, 0:kt, :], ACT.Copy).then_inc(w_hi_ready.sem, 1)

            def rs(dst, src, width, e=0):
                act.activation(lnt[:], src, ACT.Ln, bias=eps[:, e:e + 1], scale=1.0 / width).then_inc(act_step.sem, 1)
                order.n += 1
                act.wait_ge(act_step.sem, order.n)
                return act.activation(dst, lnt[:], ACT.Exp, scale=-0.5)

            def logs_and_exps():
                act.preload_act_table_set("natural_log_exp_and_others")

            def norm_rstd(gen):
                logs_and_exps()
                act.wait_ge(stat_ready.sem, stat_ready.at(gen, 0))
                order.settle()
                order.told(rs(rstd[:], ps[:, STAT[0], :], DM), rstd_ready, gen, 0)

            def split_h(gen, n, s, wait_x):
                wait_x()
                if not (isinstance(gen, int) and n < 2):
                    act.wait_ge(ssq_done.sem, ssq_done.at(gen, n - 2))
                act.activation(sqt[:, s, :], tile(x, n), ACT.Square).then_inc(sq_ready.sem, 1)
                act.activation(tile(h_hi, n), tile(x, n), ACT.Identity, scale=gain(gen * KD + n))\
                    .then_inc(hhi_ready.sem, 1)

            for s in range(2):
                hi_next(0, s, KD)
            act.wait_ge(consts_made.sem, 1)
            act.wait_ge(params_kept.sem, N_ROWS)
            for n in range(KD):
                split_h(0, n, n % 2, lambda n=n: act.wait_ge(x_ready.sem, n + 1))

            with act.Fori(0, DEPTH) as L:
                V = L * PAIRS1
                act.wait_ge(unit_done.sem, V * 2 + 2)
                act.wait_ge(params_kept.sem, N_ROWS)
                act.dma_start(sgw, D["sg_w"][ds(L, 1)].rearrange("l h p q -> p (l h) q")).then_inc(sgw_loaded.sem, 16)
                for r in range(2):
                    act.dma_start(sgb[64 * r:64 * r + 64, :, :],
                                  D["sg_b"][ds(L, 1), r::2, :].to_broadcast([64, NS, P])).then_inc(sgb_loaded.sem, 16)
                norm_rstd(L * 2)

                def head_rs(i, stat, rsig):
                    act.wait_ge(stat.sem, stat.at(L, i))
                    order.settle()
                    order.told(rs(mrs[:, i % 2, :], ps[:, STAT[i % 2], :], HD), rsig, L, i)

                def qk_square(i):
                    act.wait_ge(acc_free.sem, V * 2 + i + 4)
                    if i >= 2:
                        act.wait_ge(qkstat_ready.sem, qkstat_ready.at(L, i - 2))
                    order.told(act.activation(msq[:, i % 2, :], zk[:] if i == 0 else zq[:, i - 1, :], ACT.Square), qksq_ready, L, i)

                def qk_rs(i):
                    if i >= 2:
                        act.wait_ge(qkn_ready.sem, qkn_ready.at(L, i - 2))
                    head_rs(i, qkstat_ready, qkrs_ready)

                def qk_high(i):
                    act.wait_ge(rope_ready.sem, rope_ready.at(L, i))
                    if i == 0:
                        for g in range(NKV):
                            for r in range(2):
                                order.step(act.activation(kd2[64 * r:64 * r + 64, g, :], zk[64 * g:64 * g + 64, :], ACT.Copy))
                        order.settle()
                        order.step(act.activation(kr[0][:], kd[0], ACT.Copy))
                        order.told(act.activation(kr[1][:], kd[1], ACT.Copy), qr_ready, L, 0)
                    else:
                        order.step(act.activation(qab[0:64, i - 1, 0, :], zq[0:64, i - 1, :], ACT.Copy))
                        order.told(act.activation(qab[64:128, i - 1, 1, :], zq[64:128, i - 1, :], ACT.Copy), qr_ready, L, i)

                def gelu(i):
                    z = vv[:, i, :] if i < NS else u[:, i - NS, :]
                    act.wait_ge(acc_free.sem, V * 2 + (NQ + 2 + i + 3))
                    order.told(act.activation(z, z, ACT.Gelu_apprx_tanh), gelu_ready, L, i)

                def vv_square(t):
                    if t < 2:
                        act.wait_ge(qkstat_ready.sem, qkstat_ready.at(L, NQ))
                    else:
                        act.wait_ge(vvstat_ready.sem, vvstat_ready.at(L, t - 2))
                    order.settle()
                    order.told(act.activation(msq[:, t % 2, :], vv[:, t, :], ACT.Square), vvsq_ready, L, t)

                def vv_rs(t):
                    if t < 2:
                        act.wait_ge(qkn_ready.sem, qkn_ready.at(L, NQ))
                    else:
                        act.wait_ge(vvn_ready.sem, vvn_ready.at(L, t - 2))
                    head_rs(t, vvstat_ready, vvrs_ready)

                def vvT_copy(t):
                    act.wait_ge(vvT_ready.sem, vvT_ready.at(L, t))
                    order.told(act.activation(vvT[:, :, t * P:(t + 1) * P],
                                              ps[:, TRN[t % 2], :].rearrange("q (c f) -> q c f", f=P), ACT.Copy),
                               vvT_kept, L, t)

                for i in range(N_IN):
                    hi_next(V + (i // 2 + 1), i % 2, KD)
                    if 0 <= i - 1 <= NQ:
                        qk_square(i - 1)
                    if 0 <= i - 2 <= NQ:
                        qk_rs(i - 2)
                    if 0 <= i - 4 <= NQ:
                        qk_high(i - 4)
                    if i == 5:
                        for b in range(2):
                            act.wait_ge(wT_ready.sem, wT_ready.at(L, b))
                            order.told(act.activation(wT[:, 4 * b:4 * b + 4, :].rearrange("q h p -> q (h p)"),
                                                      ps[:, TRN[b], :], ACT.Copy), wT_kept, L, b)
                    if i == 7:
                        act.wait_ge(vT_ready.sem, vT_ready.at(L, 0))
                        act.wait_ge(vones_ready.sem, vones_ready.at(L, 0))
                        for g in range(NKV):
                            for r in range(2):
                                ins = act.activation(vaug[:, g, r, :, 64 * r:64 * r + 64],
                                                     ps[:, TRN[0], :].rearrange("q (k f) -> q k f", f=P)[:, :, 64 * g:64 * g + 64],
                                                     ACT.Copy)
                                if (g, r) == (NKV - 1, 1):
                                    order.told(ins, vaug_ready, L, 0)
                                else:
                                    order.step(ins)
                        gelu(0)
                    if i == 8:
                        gelu(1)
                        gelu(2)
                        vv_square(0)
                    if i == 9:
                        gelu(3)
                        vv_square(1)
                    if i == 10:
                        gelu(NS)
                    if i == 11:
                        logs_and_exps()
                        vv_rs(0)
                        vv_rs(1)
                        vv_square(2)
                        vv_square(3)
                    if i == 13:
                        vvT_copy(0)
                        vvT_copy(1)
                        vv_rs(2)
                        vv_rs(3)
                for t in range(1, NS):
                    gelu(NS + t)
                logs_and_exps()
                vvT_copy(2)
                vvT_copy(3)

                def exponentials(h, kt):
                    n = h * TB + kt
                    act.wait_ge(ST_ready.sem, ST_ready.at(L, n))
                    if n >= TB:
                        act.wait_ge(PV_done.sem, PV_done.at(L, n - TB))
                    else:
                        act.wait_ge(wT_ready.sem, wT_ready.at(L, 1))
                    order.told(act.activation(probs[:, kt, :], ps[:, ROT[kt % 2], :], ACT.Exp, scale=HD ** -0.5), P_ready, L, n)

                def sums_inverted(h):
                    r = 64 * (h % 2)
                    act.wait_ge(PV_done.sem, PV_done.at(L, h * TB + TB - 1))
                    order.settle()
                    order.step(act.activation(lnt[r:r + 64, :], ps[64 - r:128 - r, TRN[h % 2], :], ACT.Ln))
                    if h >= 2:
                        act.wait_ge(ao_ready.sem, ao_ready.at(L, h - 2))
                    else:
                        act.wait_ge(vvn_ready.sem, vvn_ready.at(L, NS - 1))
                    order.settle()
                    order.told(act.activation(mrs[r:r + 64, 0, :], lnt[r:r + 64, :], ACT.Exp, scale=-1.0), rl_ready, L, h)

                def mixer_square(i):
                    if i < NS:
                        act.wait_ge(sg_ready.sem, sg_ready.at(L, i))
                    else:
                        act.wait_ge(ao_ready.sem, ao_ready.at(L, 2 * (i - NS) + 1))
                    if i >= 2:
                        act.wait_ge(osq_used.sem, osq_used.at(L, i - 2))
                    else:
                        act.wait_ge(vvstat_ready.sem, vvstat_ready.at(L, NS - 1))
                    order.told(act.activation(msq[:, i % 2, :], u[:, i, :] if i < NS else ao[:, i - NS, :], ACT.Square), osq_ready, L, i)

                def mixer_rs(b):
                    act.wait_ge(osq_used.sem, osq_used.at(L, b * NS + NS - 1))
                    order.settle()
                    order.told(rs(ors[:, b, :], ps[:, (ACC[0], STAT[1])[b], :], (SGW, AW)[b]), ors_ready, L, b)

                def merged_high(i):
                    act.wait_ge(mtmp_ready.sem, mtmp_ready.at(L, i))
                    order.told(act.activation(a_hi[:, (i + NQ) % KD, :], mtmp[:, i % 2, :], ACT.Copy), mhi_ready, L, i)

                for h in range(NH):
                    for kt in range(TB):
                        exponentials(h, kt)
                        if kt == 1 and h >= 1:
                            sums_inverted(h - 1)
                    if h in (1, 2):
                        mixer_square(2 * h - 2)
                        mixer_square(2 * h - 1)
                    if h == 4:
                        mixer_rs(0)
                    if h in (3, 5):
                        mixer_square(NS + (h - 3) // 2)
                    if h in (5, 6):
                        merged_high(2 * h - 10)
                        merged_high(2 * h - 9)
                mixer_square(NS + 2)
                sums_inverted(NH - 1)
                mixer_square(NS + 3)
                mixer_rs(1)
                for i in range(NS, NS + NQ):
                    merged_high(i)

                order.restart()
                with act.Fori(0, PAIRS_O) as j:
                    for s in range(2):
                        hi_next(V + OFF_O + 1 + j, s, KD)
                        split_h(L * 2 + 1, j * 2 + s, s, lambda: act.wait_ge(acc_free.sem, (V + OFF_O + j) * 2 + (s + 3)))
                norm_rstd(L * 2 + 1)
                order.restart()
                for hf in range(2):
                    def feed(j, kt, hf=hf):
                        v = V + OFF_UP[hf] + j
                        for s in range(2):
                            hi_next(v + 1, s, kt)
                            act.wait_ge(acc_free.sem, v * 2 + (s + 3))
                            col = s * NF + hf * HALF + j
                            act.activation(cv[s][:], pad[s][:, 1:SEQ + 1], ACT.Identity,
                                           scale=param(pb, L, 2 * NF + col), bias=param(pc, L, 2 * NF + col))\
                                .then_inc(center_ready.sem, 1)
                        t = hf * HALF + j
                        act.wait_ge(conv_ready.sem, L * 2 * NF + 2 * t + 1)
                        act.activation(cv[0][:], cv[0][:], ACT.Silu).then_inc(silu_ready.sem, 1)
                        act.wait_ge(prod_ready.sem, prod_ready.at(L, t))
                        act.activation(tile(a_hi, j), prod[:], ACT.Copy).then_inc(ahi_ready.sem, 1)

                    act.preload_act_table(ACT.Silu)
                    with act.Fori(0, PAIRS_UP - 1) as j:
                        feed(j, KD)
                    feed(PAIRS_UP - 1, HALF)

                    def drain(j, kt, hf=hf):
                        v = V + OFF_DOWN[hf] + j
                        for s in range(2):
                            hi_next(v + 1, s, kt)
                            if hf == 1:
                                split_h(L * 2 + 2, j * 2 + s, s, lambda: act.wait_ge(acc_free.sem, v * 2 + (s + 3)))

                    with act.Fori(0, PAIRS_DOWN - 1) as j:
                        drain(j, HALF)
                    drain(PAIRS_DOWN - 1, KD)

            act.wait_ge(consts_made.sem, 1)
            act.wait_ge(h_ready.sem, h_ready.at(2 * DEPTH, KD - 1))
            act.dma_start(rope2[:], D["c_rope2"].rearrange("a p n -> p a n")).then_inc(c2_loaded.sem, 16)
            act.dma_start(perm2[:], D["c_perm2"]).then_inc(c2_loaded.sem, 16)
            act.dma_start(tri[:], D["c_tri"]).then_inc(c2_loaded.sem, 16)
            with act.Fori(0, DEPTH) as L:
                V = BASE2 + L * PAIRS2
                G = L * 2 + 2 * DEPTH
                act.wait_ge(consts_made.sem, 1)
                act.wait_ge(h_ready.sem, h_ready.at(G, KD - 1))
                act.dma_start(wab[:], D["w_in_2"].rearrange("l (k p) n -> l p k n", p=P)[ds(L, 1), :, :, N_IN2 * P:N_IN2 * P + 2 * GH]
                              .rearrange("l p k n -> p (l k) n")).then_inc(wab_loaded.sem, 16)
                norm_rstd(G)
                for i in range(N_IN2):
                    hi_next(V + (i // 2 + 1), i % 2, KD)
                    if i < NG + GH or NG + GH + NC <= i < NG + GH + 2 * NC:
                        act.wait_ge(acc_free.sem, V * 2 + i + 3)
                    if i < NG:
                        order.told(act.activation(gqkv[i], zp[:, i % 2, GT - 1:GT - 1 + SEQ], ACT.Copy,
                                                  scale=param(pd, L, D_SC + (GT - 1) * NG + i)), sc_center, L, i)
                        act.wait_ge(sc_ready.sem, sc_ready.at(L, i))
                        order.told(act.activation(gqkv[i], gqkv[i], ACT.Silu), sc_silu, L, i)
                    elif i < NG + GH:
                        h = i - NG
                        order.told(act.activation(gz[:, h, :], gz[:, h, :], ACT.Silu), gate_ready, L, h)
                    elif NG + GH + NC <= i < NG + GH + 2 * NC:
                        t = i - NG - GH - NC
                        order.told(act.activation(cg[:, t, :], cg[:, t, :], ACT.Sigmoid), cg_ready, L, t)
                logs_and_exps()
                act.wait_ge(gate_in.sem, gate_in.at(L, 0))
                order.settle()
                order.step(act.activation(expa[:], gate_par[:, 0, ds(L, 1), :].rearrange("p l h -> p (l h)"), ACT.Exp))
                order.step(act.activation(cols["e"][:], cols["ax"][:], ACT.Exp, scale=-1.0))
                order.told(act.activation(cols["beta"][:], cols["b"][:], ACT.Exp, scale=-1.0), gate_e1, L, 0)
                order.settle()
                order.told(act.activation(cols["l"][:], cols["e"][:], ACT.Ln, bias=ones[:, 0:1]), gate_e2, L, 0)
                for i in range(2 * NA):
                    act.wait_ge(rope2_ready.sem, rope2_ready.at(L, i))
                    order.told(act.activation(qkr2[:, i, :], za[:, i, :], ACT.Copy), qkr2_ready, L, i)
                act.wait_ge(v2ones_ready.sem, v2ones_ready.at(L, 0))
                for i in range(NA):
                    act.wait_ge(v2T_ready.sem, v2T_ready.at(L, i))
                    for r in range(2):
                        ins = act.activation(vaug2[:, 2 * i + r, :, 64 * r:64 * r + 64],
                                             ps[:, TRN[i], :].rearrange("q (k f) -> q k f", f=P)[:, :, 64 * r:64 * r + 64], ACT.Copy)
                        if r:
                            order.told(ins, vaug2_ready, L, i)
                        else:
                            order.step(ins)
                for n in range(AH * TB):
                    act.wait_ge(ST2_ready.sem, ST2_ready.at(L, n))
                    if n >= TB:
                        act.wait_ge(PV2_done.sem, PV2_done.at(L, n - TB))
                    order.told(act.activation(probs2[:, n % TB, :], ps[:, ROT[n % 2], :], ACT.Exp, scale=64 ** -0.5), E2_ready, L, n)
                act.wait_ge(mean_ready.sem, mean_ready.at(L, 0))
                order.told(act.activation(lnt[:], ps[:, STAT[0], :], ACT.Copy, scale=1.0 / CC), mean_kept, L, 0)
                for i in range(NC):
                    act.wait_ge(centered.sem, centered.at(L, i))
                    order.told(act.activation(msq2[:, i % 2, :], yc[:, i, :], ACT.Square), lnsq, L, i)
                act.wait_ge(lnsq_used.sem, lnsq_used.at(L, NC - 1))
                order.settle()
                order.told(rs(mrs2[:, 0, :], ps[:, STAT[1], :], CC, 1), ln_rs, L, 0)
                for i in range(NC):
                    act.wait_ge(ln_scaled.sem, ln_scaled.at(L, i))
                    order.told(act.activation(yc[:, i, :], yc[:, i, :], ACT.Silu, bias=param(pd, L, D_LNB + i)), yc_ready, L, i)
                logs_and_exps()
                for i in range(2 * GH + 1):
                    if i < 2 * GH:
                        if i >= 2:
                            act.wait_ge(l2stat.sem, l2stat.at(L, i - 2))
                        order.told(act.activation(msq2[:, i % 2, :], gqkv[i], ACT.Square), l2sq, L, i)
                    if i >= 1:
                        act.wait_ge(l2stat.sem, l2stat.at(L, i - 1))
                        if i >= 3:
                            act.wait_ge(l2n.sem, l2n.at(L, i - 3))
                        else:
                            act.wait_ge(ln_scaled.sem, ln_scaled.at(L, NC - 1))
                        order.settle()
                        order.told(rs(mrs2[:, (i - 1) % 2, :], ps[:, STAT[(i - 1) % 2], :], 1), l2rs, L, i - 1)
                NCOL = TB * GH
                flat = lambda n: cols[n][:].rearrange("p t h -> p (t h)")
                act.wait_ge(gc_kept.sem, gc_kept.at(L, 0))
                order.step(act.activation(flat("egc"), flat("gc"), ACT.Exp))
                act.wait_ge(dg_ready.sem, dg_ready.at(L, 0))
                order.told(act.activation(flat("egl"), flat("dg"), ACT.Exp), eg_cols, L, 0)
                for h in range(GH):
                    act.wait_ge(gap_ready.sem, gap_ready.at(L, h))
                    if h >= 2:
                        act.wait_ge(head_ready.sem, head_ready.at(L, h - 2))
                    order.told(act.activation(eg[:, h % 2, :], ps[:, ROT[h % 2], :], ACT.Exp), eg_ready, L, h)
                    order.told(act.activation(dm[:, h % 2, :], dm[:, h % 2, :], ACT.Exp), decay_ready, L, h)
                for n in range(GH * LEVELS):
                    act.wait_ge(p1_ready.sem, p1_ready.at(L, n))
                    if n >= 2:
                        act.wait_ge(xpt_ready.sem, xpt_ready.at(L, n - 2))
                    else:
                        act.wait_ge(head_ready.sem, head_ready.at(L, GH - 1))
                    order.told(act.activation(p1[:, n % 2, :], ps[:, ROT[n % 2], :], ACT.Copy), p1_kept, L, n)
                for h in range(GH):
                    act.wait_ge(uu_ready.sem, uu_ready.at(L, h))
                    order.told(act.activation(vb[:, h, :, :].rearrange("p t d -> p (t d)"), ps[:, ROT[h % 2], :], ACT.Copy), uu_kept, L, h)
                act.wait_ge(ww_ready.sem, ww_ready.at(L, GH - 1))
                for c in range(NCH):
                    act.wait_ge(o_ready.sem, o_ready.at(L, c))
                    order.told(act.activation(og[:, :, c * CH:(c + 1) * CH],
                                              ps[:, STAT[c % 2], 0:GH * CH].rearrange("p (h t) -> p h t", t=CH), ACT.Copy), o_kept, L, c)
                order.settle()
                for i in range(GH + 1):
                    if i < GH:
                        if i >= 2:
                            act.wait_ge(ogstat.sem, ogstat.at(L, i - 2))
                        order.told(act.activation(msq2[:, i % 2, :], og[:, i, :], ACT.Square), ogsq, L, i)
                    if i >= 1:
                        act.wait_ge(ogstat.sem, ogstat.at(L, i - 1))
                        if i >= 3:
                            act.wait_ge(og_ready.sem, og_ready.at(L, i - 3))
                        order.settle()
                        order.told(rs(mrs2[:, (i - 1) % 2, :], ps[:, STAT[(i - 1) % 2], :], P), ogrs, L, i - 1)
                act.wait_ge(og_ready.sem, og_ready.at(L, GH - 1))
                for n, src in enumerate(mixed):
                    order.told(act.activation(a_hi[:, n, :], src, ACT.Copy), m2hi_ready, L, n)

                order.settle()
                order.step(act.activation(after_core[:], ones[:, 0:1], ACT.Copy))
                order.restart()

                def post_squares(i, v, j, hi_kt):
                    for s in range(2):
                        hi_next(v + 1, s, hi_kt)
                        act.wait_ge(acc_free.sem, v * 2 + (s + 3))
                        n = j * 2 + s
                        if not (isinstance(j, int) and j == 0):
                            act.wait_ge(yssq_done.sem, yssq_done.at(L, i * KD + n - 2))
                        act.activation(cv[s][:], tile(y, n), ACT.Square).then_inc(ysq_ready.sem, 1)

                def post_norm(i, gen):
                    logs_and_exps()
                    act.wait_ge(ystat_ready.sem, ystat_ready.at(L, i))
                    order.settle()
                    order.told(rs(cv[0][:], ps[:, STAT[1], :], DM), yrs_ready, L, i)
                    order.restart()
                    with act.Fori(0, PAIRS_O) as j:
                        for s in range(2):
                            split_h(gen, j * 2 + s, s, lambda: act.wait_ge(x2_ready.sem, x2_ready.at(L, i * KD + j * 2 + s)))

                post_squares(0, V + OFF_O2, 0, KD)
                with act.Fori(1, PAIRS_O) as j:
                    post_squares(0, V + OFF_O2 + j, j, KD)
                post_norm(0, G + 1)
                norm_rstd(G + 1)
                order.restart()
                for hf in range(2):
                    def feed2(j, kt, hf=hf):
                        v = V + OFF_UP2[hf] + j
                        t = hf * HALF + j
                        hi_next(v + 1, 0, kt)
                        act.wait_ge(acc_free.sem, v * 2 + 3)
                        act.activation(cv[0][:], cv[0][:], ACT.Silu).then_inc(silu2_ready.sem, 1)
                        hi_next(v + 1, 1, kt)
                        act.wait_ge(prod2_ready.sem, prod2_ready.at(L, t))
                        act.activation(tile(a_hi, j), prod[:], ACT.Copy).then_inc(a2hi_ready.sem, 1)

                    act.preload_act_table(ACT.Silu)
                    with act.Fori(0, PAIRS_UP - 1) as j:
                        feed2(j, KD)
                    feed2(PAIRS_UP - 1, HALF)
                    if hf == 0:
                        with act.Fori(0, PAIRS_DOWN - 1) as j:
                            for s in range(2):
                                hi_next(V + OFF_DOWN2[hf] + 1 + j, s, HALF)
                        for s in range(2):
                            hi_next(V + OFF_DOWN2[hf] + PAIRS_DOWN, s, KD)
                    else:
                        post_squares(1, V + OFF_DOWN2[hf], 0, HALF)
                        with act.Fori(1, PAIRS_DOWN - 1) as j:
                            post_squares(1, V + OFF_DOWN2[hf] + j, j, HALF)
                        post_squares(1, V + OFF_DOWN2[hf] + PAIRS_DOWN - 1, PAIRS_DOWN - 1, KD)
                post_norm(1, G + 2)

        @block.vector
        def _(dve):
            order = Order(dve, dve_step.sem, consts_made)
            dve.memset(ones[:], 1.0).then_inc(dve_step.sem, 1)
            dve.memset(eps[:, 0:1], EPS).then_inc(dve_step.sem, 1)
            dve.memset(eps[:, 1:2], LN_EPS).then_inc(dve_step.sem, 1)
            dve.memset(rows[:], 1.0).then_inc(dve_step.sem, 1)
            order.n, order.last = 4, (dve_step.sem, 4)
            order.settle()
            dve.tensor_scalar(negones[:], ones[:], -1.0, None, ALU.mult).then_inc(consts_made.sem, 1)
            dve.wait_ge(consts_made.sem, 1)
            dve.sem_inc(acc_free.sem, 2)
            for i, r in enumerate(ROWS):
                dve.wait_ge(params_turned.sem, i + 1)
                dve.tensor_copy(COLS[i], ps[:, TRN[i % 2], 0:r]).then_inc(params_kept.sem, 1)

            def grown(gen, n, s, first):
                dve.wait_ge(sq_ready.sem, sq_ready.at(gen, n))
                if not first:
                    dve.wait_ge(ssq_done.sem, ssq_done.at(gen, n - 1))
                if first:
                    ins = dve.tensor_copy(ssq[:], sqt[:, s, :])
                else:
                    ins = dve.tensor_tensor(ssq[:], ssq[:], sqt[:, s, :], ALU.add)
                order.told(ins, ssq_done, gen, n)

            def low_half(gen, n):
                dve.wait_ge(hhi_ready.sem, hhi_ready.at(gen, n))
                ins = dve.scalar_tensor_tensor(tile(h_lo, n), tile(x, n), gain(gen * KD + n),
                                               tile(h_hi, n).bitcast(F32), ALU.mult, ALU.subtract)
                order.told(ins, h_ready, gen, n)

            def tail(gen, n, s, first):
                grown(gen, n, s, first)
                low_half(gen, n)

            for n in range(KD):
                dve.wait_ge(x_turned.sem, n + 1)
                order.told(dve.tensor_copy(x[:, n, :], ps[:, ROT[n % 2], :]), x_ready, 0, n)
                tail(0, n, n % 2, n == 0)

            order.restart()
            with dve.Fori(0, DEPTH) as L:
                V = L * PAIRS1
                dve.wait_ge(rstd_ready.sem, rstd_ready.at(L * 2, 0))
                dests = [zv[:], zk[:]] + [t[:, i, :] for t, m in ((zq, NQ), (vv, NS), (u, NS)) for i in range(m)]

                def qk_norm(i):
                    z = dests[i + 1]
                    dve.wait_ge(qkrs_ready.sem, qkrs_ready.at(L, i))
                    order.told(dve.scalar_tensor_tensor(z, z, param(pa, L, 1 if i == 0 else 0), mrs[:, i % 2, :],
                                                        ALU.mult, ALU.mult), qkn_ready, L, i)

                def qk_rotary(i):
                    z = dests[i + 1]
                    dve.wait_ge(rot_ready.sem, rot_ready.at(L, i))
                    order.settle()
                    order.told(dve.tensor_tensor(t2[:], ps[:, ROT[i % 2], :], rope[:, 1, :], ALU.mult), rot_used, L, i)
                    order.step(dve.tensor_tensor(t1[:], z, rope[:, 0, :], ALU.mult))
                    order.settle()
                    order.told(dve.tensor_tensor(z, t1[:], t2[:], ALU.add), rope_ready, L, i)

                def qk_low(i):
                    dve.wait_ge(qr_ready.sem, qr_ready.at(L, i))
                    if i == 0:
                        order.step(dve.tensor_tensor(kl[0][:], kd[0], kr[0][:].bitcast(F32), ALU.subtract))
                        order.told(dve.tensor_tensor(kl[1][:], kd[1], kr[1][:].bitcast(F32), ALU.subtract), ql_ready, L, 0)
                    else:
                        order.step(dve.tensor_tensor(qab[64:128, i - 1, 0, :], zq[0:64, i - 1, :],
                                                     qab[0:64, i - 1, 0, :].bitcast(F32), ALU.subtract))
                        order.told(dve.tensor_tensor(qab[0:64, i - 1, 1, :], zq[64:128, i - 1, :],
                                                     qab[64:128, i - 1, 1, :].bitcast(F32), ALU.subtract), ql_ready, L, i)

                def vv_norm(t):
                    dve.wait_ge(vvrs_ready.sem, vvrs_ready.at(L, t))
                    order.told(dve.scalar_tensor_tensor(vv[:, t, :], vv[:, t, :], param(pa, L, 2 + t), mrs[:, t % 2, :],
                                                        ALU.mult, ALU.mult), vvn_ready, L, t)

                for i, z in enumerate(dests):
                    dve.wait_ge(unit_done.sem, V * 2 + i + 3)
                    dve.tensor_tensor(z, ps[:, ACC[i % 2], :], rstd[:], ALU.mult).then_inc(acc_free.sem, 1)
                    order.last = (acc_free.sem, V * 2 + i + 3)
                    if i == 1:
                        for g in range(NKV):
                            for r in range(2):
                                ins = dve.memset(vaug[:, g, r, :, 64 - 64 * r:128 - 64 * r], 1.0)
                                if (g, r) == (NKV - 1, 1):
                                    order.told(ins, vones_ready, L, 0)
                                else:
                                    order.step(ins)
                    if 0 <= i - 3 <= NQ:
                        qk_rotary(i - 3)
                    if 0 <= i - 2 <= NQ:
                        qk_norm(i - 2)
                    if 0 <= i - 5 <= NQ:
                        qk_low(i - 5)
                    if i in (11, 13):
                        vv_norm(i - 11)
                        vv_norm(i - 10)

                def row_max(h):
                    for b in range(2):
                        dve.wait_ge(S_ready.sem, S_ready.at(L, 2 * h + b))
                        order.settle()
                        order.told(dve.tensor_reduce(mx[:, h % 2, 2 * b:2 * b + 2], ps[:, STAT[0]:STAT[1] + 1, :], AX, ALU.max),
                                   S_used, L, 2 * h + b)
                    if h >= 2:
                        dve.wait_ge(ST_ready.sem, ST_ready.at(L, (h - 1) * TB - 1))
                    order.settle()
                    order.told(dve.tensor_tensor(diag[:, h % 2, :, :], ident[:].unsqueeze(1).to_broadcast([P, TB, P]),
                                                 mx[:, h % 2, :].unsqueeze(2).to_broadcast([P, TB, P]), ALU.mult),
                               diag_ready, L, h)

                def gating(t):
                    dve.wait_ge(mix_ready.sem, mix_ready.at(L, t))
                    order.settle()
                    order.told(dve.tensor_tensor(
                        t1[:].rearrange("p (c q) -> p c q", q=P), ps[:, ACC[t % 2], :].rearrange("p (c q) -> p c q", q=P),
                        sgb[:, t, :].unsqueeze(1).to_broadcast([P, TB, P]), ALU.add), mix_used, L, t)
                    dve.wait_ge(gelu_ready.sem, gelu_ready.at(L, NS + t))
                    order.settle()
                    order.told(dve.tensor_tensor(u[:, t, :], u[:, t, :], t1[:], ALU.mult), sg_ready, L, t)

                def normed(h):
                    t, r = h // 2, 64 * (h % 2)
                    dve.wait_ge(rl_ready.sem, rl_ready.at(L, h))
                    order.told(dve.tensor_tensor(ao[r:r + 64, t, :], ps[r:r + 64, TRN[h % 2], :], mrs[r:r + 64, 0, :], ALU.mult),
                               ao_ready, L, h)

                def merge(i):
                    if i % NS == 0:
                        dve.wait_ge(ors_ready.sem, ors_ready.at(L, i // NS))
                    z, g = (u[:, i, :], 6 + NQ + i) if i < NS else (ao[:, i - NS, :], 6 + i - NS)
                    order.settle()
                    order.told(dve.scalar_tensor_tensor(mtmp[:, i % 2, :], z, param(pa, L, g), ors[:, i // NS, :],
                                                        ALU.mult, ALU.mult), mtmp_ready, L, i)

                def merged_low(i):
                    dve.wait_ge(mhi_ready.sem, mhi_ready.at(L, i))
                    k = (i + NQ) % KD
                    order.told(dve.tensor_tensor(a_lo[:, k, :], mtmp[:, i % 2, :], a_hi[:, k, :].bitcast(F32), ALU.subtract),
                               merged_ready, L, i)

                dve.wait_ge(sgb_loaded.sem, L * 32 + 32)
                row_max(0)
                gating(0)
                gating(1)
                for h in range(NH):
                    if h + 1 < NH:
                        row_max(h + 1)
                    if h >= 1:
                        normed(h - 1)
                    if h == 1:
                        gating(2)
                        gating(3)
                    if h == 6:
                        merged_low(0)
                        merged_low(1)
                    if h in (5, 6):
                        merge(2 * h - 10)
                        merge(2 * h - 9)
                    if h == 7:
                        merged_low(2)
                        merged_low(3)
                normed(NH - 1)
                for i in range(NS, NS + NQ + 1):
                    if i < NS + NQ:
                        merge(i)
                    if i > NS:
                        merged_low(i - 1)

                def residual(v, s, n):
                    dve.wait_ge(unit_done.sem, v * 2 + (s + 3))
                    dve.tensor_tensor(tile(x, n), tile(x, n), ps[:, ACC[s], :], ALU.add).then_inc(acc_free.sem, 1)
                    order.last = (acc_free.sem, v * 2 + (s + 3))

                def residual_norm(gen, v, j, first):
                    for s in range(2):
                        residual(v, s, j * 2 + s)
                        tail(gen, j * 2 + s, s, first and s == 0)

                order.restart()
                residual_norm(L * 2 + 1, V + OFF_O, 0, True)
                order.restart()
                with dve.Fori(1, PAIRS_O) as j:
                    residual_norm(L * 2 + 1, V + OFF_O + j, j, False)
                    order.restart()
                order.settle()
                for s in range(2):
                    for e in (0, SEQ + 1):
                        order.step(dve.memset(pad[s][:, e:e + 1], 0.0))
                order.restart()
                order.wait_alone(rstd_ready.sem, rstd_ready.at(L * 2 + 1, 0))
                for hf in range(2):
                    with dve.Fori(0, PAIRS_UP) as j:
                        v = V + OFF_UP[hf] + j
                        for s in range(2):
                            dve.wait_ge(unit_done.sem, v * 2 + (s + 3))
                            if s == 0:
                                order.settle()
                            dve.tensor_tensor(pad[s][:, 1:SEQ + 1], ps[:, ACC[s], :], rstd[:], ALU.mult)\
                                .then_inc(acc_free.sem, 1)
                            col = s * NF + hf * HALF + j
                            i = 2 * (hf * HALF + j) + s
                            dve.wait_ge(center_ready.sem, L * 2 * NF + i + 1)
                            order.step(dve.scalar_tensor_tensor(cv[s][:], pad[s][:, 0:SEQ], param(pb, L, col), cv[s][:],
                                                                ALU.mult, ALU.add))
                            order.settle()
                            order.told(dve.scalar_tensor_tensor(cv[s][:], pad[s][:, 2:SEQ + 2], param(pc, L, col), cv[s][:],
                                                                ALU.mult, ALU.add), conv_ready, L, i)
                        t = hf * HALF + j
                        dve.wait_ge(silu_ready.sem, silu_ready.at(L, t))
                        order.settle()
                        order.told(dve.tensor_tensor(prod[:], cv[0][:], cv[1][:], ALU.mult), prod_ready, L, t)
                        dve.wait_ge(ahi_ready.sem, ahi_ready.at(L, t))
                        order.told(dve.tensor_tensor(tile(a_lo, j), prod[:], tile(a_hi, j).bitcast(F32), ALU.subtract),
                                   a_ready, L, t)
                        order.restart()
                    if hf == 0:
                        with dve.Fori(0, PAIRS_DOWN) as j:
                            for s in range(2):
                                residual(V + OFF_DOWN[hf] + j, s, j * 2 + s)
                            order.restart()
                    else:
                        residual_norm(L * 2 + 2, V + OFF_DOWN[hf], 0, True)
                        order.restart()
                        with dve.Fori(1, PAIRS_DOWN) as j:
                            residual_norm(L * 2 + 2, V + OFF_DOWN[hf] + j, j, False)
                            order.restart()

            with dve.Fori(0, DEPTH) as L:
                V = BASE2 + L * PAIRS2
                G = L * 2 + 2 * DEPTH
                dve.wait_ge(rstd_ready.sem, rstd_ready.at(G, 0))
                order.step(dve.memset(zp[:, :, 0:GT - 1], 0.0))
                order.step(dve.memset(ypad[:, :, 0:CT - 1], 0.0))
                for i in range(NA):
                    order.step(dve.memset(vaug2[:, 2 * i, :, 64:128], 1.0))
                    ins = dve.memset(vaug2[:, 2 * i + 1, :, 0:64], 1.0)
                    if i == NA - 1:
                        order.told(ins, v2ones_ready, L, 0)
                    else:
                        order.step(ins)
                dve.wait_ge(wab_loaded.sem, L * 16 + 16)
                order.settle()
                order.told(dve.tensor_copy(wab_hi[:], wab[:]), wab_split, L, 0)
                order.settle()
                order.told(dve.tensor_tensor(wab_lo[:], wab[:], wab_hi[:].bitcast(F32), ALU.subtract), wab_split, L, 1)

                def project(i, dst):
                    dve.wait_ge(unit_done.sem, V * 2 + i + 3)
                    order.settle()
                    dve.tensor_tensor(dst, ps[:, ACC[i % 2], :], rstd[:], ALU.mult).then_inc(acc_free.sem, 1)
                    order.last = (acc_free.sem, V * 2 + i + 3)

                for i in range(NG):
                    project(i, zp[:, i % 2, GT - 1:GT - 1 + SEQ])
                    dve.wait_ge(sc_center.sem, sc_center.at(L, i))
                    for k in range(GT - 1):
                        order.settle()
                        ins = dve.scalar_tensor_tensor(gqkv[i], zp[:, i % 2, k:k + SEQ], param(pd, L, D_SC + k * NG + i), gqkv[i],
                                                       ALU.mult, ALU.add)
                        if k == GT - 2:
                            order.told(ins, sc_ready, L, i)
                        else:
                            order.step(ins)
                for h in range(GH):
                    project(NG + h, gz[:, h, :])
                at = NG + GH
                for t in range(NC):
                    project(at + t, ypad[:, t, CT - 1:])
                for t in range(NC):
                    project(at + NC + t, cg[:, t, :])
                at += 2 * NC

                def taps(k0, k1):
                    for k in range(k0, k1):
                        for t in range(NC):
                            w = param(pd, L, D_DW + k * NC + t)
                            src = ypad[:, t, k:k + SEQ]
                            if k == 0:
                                ins = dve.tensor_scalar(yc[:, t, :], src, w, param(pd, L, D_BIAS + t), ALU.mult, ALU.add)
                            else:
                                ins = dve.scalar_tensor_tensor(yc[:, t, :], src, w, yc[:, t, :], ALU.mult, ALU.add)
                            if k == CT - 1:
                                order.told(ins, dw_ready, L, t)
                            else:
                                order.step(ins)
                        order.settle()

                n_att = 3 * NA
                for i in range(n_att):
                    project(at + i, za[:, i, :])
                    if i == 0:
                        for t in range(NC):
                            dve.wait_ge(cg_ready.sem, cg_ready.at(L, t))
                            order.step(dve.tensor_tensor(ypad[:, t, CT - 1:], ypad[:, t, CT - 1:], cg[:, t, :], ALU.mult))
                        order.settle()
                    taps(CT * i // n_att, CT * (i + 1) // n_att)

                dve.wait_ge(rcol_ready.sem, rcol_ready.at(L, 0))
                order.told(dve.tensor_copy(rcol[:], ps[:, TRN[0], :].rearrange("p (t q) -> p t q", q=P)[:, :, 0:1]
                                           .rearrange("p t q -> p (t q)")), rcol_kept, L, 0)
                order.settle()
                dve.wait_ge(ab_ready.sem, ab_ready.at(L, 0))
                abp = ps[:, TRN[1], 0:TB * 2 * GH].rearrange("p (t c) -> p t c", c=2 * GH)
                rb = rcol[:].unsqueeze(2).to_broadcast([P, TB, GH])
                dtb = gate_par[:, 1, ds(L, 1), :].to_broadcast([P, TB, GH])
                order.step(dve.tensor_tensor(cols["a"][:], abp[:, :, 0:GH], rb, ALU.mult))
                order.step(dve.tensor_tensor(cols["b"][:], abp[:, :, GH:2 * GH], rb, ALU.mult))
                order.settle()
                order.step(dve.tensor_tensor(cols["a"][:], cols["a"][:], dtb, ALU.add))
                order.settle()
                order.step(dve.tensor_scalar(cols["ax"][:], cols["a"][:], -1.0, None, ALU.mult))
                order.settle()
                order.told(dve.tensor_tensor(cols["ax"][:], cols["ax"][:], cols["a"][:], ALU.max), gate_in, L, 0)
                dve.wait_ge(gate_e1.sem, gate_e1.at(L, 0))
                order.step(dve.tensor_scalar(cols["beta"][:], cols["beta"][:], 1.0, None, ALU.add))
                order.settle()
                order.step(dve.reciprocal(cols["beta"][:], cols["beta"][:]))
                dve.wait_ge(gate_e2.sem, gate_e2.at(L, 0))
                order.step(dve.scalar_tensor_tensor(cols["a"][:], cols["a"][:], 0.0, cols["l"][:], ALU.max, ALU.add))
                order.settle()
                order.told(dve.scalar_tensor_tensor(cols["g"][:], cols["a"][:], -1.0,
                                                    expa[:].unsqueeze(1).to_broadcast([P, TB, GH]), ALU.mult, ALU.mult), g_ready, L, 0)
                dve.wait_ge(c2_loaded.sem, 3 * 16)
                for i in range(2 * NA):
                    z = za[:, i, :]
                    dve.wait_ge(rot2_ready.sem, rot2_ready.at(L, i))
                    order.settle()
                    order.told(dve.tensor_tensor(ta[:], ps[:, ROT[i % 2], :], rope2[:, 1, :], ALU.mult), rot2_used, L, i)
                    order.step(dve.tensor_tensor(tb2[:], z, rope2[:, 0, :], ALU.mult))
                    order.settle()
                    order.told(dve.tensor_tensor(z, ta[:], tb2[:], ALU.add), rope2_ready, L, i)
                dve.wait_ge(c2_cast.sem, 5 * 16)

                def row_max(h):
                    for b in range(2):
                        dve.wait_ge(S2_ready.sem, S2_ready.at(L, 2 * h + b))
                        order.settle()
                        order.told(dve.tensor_reduce(mx2[:, h % 2, 2 * b:2 * b + 2], ps[:, STAT[0]:STAT[1] + 1, :], AX, ALU.max),
                                   S2_used, L, 2 * h + b)

                row_max(0)
                for h in range(AH):
                    if h >= 1:
                        dve.wait_ge(ST2_ready.sem, ST2_ready.at(L, h * TB - 1))
                    order.settle()
                    order.told(dve.tensor_tensor(diag2[:], ident[:].unsqueeze(1).to_broadcast([P, TB, P]),
                                                 mx2[:, h % 2, :].unsqueeze(2).to_broadcast([P, TB, P]), ALU.mult), diag2_ready, L, h)
                    if h + 1 < AH:
                        row_max(h + 1)
                    for kt in range(TB):
                        n = h * TB + kt
                        dve.wait_ge(E2_ready.sem, E2_ready.at(L, n))
                        o = (TB - 1 - kt) * P
                        order.told(dve.tensor_tensor(probs2[:, kt, :], probs2[:, kt, :], times[:, o:o + SEQ], ALU.mult), P2_ready, L, n)
                    t, r = h // 2, 64 * (h % 2)
                    dve.wait_ge(PV2_done.sem, PV2_done.at(L, h * TB + TB - 1))
                    order.settle()
                    order.step(dve.reciprocal(ta[r:r + 64, :], ps[64 - r:128 - r, TRN[h % 2], :]))
                    order.settle()
                    order.told(dve.tensor_tensor(ya[r:r + 64, t, :], ps[r:r + 64, TRN[h % 2], :], ta[r:r + 64, :], ALU.mult), ya_ready, L, h)
                dve.wait_ge(mean_kept.sem, mean_kept.at(L, 0))
                for i in range(NC):
                    order.told(dve.tensor_tensor(yc[:, i, :], yc[:, i, :], lnt[:], ALU.subtract), centered, L, i)
                dve.wait_ge(ln_rs.sem, ln_rs.at(L, 0))
                for i in range(NC):
                    order.settle()
                    order.told(dve.scalar_tensor_tensor(yc[:, i, :], yc[:, i, :], param(pd, L, D_LNG + i), mrs2[:, 0, :],
                                                        ALU.mult, ALU.mult), ln_scaled, L, i)
                for i in range(2 * GH):
                    dve.wait_ge(l2rs.sem, l2rs.at(L, i))
                    order.told(dve.scalar_tensor_tensor(gqkv[i], gqkv[i], float(P) ** -0.5 if i < GH else 1.0, mrs2[:, i % 2, :],
                                                        ALU.mult, ALU.mult), l2n, L, i)
                NCOL = TB * GH
                flat = lambda n: cols[n][:].rearrange("p t h -> p (t h)")
                dve.wait_ge(G_ready.sem, G_ready.at(L, 0))
                order.told(dve.tensor_copy(flat("gc"), ps[:, TRN[0], 0:NCOL]), gc_kept, L, 0)
                order.settle()
                order.told(dve.tensor_tensor(flat("dg"), ps[:, TRN[0], NCOL:2 * NCOL], flat("gc"), ALU.subtract), dg_ready, L, 0)
                dve.wait_ge(eg_cols.sem, eg_cols.at(L, 0))
                order.told(dve.tensor_tensor(flat("beg"), flat("beta"), flat("egc"), ALU.mult), beg_ready, L, 0)
                order.settle()

                def by_token(t):
                    return t.rearrange("p (t d) -> p t d", d=P)

                def column(n, h):
                    return cols[n][:, :, h:h + 1].to_broadcast([P, TB, P])

                for h in range(GH):
                    s = h % 2
                    dve.wait_ge(grow_ready.sem, grow_ready.at(L, h))
                    order.settle()
                    order.step(dve.tensor_tensor(by_token(dm[:, s, :]), by_token(ps[:, ROT[s], :]), column("gc", h), ALU.subtract))
                    order.settle()
                    order.told(dve.tensor_scalar(dm[:, s, :], dm[:, s, :], 0.0, None, ALU.min), gap_ready, L, h)
                    dve.wait_ge(brow_ready.sem, brow_ready.at(L, h))
                    order.told(dve.tensor_tensor(kb[:, s, :], ps[:, STAT[s], :], gk[:, h, :], ALU.mult), kb_ready, L, h)
                    dve.wait_ge(kT_ready.sem, kT_ready.at(L, h))
                    order.step(dve.tensor_tensor(kbeg[:, h, :, :], by_token(ps[:, TRN[0], :]), column("beg", h), ALU.mult))
                    order.step(dve.tensor_tensor(kout[:, h, :, :], by_token(ps[:, TRN[0], :]), column("egl", h), ALU.mult))
                    dve.wait_ge(gvT_ready.sem, gvT_ready.at(L, h))
                    order.told(dve.tensor_tensor(vb[:, h, :, :], by_token(ps[:, TRN[1], :]), column("beta", h), ALU.mult), turned_used, L, h)
                    dve.wait_ge(decay_ready.sem, decay_ready.at(L, h))
                    dve.wait_ge(kk_ready.sem, kk_ready.at(L, h))
                    order.settle()
                    order.step(dve.tensor_tensor(gv[:, h, :], ps[:, ACC[0], :], dm[:, s, :], ALU.mult))
                    dve.wait_ge(qk_ready.sem, qk_ready.at(L, h))
                    order.step(dve.tensor_tensor(intraT[:, h, :], ps[:, ACC[1], :], dm[:, s, :], ALU.mult))
                    order.settle()
                    order.step(dve.tensor_tensor(by_token(intraT[:, h, :]), by_token(intraT[:, h, :]),
                                                 tri[:].unsqueeze(1).to_broadcast([P, TB, P]), ALU.mult))
                    dve.wait_ge(eg_ready.sem, eg_ready.at(L, h))
                    order.step(dve.tensor_tensor(gq[:, h, :], gq[:, h, :], eg[:, s, :], ALU.mult))
                    order.step(dve.tensor_copy(eg_last[:, h, :], eg[:, s, CH - 1::CH]))
                    for t in (gk, xT):
                        ins = dve.tensor_copy(by_token(t[:, h, :]), ident[:].unsqueeze(1).to_broadcast([P, TB, P]))
                        if t is xT:
                            order.told(ins, head_ready, L, h)
                        else:
                            order.step(ins)
                for n in range(GH * LEVELS + 2):
                    if n < GH * LEVELS:
                        if n >= 2:
                            dve.wait_ge(p1_ready.sem, p1_ready.at(L, n - 2))
                        order.settle()
                        order.told(dve.tensor_tensor(by_token(lt[:, n % 2, :]), by_token(gv[:, n % GH, :]),
                                                     lev[:, n // GH, :].unsqueeze(1).to_broadcast([P, TB, P]), ALU.mult), lt_ready, L, n)
                    m = n - 2
                    if m >= 0:
                        h = m % GH
                        dve.wait_ge(xp_ready.sem, xp_ready.at(L, m))
                        dve.wait_ge(xpt_ready.sem, xpt_ready.at(L, m))
                        order.step(dve.tensor_tensor(gk[:, h, :], gk[:, h, :], ps[:, STAT[m % 2], :], ALU.subtract))
                        order.told(dve.tensor_tensor(xT[:, h, :], xT[:, h, :], ps[:, TRN[m % 2], :], ALU.subtract), x_new, L, m)
                for h in range(GH):
                    dve.wait_ge(ww_ready.sem, ww_ready.at(L, h))
                    order.told(dve.tensor_copy(kbeg[:, h, :, :].rearrange("p t d -> p (t d)"), ps[:, STAT[h % 2], :]), ww_kept, L, h)
                order.told(dve.memset(state, 0.0), state_ready, L, 0)
                for c in range(NCH):
                    tb, r = c // 2, CH * (c % 2)
                    dve.wait_ge(ws_ready.sem, ws_ready.at(L, c))
                    if c == 0:
                        dve.wait_ge(uu_kept.sem, uu_kept.at(L, GH - 1))
                    order.told(dve.tensor_tensor(vn[r:r + CH, :, :], vb[r:r + CH, :, tb, :],
                                                 ps[r:r + CH, ROT[c % 2], :].rearrange("p (h d) -> p h d", d=P), ALU.subtract), vn_ready, L, c)
                    if c < NCH - 1:
                        dve.wait_ge(ds_ready.sem, ds_ready.at(L, c))
                        order.settle()
                        for h in range(GH):
                            ins = dve.scalar_tensor_tensor(state[:, h, :], state[:, h, :], eg_last[:, h, c:c + 1],
                                                           ps[:, TRN[c % 2], h * P:(h + 1) * P], ALU.mult, ALU.add)
                            if h == GH - 1:
                                order.told(ins, state_ready, L, c + 1)
                            else:
                                order.step(ins)
                for h in range(GH):
                    dve.wait_ge(ogrs.sem, ogrs.at(L, h))
                    order.step(dve.scalar_tensor_tensor(og[:, h, :], og[:, h, :], param(pd, L, D_ON), mrs2[:, h % 2, :], ALU.mult, ALU.mult))
                    order.settle()
                    order.told(dve.tensor_tensor(og[:, h, :], og[:, h, :], gz[:, h, :], ALU.mult), og_ready, L, h)
                for n, src in enumerate(mixed):
                    dve.wait_ge(m2hi_ready.sem, m2hi_ready.at(L, n))
                    order.settle()
                    order.told(dve.tensor_tensor(a_lo[:, n, :], src, a_hi[:, n, :].bitcast(F32), ALU.subtract), merged2_ready, L, n)
                order.restart()

                def branch(i, v, j, more):
                    for s in range(2):
                        n = j * 2 + s
                        dve.wait_ge(unit_done.sem, v * 2 + (s + 3))
                        if more:
                            ins = dve.tensor_tensor(tile(y, n), tile(y, n), ps[:, ACC[s], :], ALU.add)
                        else:
                            ins = dve.tensor_copy(tile(y, n), ps[:, ACC[s], :])
                        ins.then_inc(acc_free.sem, 1)
                        order.last = (acc_free.sem, v * 2 + (s + 3))
                        if i is None:
                            continue
                        dve.wait_ge(ysq_ready.sem, ysq_ready.at(L, i * KD + n))
                        if isinstance(n, int) and n == 0:
                            ins = dve.tensor_copy(prod[:], cv[s][:])
                        else:
                            dve.wait_ge(yssq_done.sem, yssq_done.at(L, i * KD + n - 1))
                            ins = dve.tensor_tensor(prod[:], prod[:], cv[s][:], ALU.add)
                        order.told(ins, yssq_done, L, i * KD + n)
                    order.restart()

                def post_norm(i, gen):
                    dve.wait_ge(yrs_ready.sem, yrs_ready.at(L, i))

                    for n in range(KD + 1):
                        if n < KD:
                            scaled = (cv[1], prod)[n % 2]
                            order.step(dve.scalar_tensor_tensor(scaled[:], y[:, n, :], gain(L * 2 * KD + ((GENS + i) * KD + n)), cv[0][:],
                                                                ALU.mult, ALU.mult))
                            order.settle()
                            order.told(dve.tensor_tensor(x[:, n, :], x[:, n, :], scaled[:], ALU.add), x2_ready, L, i * KD + n)
                        if n == 1:
                            grown(gen, 0, 0, True)
                        if n >= 1:
                            low_half(gen, n - 1)
                    order.restart()

                branch(0, V + OFF_O2, 0, False)
                with dve.Fori(1, PAIRS_O) as j:
                    branch(0, V + OFF_O2 + j, j, False)
                post_norm(0, G + 1)
                for hf in range(2):
                    with dve.Fori(0, PAIRS_UP) as j:
                        v = V + OFF_UP2[hf] + j
                        t = hf * HALF + j
                        dve.wait_ge(rstd_ready.sem, rstd_ready.at(G + 1, 0))
                        for s in range(2):
                            dve.wait_ge(unit_done.sem, v * 2 + (s + 3))
                            dve.tensor_tensor(cv[s][:], ps[:, ACC[s], :], rstd[:], ALU.mult).then_inc(acc_free.sem, 1)
                            order.last = (acc_free.sem, v * 2 + (s + 3))
                        dve.wait_ge(silu2_ready.sem, silu2_ready.at(L, t))
                        order.settle()
                        order.told(dve.tensor_tensor(prod[:], cv[0][:], cv[1][:], ALU.mult), prod2_ready, L, t)
                        dve.wait_ge(a2hi_ready.sem, a2hi_ready.at(L, t))
                        order.told(dve.tensor_tensor(tile(a_lo, j), prod[:], tile(a_hi, j).bitcast(F32), ALU.subtract), a2_ready, L, t)
                        order.restart()
                    if hf == 0:
                        with dve.Fori(0, PAIRS_DOWN) as j:
                            branch(None, V + OFF_DOWN2[hf] + j, j, False)
                    else:
                        branch(1, V + OFF_DOWN2[hf], 0, True)
                        with dve.Fori(1, PAIRS_DOWN) as j:
                            branch(1, V + OFF_DOWN2[hf] + j, j, True)
                post_norm(1, G + 2)

            for i in range(TB * 2):
                tb, hf = i // 2, i % 2
                dve.wait_ge(out_turned.sem, i + 1)
                dve.tensor_copy(xs[:, tb, hf * SEQ:(hf + 1) * SEQ], ps[:, ROT[i % 2], :]).then_inc(out_kept.sem, 1)


def constants(seq, head_dim, grid_w, theta, patterns):
    import numpy as np

    f = np.float32
    ident = np.eye(P, dtype=f)
    blk = np.kron(np.eye(2, dtype=f), np.ones((64, 64), f))
    half = head_dim // 2
    inv = f(1) / (f(theta) ** (np.arange(0, half, 2, dtype=f) / f(half)))
    pos = np.arange(seq)
    rope, perm = np.zeros((2, P, seq), f), np.zeros((P, P), f)
    for p in range(P):
        d = p % head_dim
        axis = (pos // grid_w if d < half else pos % grid_w).astype(f)
        i = d % half
        ang = axis * inv[i % (half // 2)]
        rope[0, p], rope[1, p] = np.cos(ang), np.sin(ang) * (f(-1) if i < half // 2 else f(1))
        perm[p ^ (half // 2), p] = 1
    half = head_dim // 2
    inv = np.exp(f(-math.log(theta)) * np.arange(half, dtype=f) * f(2.0 / head_dim))
    rope2, perm2 = np.zeros((2, P, seq), f), np.zeros((P, P), f)
    for p in range(P):
        d = p % head_dim
        ang = pos.astype(f) * inv[d % half]
        rope2[0, p], rope2[1, p] = np.cos(ang), np.sin(ang) * (f(-1) if d < half else f(1))
        perm2[p ^ half, p] = 1
    def held(d):
        return sum((d >= 0) & (d <= window) & (d % dilation == 0) for window, dilation in patterns).astype(f)

    p, c = np.arange(P)[:, None], np.arange(2 * seq - P)[None, :]
    by_query, by_key = held(p + (seq - P) - c), held(c - (seq - P) - p)
    low = lambda n: np.where(n > 0, f(0), f(-1e30))
    j, i = np.arange(P)[:, None], np.arange(P)[None, :]
    tri = ((j // 64 == i // 64) & (j <= i)).astype(f)
    lev = np.stack([((j // (2 << s) == i // (2 << s)) & (j // (1 << s) < i // (1 << s))).astype(f) for s in range(6)])
    return {"c_ident": ident, "c_blk": blk, "c_rope": rope, "c_perm": perm, "c_rope2": rope2, "c_perm2": perm2,
            "c_mask_s": low(by_query), "c_mask_t": low(by_key), "c_times": by_key, "c_tri": tri, "c_lev": lev}


def kernel(**inputs):
    import numpy as np
    import concourse.bacc as bacc
    from concourse.bass_utils import run_bass_kernel_spmd

    nc = bacc.Bacc("TRN2", target_bir_lowering=False, num_devices=1)
    arrays = {f"in_{n}": np.ascontiguousarray(a) for n, a in inputs.items()}
    arrays |= {f"in_{n}": a for n, a in constants(inputs["x"].shape[1], inputs["q_norm_g"].shape[1], 64, 10000.0,
                                                        ((128, 1), (512, 4), (2048, 16))).items()}
    D = {n[3:]: nc.dram_tensor(n, a.shape, mybir.dt.from_np(a.dtype), kind="ExternalInput").ap() for n, a in arrays.items()}
    out = nc.dram_tensor("out", inputs["x"].shape, F32, kind="ExternalOutput").ap()
    network(nc, D, out)
    r = run_bass_kernel_spmd(nc, [arrays], core_ids=[0])
    return r.results[0]["out"]
```

```python
import math
from contextlib import ExitStack

import concourse.bass as bass
from concourse import mybir

P = 128
F32 = mybir.dt.float32
F32R = mybir.dt.float32r
BF16 = mybir.dt.bfloat16
ALU = mybir.AluOpType
ACT = mybir.ActivationFunctionType
AX = mybir.AxisListType.X
ds = bass.ds


class Signal:

    def __init__(self, sem, per=1, base=0):
        self.sem, self.per, self.base = sem, per, base

    def at(self, layer, i):
        return layer * self.per + (i + (self.base + 1))


class Order:

    def __init__(self, eng, sem, begun):
        self.eng, self.sem, self.n, self.last, self.begun = eng, sem, 0, None, begun

    def step(self, ins):
        self.n += 1
        ins.then_inc(self.sem, 1)
        self.last = (self.sem, self.n)

    def told(self, ins, signal, layer, i):
        ins.then_inc(signal.sem, 1)
        self.last = (signal.sem, signal.at(layer, i))

    def settle(self):
        if self.last is not None:
            self.eng.wait_ge(*self.last)

    def wait_alone(self, sem, value, own=None):
        self.eng.wait_ge(*(own or (self.begun.sem, 1)))
        self.eng.wait_ge(sem, value)

    def restart(self):
        own = (self.sem, self.n) if self.n else (self.begun.sem, 1)
        if self.last is not None and self.last[0] is not self.sem:
            self.wait_alone(*self.last, own)
        else:
            self.eng.wait_ge(*own)
        if self.n:
            self.eng.sem_clear(self.sem)
        self.n, self.last = 0, None


def network(nc, D, out, stop=None):
    SEQ, DM = D["x"].shape[1:]
    DEPTH = D["w_in"].shape[0]
    KD = DM // P
    TB = SEQ // P
    EPS = 1e-6
    LN_EPS = 1e-5

    HD = D["q_norm_g"].shape[1]
    AW = D["attn_out_g"].shape[1]
    SGW = D["sg_out_g"].shape[1]
    SGH = D["sg_w"].shape[1]
    INW = D["w_in"].shape[2]
    KVW = (INW - AW - 2 * SGW) // 2
    NH, NKV = AW // HD, KVW // HD
    GROUP = NH // NKV
    NQ, NS = AW // P, SGW // P
    N_IN = INW // P
    FF = D["w_down"].shape[1]
    NF = FF // P
    HALF = NF // 2
    TAPS = D["conv_w"].shape[1]
    assert (KD, TB, SEQ, N_IN, NQ, NS, KVW, HALF * 2, TAPS) == (8, 4, 512, 14, 4, 4, P, NF, 3)

    PAIRS_IN, PAIRS_O, PAIRS_UP, PAIRS_DOWN = N_IN // 2, KD // 2, HALF, KD // 2
    OFF_O = PAIRS_IN
    OFF_UP = [OFF_O + PAIRS_O + hf * (PAIRS_UP + PAIRS_DOWN) for hf in range(2)]
    OFF_DOWN = [o + PAIRS_UP for o in OFF_UP]
    PAIRS1 = OFF_DOWN[1] + PAIRS_DOWN

    CC = D["conv_dw_2"].shape[2]
    CT = D["conv_dw_2"].shape[1]
    GH = D["gdn_a_log_2"].shape[1]
    GT = D["gdn_short_conv_2"].shape[1]
    GW = D["gdn_short_conv_2"].shape[2] // 3
    AH = (DM - CC - GW) // 64
    CH = 64
    NCH = SEQ // CH
    NC, NA, NG = CC // P, AH // 2, 3 * GH
    LEVELS = 6
    N_IN2 = 3 * NA + 2 * NC + 4 * GH
    assert GW // GH == P and D["w_gate_2"].shape[2] == FF and N_IN2 % 2 == 0 and CH == 2 ** LEVELS == P // 2
    PAIRS_IN2 = N_IN2 // 2
    OFF_O2 = PAIRS_IN2
    OFF_UP2 = [OFF_O2 + PAIRS_O + hf * (PAIRS_UP + PAIRS_DOWN) for hf in range(2)]
    OFF_DOWN2 = [o + PAIRS_UP for o in OFF_UP2]
    PAIRS2 = OFF_DOWN2[1] + PAIRS_DOWN
    BASE2 = DEPTH * PAIRS1
    PAIRS = BASE2 + DEPTH * PAIRS2
    D_DW, D_BIAS = 0, CT * NC
    D_LNG, D_LNB = D_BIAS + NC, D_BIAS + 2 * NC
    D_SC = D_BIAS + 3 * NC
    D_ON = D_SC + GT * NG
    N_PD = D_ON + 1

    with ExitStack() as ctx:
        def sb(name, shape, dt=F32, on=ctx):
            return on.enter_context(nc.sbuf_tensor(name, shape, dt))

        def sem(name, per=1):
            return Signal(ctx.enter_context(nc.semaphore(name)), per)

        def again(signal, per):
            return Signal(signal.sem, per, DEPTH * signal.per)

        ps = ctx.enter_context(nc.psum_tensor("ps", [P, 8, SEQ], F32))
        ACC, STAT, ROT, TRN = (0, 1), (2, 3), (4, 5), (6, 7)

        x = sb("x_sb", [P, KD, SEQ])
        h_hi, h_lo = sb("h_hi", [P, KD, SEQ], F32R), sb("h_lo", [P, KD, SEQ], F32R)
        raw = [sb(f"raw{s}", [P, HALF, P]) for s in range(2)]
        whi = [sb(f"whi{s}", [P, HALF, P], F32R) for s in range(2)]
        wlo = [sb(f"wlo{s}", [P, HALF, P], F32R) for s in range(2)]
        rstd = sb("rstd", [P, SEQ])
        ssq = sb("ssq", [P, SEQ])
        sqt = sb("sqt", [P, 2, SEQ])
        lnt = sb("lnt", [P, SEQ])
        ident = sb("ident", [P, P])
        ones = sb("ones", [P, P])
        blk = sb("blk", [P, P])
        negones = sb("negones", [P, P], F32R)
        eps = sb("eps", [P, 2])
        GENS = 4 * DEPTH + 1
        gains = sb("gains", [P, GENS * KD + 2 * DEPTH * KD])
        pa = sb("pa", [P, DEPTH, 14])
        pb = sb("pb", [P, DEPTH, 2 * 2 * NF])
        pc = sb("pc", [P, DEPTH, 2 * 2 * NF])
        pd = sb("pd", [P, DEPTH, N_PD])
        gate_par = sb("gate_par", [P, 2, DEPTH, GH])

        setup_loaded = sem("setup_loaded")
        consts_made = sem("consts_made")
        params_turned = sem("params_turned")
        params_kept = sem("params_kept")
        x_loaded = sem("x_loaded")
        x_turned = sem("x_turned")
        x_ready = sem("x_ready", KD)
        act_step, dve_step, pool_step = sem("act_step"), sem("dve_step"), sem("pool_step")
        w_loaded = [sem(f"w_loaded{s}") for s in range(2)]
        w_hi_ready = sem("w_hi_ready")
        w_lo_ready = sem("w_lo_ready")
        unit_done = sem("unit_done")
        acc_free = sem("acc_free")
        sq_ready, ssq_done = sem("sq_ready", KD), sem("ssq_done", KD)
        hhi_ready, h_ready = sem("hhi_ready", KD), sem("h_ready", KD)
        stat_ready, rstd_ready = sem("stat_ready"), sem("rstd_ready")
        sgw_loaded, sgb_loaded = sem("sgw_loaded", 1), sem("sgb_loaded", 1)
        wT_ready, wT_kept = sem("wT_ready", 2), sem("wT_kept", 2)
        gelu_ready = sem("gelu_ready", 2 * NS)
        vvsq_ready, vvstat_ready = sem("vvsq_ready", NS), sem("vvstat_ready", NS)
        vvrs_ready, vvn_ready = sem("vvrs_ready", NS), sem("vvn_ready", NS)
        vvT_ready, vvT_kept = sem("vvT_ready", NS), sem("vvT_kept", NS)
        mix_ready, sg_ready = sem("mix_ready", NS), sem("sg_ready", NS)
        mix_used = sem("mix_used", NS)
        qksq_ready, qkstat_ready = sem("qksq_ready", NQ + 1), sem("qkstat_ready", NQ + 1)
        qkrs_ready, qkn_ready = sem("qkrs_ready", NQ + 1), sem("qkn_ready", NQ + 1)
        rot_ready, rot_used, rope_ready = sem("rot_ready", NQ + 1), sem("rot_used", NQ + 1), sem("rope_ready", NQ + 1)
        qr_ready, ql_ready = sem("qr_ready", NQ + 1), sem("ql_ready", NQ + 1)
        rl_ready = sem("rl_ready", NH)
        vT_ready, vaug_ready = sem("vT_ready", 1), sem("vaug_ready", 1)
        vones_ready = sem("vones_ready", 1)
        S_ready, S_used = sem("S_ready", 2 * NH), sem("S_used", 2 * NH)
        diag_ready = sem("diag_ready", NH)
        ST_ready, P_ready = sem("ST_ready", NH * TB), sem("P_ready", NH * TB)
        PV_done, ao_ready = sem("PV_done", NH * TB), sem("ao_ready", NH)
        osq_ready, osq_used = sem("osq_ready", NQ + NS), sem("osq_used", NQ + NS)
        ors_ready = sem("ors_ready", 2)
        mtmp_ready, mhi_ready, merged_ready = (sem(n, NQ + NS) for n in ("mtmp_ready", "mhi_ready", "merged_ready"))
        center_ready, conv_ready = sem("center_ready", 2 * NF), sem("conv_ready", 2 * NF)
        silu_ready, prod_ready = sem("silu_ready", NF), sem("prod_ready", NF)
        ahi_ready, a_ready = sem("ahi_ready", NF), sem("a_ready", NF)
        c2_loaded, c2_cast, wab_loaded, wab_split = sem("c2_loaded"), sem("c2_cast"), sem("wab_loaded"), sem("wab_split", 2)
        zp_clear = sem("zp_clear")
        sc_center, sc_ready, sc_silu = (sem(n, NG) for n in ("sc_center", "sc_ready", "sc_silu"))
        gate_ready, glu_ready, cg_ready = sem("gate_ready", GH), sem("glu_ready", NC), sem("cg_ready", NC)
        ab_ready, ab_kept, abT_ready = sem("ab_ready"), sem("ab_kept"), sem("abT_ready")
        l2sq, l2stat, l2rs, l2n = (sem(n, 2 * GH) for n in ("l2sq", "l2stat", "l2rs", "l2n"))
        rot2_ready, rot2_used, rope2_ready, qkr2_ready = (again(n, 2 * NA) for n in (rot_ready, rot_used, rope_ready, qr_ready))
        v2T_ready, vaug2_ready, v2ones_ready = again(vT_ready, NA), again(vaug_ready, NA), again(vones_ready, 1)
        S2_ready, S2_used, diag2_ready = again(S_ready, 2 * AH), again(S_used, 2 * AH), again(diag_ready, AH)
        E2_ready = sem("E2_ready", AH * TB)
        ST2_ready, P2_ready, PV2_done = (again(n, AH * TB) for n in (ST_ready, P_ready, PV_done))
        ya_ready, rl2_ready = sem("ya_ready", AH), again(rl_ready, AH)
        dw_ready, mean_ready, mean_kept = sem("dw_ready", NC), sem("mean_ready"), sem("mean_kept")
        centered, lnsq, lnsq_used, ln_scaled, yc_ready = (sem(n, NC) for n in ("centered", "lnsq", "lnsq_used", "ln_scaled", "yc_ready"))
        ln_rs = sem("ln_rs")
        gate_in, gate_e1, gate_e2, g_ready, G_ready, gc_kept, dg_ready, eg_cols = (sem(n) for n in (
            "gate_in", "gate_e1", "gate_e2", "g_ready", "G_ready", "gc_kept", "dg_ready", "eg_cols"))
        beg_ready = sem("beg_ready")
        grow_ready, brow_ready, kT_ready, gvT_ready = (sem(n, GH) for n in ("grow_ready", "brow_ready", "kT_ready", "gvT_ready"))
        kb_ready, gap_ready, decay_ready, eg_ready = (sem(n, GH) for n in ("kb_ready", "gap_ready", "decay_ready", "eg_ready"))
        turned_used, kk_ready, qk_ready, head_ready = (sem(n, GH) for n in ("turned_used", "kk_ready", "qk_ready", "head_ready"))
        lt_ready, p1_ready, x_new = (sem(n, GH * LEVELS) for n in ("lt_ready", "p1_ready", "x_new"))
        p1_kept, xpt_ready = (sem(n, GH * (LEVELS - 1)) for n in ("p1_kept", "xpt_ready"))
        xp_ready = sem("xp_ready", GH * (LEVELS - 2))
        uu_ready, uu_kept, ww_ready, ww_kept = (sem(n, GH) for n in ("uu_ready", "uu_kept", "ww_ready", "ww_kept"))
        state_ready, ws_ready, vn_ready, o_ready, o_kept = (sem(n, NCH) for n in (
            "state_ready", "ws_ready", "vn_ready", "o_ready", "o_kept"))
        ds_ready = sem("ds_ready", NCH - 1)
        ogsq, ogstat, ogrs, og_ready = (sem(n, GH) for n in ("ogsq", "ogstat", "ogrs", "og_ready"))
        m2hi_ready, merged2_ready = again(mhi_ready, KD), again(merged_ready, KD)
        ysq_ready, yssq_done = sem("ysq_ready", 2 * KD), sem("yssq_done", 2 * KD)
        ystat_ready, yrs_ready = sem("ystat_ready", 2), sem("yrs_ready", 2)
        x2_ready = sem("x2_ready", 2 * KD)
        silu2_ready, prod2_ready, a2hi_ready, a2_ready = (again(n, NF) for n in (silu_ready, prod_ready, ahi_ready, a_ready))
        out_turned, out_kept, out_stored = sem("out_turned"), sem("out_kept"), sem("out_stored")

        def tile(t, n):
            return t[:, n, :] if isinstance(n, int) else t[:, ds(n, 1), :].rearrange("p a n -> p (a n)")

        def gain(i):
            return gains[:, i:i + 1] if isinstance(i, int) else gains[:, ds(i, 1)]

        def param(t, layer, i):
            i = slice(i, i + 1) if isinstance(i, int) else ds(i, 1)
            return t[:, ds(layer, 1), i].rearrange("p a b -> p (a b)")

        with ExitStack() as on:
            xs = sb("xs", [P, TB, DM], on=on)
            rows = sb("rows", [P, 9, P], on=on)
        N_GAINS = GENS * KD + 2 * DEPTH * KD
        ROWS = [N_GAINS] + [14, 4 * NF, 4 * NF, N_PD] * DEPTH
        COLS = [gains[:]] + [t[:, l, :] for l in range(DEPTH) for t in (pa, pb, pc, pd)]
        N_ROWS = len(ROWS)

        with ExitStack() as on:
            zq = sb("zq", [P, NQ, SEQ], on=on)
            vv = sb("vv", [P, NS, SEQ], on=on)
            kd2 = sb("kd", [P, NKV, SEQ], on=on)
            kd = [kd2[:, g, :] for g in range(NKV)]
            zk = sb("zk", [P, SEQ], on=on)
            zv = sb("zv", [P, SEQ], on=on)
            t1 = sb("t1", [P, SEQ], on=on)
            t2 = sb("t2", [P, SEQ], on=on)
            kr = [sb("kr0", [P, SEQ], F32R, on=on)]
            vvT = sb("vvT", [P, TB, SGW], on=on)
            kr.append(sb("kr1", [P, SEQ], F32R, on=on))
            kl = [sb(f"kl{g}", [P, SEQ], F32R, on=on) for g in range(NKV)]
            qab = sb("qab", [P, NQ, 2, SEQ], F32R, on=on)
            vaug = sb("vaug", [P, NKV, 2, TB, P], on=on)
            probs = sb("probs", [P, TB, SEQ], on=on)
            diag = sb("diag", [P, 2, TB, P], F32R, on=on)
            wT = sb("wT", [P, SGH, P], on=on)
            mrs = sb("mrs", [P, 2, SEQ], on=on)
            mx = sb("mx", [P, 2, TB], on=on)
            u = sb("u", [P, NS, SEQ], on=on)
            ao = sb("ao", [P, NQ, SEQ], on=on)
            rope = sb("rope", [P, 2, SEQ], on=on)
            perm = sb("perm", [P, P], on=on)
            sgb = sb("sgb", [P, NS, P], on=on)
        msq = sqt
        ors, mtmp = kd2, wT[:].rearrange("p h q -> p (h q)").rearrange("p (a n) -> p a n", n=SEQ)
        sgw = probs[:, 0:2, :].rearrange("p a (h q) -> p (a h) q", q=P)

        with ExitStack() as on:
            a_hi = sb("a_hi", [P, HALF, SEQ], F32R, on=on)
            a_lo = sb("a_lo", [P, HALF, SEQ], F32R, on=on)
            pad = [sb(f"pad{s}", [P, SEQ + 2], on=on) for s in range(2)]
            cv = [sb(f"cv{s}", [P, SEQ], on=on) for s in range(2)]
            prod = sb("prod", [P, SEQ], on=on)
            y = sb("y_sb", [P, KD, SEQ], on=on)

        with ExitStack() as on:
            gq, gk, gv, gz = (sb(n, [P, GH, SEQ], on=on) for n in ("gq", "gk", "gv", "gz"))
            with ExitStack() as core:
                kbeg, kout, vb = (sb(n, [P, GH, TB, P], on=core) for n in ("kbeg", "kout", "vb"))
                eg, dm, kb = (sb(n, [P, 2, SEQ], on=core) for n in ("eg", "dm", "kb"))
                intraT, xT = sb("intraT", [P, GH, SEQ], on=core), sb("xT", [P, GH, SEQ], on=core)
                after_core = sb("after_core", [P, 1], on=core)
            with ExitStack() as early:
                zp = sb("zp", [P, 2, SEQ + GT - 1], on=early)
                cg = sb("cg", [P, NC, SEQ], on=early)
                za = sb("za", [P, 3 * NA, SEQ], on=early)
                qkr2 = sb("qkr2", [P, 2 * NA, SEQ], F32R, on=early)
                vaug2 = sb("vaug2", [P, AH, TB, P], on=early)
                probs2 = sb("probs2", [P, TB, SEQ], on=early)
                diag2 = sb("diag2", [P, 2, TB, P], F32R, on=early)
                ta, tb2 = sb("ta", [P, SEQ], on=early), sb("tb2", [P, SEQ], on=early)
                mx2 = sb("mx2", [P, 2, TB], on=early)
            on.enter_context(nc.sbuf_tensor("hold_core", [P, 2 * 3 * SEQ + (3 + 2) * GH * SEQ + 16], F32))
            ya = sb("ya", [P, NA, SEQ], on=on)
            yc = sb("yc", [P, NC, SEQ], on=on)
            ypad = sb("ypad", [P, NC, SEQ + CT - 1], on=on)
            rope2 = sb("rope2", [P, 2, SEQ], on=on)
            perm2 = sb("perm2", [P, P], on=on)
            wide = SEQ + SEQ - P
            mask_s, mask_t, times = (sb(n, [P, wide], BF16, on=on) for n in ("mask_s", "mask_t", "times"))
            ident_b = sb("ident_b", [P, P], BF16, on=on)
            tri = sb("tri", [P, P], on=on)
            lev = sb("lev", [P, LEVELS, P], BF16, on=on)
            wab, wab_hi, wab_lo = sb("wab", [P, KD, 2 * GH], on=on), sb("wab_hi", [P, KD, 2 * GH], F32R, on=on), sb("wab_lo", [P, KD, 2 * GH], F32R, on=on)
            cols = {n: sb(f"col_{n}", [P, TB, GH], on=on) for n in
                    ("a", "ax", "e", "l", "g", "beta", "gc", "egc", "dg", "egl", "beg", "b")}
            expa = sb("expa", [P, GH], on=on)
            eg_last = sb("eg_last", [P, GH, NCH], on=on)
        lt, p1, mrs2, msq2 = eg, dm, kb, sqt
        ab = probs2[0:2 * GH, 0, :]
        l2s, l2r = probs2, vaug2[:].rearrange("p h t d -> p h (t d)")
        vn, state = ypad[:, 0, 0:GH * P].rearrange("p (h d) -> p h d", d=P), ypad[:, 1, 0:GH * P].rearrange("p (h d) -> p h d", d=P)
        states, decayed = (state, mrs2[:, 1, :].rearrange("p (h d) -> p h d", d=P)), mrs2[:, 0, :].rearrange("p (h d) -> p h d", d=P)
        og = xT
        gqkv = [t[:, i, :] for t in (gq, gk, gv) for i in range(GH)]

        def by_rows(src):
            return src.rearrange("(r p) -> r p", p=P)

        def setup_rows():
            for dst, name in ((ident, "c_ident"), (blk, "c_blk"), (perm, "c_perm")):
                yield dst[:], D[name]
            yield rope[:], D["c_rope"].rearrange("a p n -> p a n")
            for l in range(DEPTH):
                for b, names in enumerate((("attn_norm_g", "ffn_norm_g"), ("attn_pre_norm_2", "ffn_pre_norm_2"))):
                    for i, name in enumerate(names):
                        g = (b * DEPTH + l) * 2 + i
                        yield rows[g * KD:(g + 1) * KD, 0, :], by_rows(D[name][l])
                for i, name in enumerate(("attn_post_norm_2", "ffn_post_norm_2")):
                    g = GENS + 2 * l + i
                    yield rows[g * KD:(g + 1) * KD, 0, :], by_rows(D[name][l])
                a = 1 + 4 * l
                for i, name in enumerate(("q_norm_g", "k_norm_g")):
                    for r in range(2):
                        yield rows[i:i + 1, a, r * HD:(r + 1) * HD], D[name][l:l + 1, :]
                yield rows[2:2 + NS, a, :], by_rows(D["sg_norm_g"][l].rearrange("h d -> (h d)"))
                yield rows[2 + NS:2 + NS + NQ, a, :], by_rows(D["attn_out_g"][l])
                yield rows[2 + NS + NQ:2 + 2 * NS + NQ, a, :], by_rows(D["sg_out_g"][l])
                yield rows[0:2 * NF, a + 1, :], by_rows(D["conv_w"][l, 0])
                yield rows[2 * NF:4 * NF, a + 1, :], by_rows(D["conv_w"][l, 1])
                yield rows[0:2 * NF, a + 2, :], by_rows(D["conv_w"][l, 2])
                yield rows[2 * NF:4 * NF, a + 2, :], by_rows(D["conv_b"][l])
                yield rows[D_DW:D_BIAS, a + 3, :], by_rows(D["conv_dw_2"][l].rearrange("t c -> (t c)"))
                for at, name in ((D_BIAS, "conv_dw_bias_2"), (D_LNG, "conv_norm_gain_2"), (D_LNB, "conv_norm_bias_2")):
                    yield rows[at:at + NC, a + 3, :], by_rows(D[name][l])
                yield rows[D_SC:D_ON, a + 3, :], by_rows(D["gdn_short_conv_2"][l].rearrange("t c -> (t c)"))
                yield rows[D_ON:N_PD, a + 3, :], by_rows(D["gdn_out_norm_2"][l])
            for i, name in enumerate(("gdn_a_log_2", "gdn_dt_bias_2")):
                yield gate_par[:, i, :, :], D[name].unsqueeze(0).to_broadcast([P, DEPTH, GH])

        SETUP = [16 * sum(1 for _ in setup_rows())]

        wv = {n: D[n].rearrange("l (k p) n -> l p k n", p=P) for n in
              ("w_in", "w_o", "w_up", "w_down", "w_in_2", "w_out_2", "w_gate_2", "w_up_2", "w_down_2")}

        def weight(name, layer, k0, kt, col):
            return wv[name][ds(layer, 1), :, k0:k0 + kt, ds(col, P)].rearrange("l p k n -> p (l k) n")

        def plan1(layer):
            yield 0, 1, KD, lambda j, s: weight("w_in", layer, 0, KD, j * 2 * P + (NQ + 1 - s) * P)
            for at, tile0 in ((1, 0), (1 + NQ // 2, NQ + 2 + NS), (1 + NQ // 2 + NS // 2, NQ + 2)):
                yield at, 2, KD, lambda j, s, t=tile0: weight("w_in", layer, 0, KD, j * 2 * P + (t + s) * P)
            yield OFF_O, PAIRS_O, KD, lambda j, s: weight("w_o", layer, 0, KD, j * 2 * P + s * P)
            for hf in range(2):
                yield OFF_UP[hf], PAIRS_UP, KD, lambda j, s, hf=hf: weight(
                    "w_up", layer, 0, KD, j * P + (s * NF + hf * HALF) * P)
                yield OFF_DOWN[hf], PAIRS_DOWN, HALF, lambda j, s, hf=hf: weight(
                    "w_down", layer, hf * HALF, HALF, j * 2 * P + s * P)

        mixed = [t[:, i, :] for t, n in ((ya, NA), (yc, NC), (og, GH)) for i in range(n)]

        def plan2(layer):
            yield 0, PAIRS_IN2, KD, lambda j, s: weight("w_in_2", layer, 0, KD, j * 2 * P + s * P)
            yield OFF_O2, PAIRS_O, KD, lambda j, s: weight("w_out_2", layer, 0, KD, j * 2 * P + s * P)
            for hf in range(2):
                yield OFF_UP2[hf], PAIRS_UP, KD, lambda j, s, hf=hf: weight(
                    ("w_gate_2", "w_up_2")[s], layer, 0, KD, j * P + hf * HALF * P)
                yield OFF_DOWN2[hf], PAIRS_DOWN, HALF, lambda j, s, hf=hf: weight(
                    "w_down_2", layer, hf * HALF, HALF, j * 2 * P + s * P)

        block = ctx.enter_context(nc.Block())

        @block.sync
        def _(sp):
            def load(v, s, kt, src):
                sp.wait_ge(w_lo_ready.sem, v * 2 + (s + 1))
                sp.wait_ge(consts_made.sem, 1)
                sp.dma_start(raw[s][:, 0:kt, :], src).then_inc(w_loaded[s].sem, 16)

            sp.dma_start(xs[:], D["x"][0].rearrange("(t p) d -> p t d", p=P)).then_inc(x_loaded.sem, 16)
            with sp.Fori(0, DEPTH) as L:
                for off, n, kt, src in plan1(L):
                    with sp.Fori(0, n) as j:
                        for s in range(2):
                            load(L * PAIRS1 + off + j, s, kt, src(j, s))
            with sp.Fori(0, DEPTH) as L:
                for off, n, kt, src in plan2(L):
                    def pairs(j0, j1, off=off, kt=kt, src=src):
                        with sp.Fori(j0, j1) as j:
                            for s in range(2):
                                load(BASE2 + L * PAIRS2 + off + j, s, kt, src(j, s))

                    if off == 0:
                        pairs(0, 2)
                        sp.wait_ge(consts_made.sem, 1)
                        sp.wait_ge(h_ready.sem, h_ready.at(L * 2 + 2 * DEPTH, KD - 1))
                        sp.dma_start(wab[:], D["w_in_2"].rearrange("l (k p) n -> l p k n", p=P)[ds(L, 1), :, :, N_IN2 * P:N_IN2 * P + 2 * GH]
                                     .rearrange("l p k n -> p (l k) n")).then_inc(wab_loaded.sem, 16)
                        pairs(2, n)
                    else:
                        pairs(0, n)
            for s in range(2):
                load(PAIRS, s, KD, weight("w_in", 0, 0, KD, s * P))
            for tb in range(TB):
                for hf in range(2):
                    sp.wait_ge(out_kept.sem, tb * 2 + hf + 1)
                    sp.dma_start(out[0, tb * P:(tb + 1) * P, hf * SEQ:(hf + 1) * SEQ],
                                 xs[:, tb, hf * SEQ:(hf + 1) * SEQ]).then_inc(out_stored.sem, 16)
            sp.wait_ge(out_stored.sem, TB * 2 * 16)
            for s in range(2):
                sp.wait_ge(w_loaded[s].sem, 16 * (PAIRS + 1))

        @block.gpsimd
        def _(pool):
            pool.sem_inc(w_lo_ready.sem, 2)

            def low(v, s, kt):
                pool.wait_ge(w_hi_ready.sem, v * 2 + (s + 1))
                nc.gpsimd.tensor_tensor(wlo[s][:, 0:kt, :], raw[s][:, 0:kt, :], whi[s][:, 0:kt, :].bitcast(F32),
                                        ALU.subtract).then_inc(w_lo_ready.sem, 1)

            with pool.Fori(0, DEPTH) as L:
                for off, n, kt, _src in plan1(L):
                    with pool.Fori(0, n) as j:
                        for s in range(2):
                            low(L * PAIRS1 + off + j, s, kt)

            for s in range(2):
                low(BASE2, s, KD)
            pool.wait_ge(h_ready.sem, h_ready.at(2 * DEPTH, KD - 1))
            for dst, name in ((mask_s, "c_mask_s"), (mask_t, "c_mask_t"), (times, "c_times"), (ident_b, "c_ident")):
                pool.dma_start(dst[:], D[name]).then_inc(c2_cast.sem, 16)
            pool.dma_start(lev[:], D["c_lev"].rearrange("a p n -> p a n")).then_inc(c2_cast.sem, 16)
            pool.dma_start(rope2[:], D["c_rope2"].rearrange("a p n -> p a n")).then_inc(c2_loaded.sem, 16)
            pool.dma_start(perm2[:], D["c_perm2"]).then_inc(c2_loaded.sem, 16)
            pool.dma_start(tri[:], D["c_tri"]).then_inc(c2_loaded.sem, 16)

            def squares(gen):
                for n in range(1, KD):
                    pool.wait_ge(sq_ready.sem, sq_ready.at(gen, n))
                    pool.wait_ge(ssq_done.sem, ssq_done.at(gen, n - 1))
                    nc.gpsimd.tensor_tensor(ssq[:], ssq[:], sqt[:, n % 2, :], ALU.add).then_inc(ssq_done.sem, 1)

            with pool.Fori(0, DEPTH) as L:
                for off, n, kt, _src in plan2(L):
                    first = 1 if off == 0 else 0
                    if off == OFF_UP2[0]:
                        first = 1
                        for s in range(2):
                            low(BASE2 + L * PAIRS2 + off, s, kt)
                        squares(L * 2 + (2 * DEPTH + 1))
                    with pool.Fori(first, n) as j:
                        for s in range(2):
                            low(BASE2 + L * PAIRS2 + off + j, s, kt)
                for s in range(2):
                    low(BASE2 + L * PAIRS2 + PAIRS2, s, KD)
                squares(L * 2 + (2 * DEPTH + 2))
            pool.wait_ge(c2_cast.sem, 5 * 16)
            pool.wait_ge(c2_loaded.sem, 3 * 16)

        @block.tensor
        def _(pe):
            pe.sem_inc(unit_done.sem, 2)

            def unit(v, s, kt, rhs_hi, rhs_lo, wait_rhs):
                pe.wait_ge(w_lo_ready.sem, v * 2 + (s + 3))
                pe.wait_ge(acc_free.sem, v * 2 + (s + 1))
                for k in range(kt):
                    wait_rhs(k, s)
                    for n, (w, r) in enumerate(((whi, rhs_hi), (whi, rhs_lo), (wlo, rhs_hi))):
                        mm = pe.matmul(ps[:, ACC[s], :], w[s][:, k, :], r[:, k, :],
                                       start=(k == 0 and n == 0), stop=(k == kt - 1 and n == 2))
                mm.then_inc(unit_done.sem, 1)

            def first_pair(v, kt, rhs_hi, rhs_lo, wait_rhs, before, ks=None):
                ks = list(ks or range(kt))
                for s in range(2):
                    pe.wait_ge(w_lo_ready.sem, v * 2 + (s + 3))
                    pe.wait_ge(acc_free.sem, v * 2 + (s + 1))
                for k in ks:
                    if k == before[0]:
                        before[1]()
                    wait_rhs(k, 0)
                    for s in range(2):
                        for n, (w, r) in enumerate(((whi, rhs_hi), (whi, rhs_lo), (wlo, rhs_hi))):
                            mm = pe.matmul(ps[:, ACC[s], :], w[s][:, k, :], r[:, k, :],
                                           start=(k == ks[0] and n == 0), stop=(k == ks[-1] and n == 2))
                        if k == ks[-1]:
                            mm.then_inc(unit_done.sem, 1)

            def norm_sum(gen):
                pe.wait_ge(ssq_done.sem, ssq_done.at(gen, KD - 1))
                pe.matmul(ps[:, STAT[0], :], ones[:], ssq[:], start=True, stop=True).then_inc(stat_ready.sem, 1)

            def need_h(gen):
                def wait(k, s):
                    if s == 0:
                        pe.wait_ge(h_ready.sem, h_ready.at(gen, k))
                return wait

            pe.wait_ge(setup_loaded.sem, SETUP[0])
            pe.wait_ge(consts_made.sem, 1)
            for i, r in enumerate(ROWS):
                bank = TRN[i % 2]
                if i >= 2:
                    pe.wait_ge(params_kept.sem, i - 1)
                pe.transpose(ps[:, bank, 0:r], rows[0:r, i, :], ident[0:r, 0:r]).then_inc(params_turned.sem, 1)
            pe.wait_ge(x_loaded.sem, 16)
            for n in range(KD):
                if n >= 2:
                    pe.wait_ge(x_ready.sem, n - 1)
                for tb in range(TB):
                    mm = pe.transpose(ps[:, ROT[n % 2], tb * P:(tb + 1) * P], xs[:, tb, n * P:(n + 1) * P], ident[:])
                mm.then_inc(x_turned.sem, 1)

            with pe.Fori(0, DEPTH) as L:
                V = L * PAIRS1
                first_pair(V, KD, h_hi, h_lo, need_h(L * 2), (KD - 1, lambda: norm_sum(L * 2)))

                def head_sums(i):
                    pe.wait_ge(qksq_ready.sem, qksq_ready.at(L, i))
                    if i == 0:
                        pe.wait_ge(rstd_ready.sem, rstd_ready.at(L * 2, 0))
                    if i >= 2:
                        pe.wait_ge(qkrs_ready.sem, qkrs_ready.at(L, i - 2))
                    pe.matmul(ps[:, STAT[i % 2], :], blk[:], msq[:, i % 2, :], start=True, stop=True).then_inc(qkstat_ready.sem, 1)

                def partners(i):
                    pe.wait_ge(qkn_ready.sem, qkn_ready.at(L, i))
                    if i >= 2:
                        pe.wait_ge(rot_used.sem, rot_used.at(L, i - 2))
                    pe.matmul(ps[:, ROT[i % 2], :], perm[:], zk[:] if i == 0 else zq[:, i - 1, :],
                              start=True, stop=True).then_inc(rot_ready.sem, 1)

                def gated_sums(t):
                    pe.wait_ge(vvsq_ready.sem, vvsq_ready.at(L, t))
                    if t < 2:
                        pe.wait_ge(qkrs_ready.sem, qkrs_ready.at(L, NQ))
                    else:
                        pe.wait_ge(vvrs_ready.sem, vvrs_ready.at(L, t - 2))
                    pe.matmul(ps[:, STAT[t % 2], :], blk[:], msq[:, t % 2, :], start=True, stop=True).then_inc(vvstat_ready.sem, 1)

                def turn_spatial():
                    pe.wait_ge(sgw_loaded.sem, L * 16 + 16)
                    for b in range(2):
                        for i in range(4):
                            mm = pe.transpose(ps[:, TRN[b], i * P:(i + 1) * P], sgw[:, 4 * b + i, :], ident[:])
                        mm.then_inc(wT_ready.sem, 1)

                def turn_values():
                    pe.wait_ge(acc_free.sem, V * 2 + 3)
                    pe.wait_ge(wT_kept.sem, wT_kept.at(L, 0))
                    for kt in range(TB):
                        mm = pe.transpose(ps[:, TRN[0], kt * P:(kt + 1) * P], zv[:, kt * P:(kt + 1) * P], ident[:])
                    mm.then_inc(vT_ready.sem, 1)

                def turn_gated(t):
                    pe.wait_ge(vvn_ready.sem, vvn_ready.at(L, t))
                    if t == 0:
                        pe.wait_ge(vaug_ready.sem, vaug_ready.at(L, 0))
                    elif t == 1:
                        pe.wait_ge(wT_kept.sem, wT_kept.at(L, 1))
                    else:
                        pe.wait_ge(vvT_kept.sem, vvT_kept.at(L, t - 2))
                    for c in range(TB):
                        mm = pe.transpose(ps[:, TRN[t % 2], c * P:(c + 1) * P], vv[:, t, c * P:(c + 1) * P], ident[:])
                    mm.then_inc(vvT_ready.sem, 1)

                def mix(t):
                    pe.wait_ge(vvT_kept.sem, vvT_kept.at(L, t))
                    if t == 0:
                        pe.wait_ge(wT_kept.sem, wT_kept.at(L, 1))
                    if t < 2:
                        pe.wait_ge(acc_free.sem, V * 2 + N_IN + 2)
                    else:
                        pe.wait_ge(mix_used.sem, mix_used.at(L, t - 2))
                    for c in range(TB):
                        for r in range(2):
                            mm = pe.matmul(ps[64 * r:64 * r + 64, ACC[t % 2], c * P:(c + 1) * P],
                                           vvT[:, c, t * P + 64 * r:t * P + 64 * r + 64], wT[:, 2 * t + r, :],
                                           start=True, stop=True)
                    mm.then_inc(mix_ready.sem, 1)

                for i in range(2, N_IN):
                    unit(V + i // 2, i % 2, KD, h_hi, h_lo, need_h(L * 2))
                    if i - 2 <= NQ:
                        head_sums(i - 2)
                    if 0 <= i - 3 <= NQ:
                        partners(i - 3)
                    if i == 4:
                        turn_spatial()
                    if i == 6:
                        turn_values()
                    if i in (10, 12):
                        gated_sums(i - 10)
                        gated_sums(i - 9)
                    if i == 12:
                        turn_gated(0)
                        turn_gated(1)

                def scores(h, b):
                    t, e, g = h // 2, h % 2, h // GROUP
                    if h == 0 and b == 0:
                        pe.wait_ge(qr_ready.sem, qr_ready.at(L, NQ))
                        pe.wait_ge(vvrs_ready.sem, vvrs_ready.at(L, NS - 1))
                    else:
                        pe.wait_ge(S_used.sem, S_used.at(L, 2 * h + b - 1))
                    for i in range(2):
                        qb = 2 * b + i
                        mm = pe.matmul(ps[:, STAT[i], :], qab[64 * e:64 * e + 64, t, e, qb * P:(qb + 1) * P],
                                       kr[g][64 * e:64 * e + 64, :], start=True, stop=True)
                    mm.then_inc(S_ready.sem, 1)

                def scores_turned(h, kt):
                    t, e, g = h // 2, h % 2, h // GROUP
                    n = h * TB + kt
                    if n == 0:
                        pe.wait_ge(ql_ready.sem, ql_ready.at(L, NQ))
                    if kt == 0:
                        pe.wait_ge(diag_ready.sem, diag_ready.at(L, h))
                    if n >= 2:
                        pe.wait_ge(P_ready.sem, P_ready.at(L, n - 2))
                    cols_k = slice(kt * P, (kt + 1) * P)
                    pe.matmul(ps[:, ROT[kt % 2], :], kr[g][:, cols_k], qab[:, t, e, :], start=True, stop=False)
                    pe.matmul(ps[:, ROT[kt % 2], :], kl[g][64 * e:64 * e + 64, cols_k], qab[64 * e:64 * e + 64, t, e, :],
                              start=False, stop=False)
                    pe.matmul(ps[:, ROT[kt % 2], :], negones[:], diag[:, h % 2, :, :].rearrange("p b q -> p (b q)"),
                              start=False, stop=True).then_inc(ST_ready.sem, 1)

                def probs_values(h, kt):
                    pe.wait_ge(P_ready.sem, P_ready.at(L, h * TB + kt))
                    if kt == 0 and h >= 2:
                        pe.wait_ge(ao_ready.sem, ao_ready.at(L, h - 2))
                    if kt == 0 and h < 2:
                        pe.wait_ge(vvT_kept.sem, vvT_kept.at(L, NS - 2 + h))
                    pe.matmul(ps[:, TRN[h % 2], :], vaug[:, h // GROUP, h % 2, kt, :], probs[:, kt, :],
                              start=(kt == 0), stop=(kt == TB - 1)).then_inc(PV_done.sem, 1)

                def mixer_sum(i):
                    pe.wait_ge(osq_ready.sem, osq_ready.at(L, i))
                    if i == 0:
                        pe.wait_ge(mix_used.sem, mix_used.at(L, NS - 1))
                    if i == NS:
                        pe.wait_ge(S_used.sem, S_used.at(L, 2 * NH - 1))
                    pe.matmul(ps[:, (ACC[0], STAT[1])[i // NS], :], ones[:], msq[:, i % 2, :],
                              start=(i % NS == 0), stop=(i % NS == NS - 1)).then_inc(osq_used.sem, 1)

                scores(0, 0)
                mix(0)
                mix(1)
                scores(0, 1)
                turn_gated(2)
                turn_gated(3)
                for h in range(NH):
                    for kt in range(TB):
                        scores_turned(h, kt)
                        if kt in (0, 2) and h + 1 < NH:
                            scores(h + 1, kt // 2)
                        if kt >= 1:
                            probs_values(h, kt - 1)
                        if h == NH - 1 and kt == 1:
                            mixer_sum(NS)
                            mixer_sum(NS + 1)
                    probs_values(h, TB - 1)
                    if h == 0:
                        mix(2)
                        mix(3)
                    if h in (2, 3):
                        mixer_sum(2 * h - 4)
                        mixer_sum(2 * h - 3)
                mixer_sum(NS + 2)

                def need_merged(k, s):
                    if s == 0:
                        pe.wait_ge(merged_ready.sem, merged_ready.at(L, (k + NS) % (NQ + NS)))

                first_pair(V + OFF_O, KD, a_hi, a_lo, need_merged, (0, lambda: mixer_sum(NS + 3)),
                           [*range(NQ, NQ + NS), *range(NQ)])
                with pe.Fori(1, PAIRS_O) as j:
                    for s in range(2):
                        unit(V + OFF_O + j, s, KD, a_hi, a_lo, need_merged)
                first_pair(V + OFF_UP[0], KD, h_hi, h_lo, need_h(L * 2 + 1), (KD - 1, lambda: norm_sum(L * 2 + 1)))
                for hf in range(2):
                    with pe.Fori(1 - hf, PAIRS_UP) as j:
                        for s in range(2):
                            unit(V + OFF_UP[hf] + j, s, KD, h_hi, h_lo, need_h(L * 2 + 1))

                    def need_a(k, s, hf=hf):
                        if s == 0:
                            pe.wait_ge(a_ready.sem, a_ready.at(L, hf * HALF + k))

                    with pe.Fori(0, PAIRS_DOWN) as j:
                        for s in range(2):
                            unit(V + OFF_DOWN[hf] + j, s, HALF, a_hi, a_lo, need_a)

            with pe.Fori(0, DEPTH) as L:
                V = BASE2 + L * PAIRS2
                G = L * 2 + 2 * DEPTH
                first_pair(V, KD, h_hi, h_lo, need_h(G), (KD - 1, lambda: norm_sum(G)))

                def gate_columns():
                    pe.wait_ge(rstd_ready.sem, rstd_ready.at(G, 0))
                    pe.wait_ge(wab_split.sem, wab_split.at(L, 1))
                    for k in range(KD):
                        for n, (w, r) in enumerate(((wab_hi, h_hi), (wab_lo, h_hi), (wab_hi, h_lo))):
                            mm = pe.matmul(ps[0:2 * GH, TRN[0], :], w[:, k, :], r[:, k, :],
                                           start=(k == 0 and n == 0), stop=(k == KD - 1 and n == 2))
                    mm.then_inc(ab_ready.sem, 1)

                def turn_gates():
                    pe.wait_ge(ab_kept.sem, ab_kept.at(L, 0))
                    for tb in range(TB):
                        mm = pe.transpose(ps[:, TRN[1], tb * P:(tb + 1) * P], probs2[:, 0, tb * P:(tb + 1) * P], ident[:])
                    mm.then_inc(abT_ready.sem, 1)

                def partners(i):
                    pe.wait_ge(acc_free.sem, V * 2 + i + 3)
                    if i == 0:
                        pe.wait_ge(c2_loaded.sem, 3 * 16)
                    if i >= 2:
                        pe.wait_ge(rot2_used.sem, rot2_used.at(L, i - 2))
                    pe.matmul(ps[:, ROT[i % 2], :], perm2[:], za[:, i, :], start=True, stop=True).then_inc(rot2_ready.sem, 1)

                def turn_values():
                    pe.wait_ge(acc_free.sem, V * 2 + 3 * NA + 2)
                    pe.wait_ge(ab_kept.sem, ab_kept.at(L, 0))
                    pe.wait_ge(gate_in.sem, gate_in.at(L, 0))
                    for i in range(NA):
                        for kt in range(TB):
                            mm = pe.transpose(ps[:, TRN[i], kt * P:(kt + 1) * P], za[:, 2 * NA + i, kt * P:(kt + 1) * P], ident[:])
                        mm.then_inc(v2T_ready.sem, 1)

                def scores(h, b):
                    t, r = h // 2, 64 * (h % 2)
                    if h == 0 and b == 0:
                        pe.wait_ge(c2_cast.sem, 5 * 16)
                        pe.wait_ge(qkr2_ready.sem, qkr2_ready.at(L, 2 * NA - 1))
                    else:
                        pe.wait_ge(S2_used.sem, S2_used.at(L, 2 * h + b - 1))
                    for i in range(2):
                        qb = 2 * b + i
                        pe.matmul(ps[:, STAT[i], :], qkr2[r:r + 64, t, qb * P:(qb + 1) * P], qkr2[r:r + 64, NA + t, :],
                                  start=True, stop=False)
                        mm = pe.matmul(ps[:, STAT[i], :], ident_b[:], mask_s[:, (TB - 1 - qb) * P:(TB - 1 - qb) * P + SEQ],
                                       start=False, stop=True)
                    mm.then_inc(S2_ready.sem, 1)

                def scores_turned(h, kt):
                    t, r, n, q0 = h // 2, 64 * (h % 2), h * TB + kt, kt * P
                    if kt == 0:
                        pe.wait_ge(diag2_ready.sem, diag2_ready.at(L, h))
                    if n >= 2:
                        pe.wait_ge(E2_ready.sem, E2_ready.at(L, n - 2))
                    pe.matmul(ps[:, ROT[kt % 2], q0:], za[r:r + 64, NA + t, kt * P:(kt + 1) * P], za[r:r + 64, t, q0:],
                              start=True, stop=False)
                    pe.matmul(ps[:, ROT[kt % 2], q0:], negones[:], diag2[:, h % 2, :, :].rearrange("p b q -> p (b q)")[:, q0:],
                              start=False, stop=False)
                    at = (TB - 1 - kt) * P
                    pe.matmul(ps[:, ROT[kt % 2], q0:], ident_b[:], mask_t[:, at + q0:at + SEQ],
                              start=False, stop=True).then_inc(ST2_ready.sem, 1)

                def probs_values(h, kt):
                    q0 = kt * P
                    pe.wait_ge(P2_ready.sem, P2_ready.at(L, h * TB + kt))
                    if kt == 0 and h >= 2:
                        pe.wait_ge(ya_ready.sem, ya_ready.at(L, h - 2))
                    if kt == 0 and h < 2:
                        pe.wait_ge(vaug2_ready.sem, vaug2_ready.at(L, NA - 1))
                    pe.matmul(ps[:, TRN[h % 2], q0:], vaug2[:, h, kt, :], probs2[:, kt, q0:],
                              start=(kt == 0), stop=(kt == TB - 1)).then_inc(PV2_done.sem, 1)

                def l2_sums(i):
                    pe.wait_ge(l2sq.sem, l2sq.at(L, i))
                    if i >= 4:
                        pe.wait_ge(l2rs.sem, l2rs.at(L, i - 4))
                    pe.matmul(ps[:, (STAT + ROT)[i % 4], :], ones[:], l2s[:, i % 4, :], start=True, stop=True).then_inc(l2stat.sem, 1)

                def decay_sums():
                    pe.wait_ge(g_ready.sem, g_ready.at(L, 0))
                    pe.wait_ge(ya_ready.sem, ya_ready.at(L, AH - 2))
                    NCOL = TB * GH
                    gflat = cols["g"][:].rearrange("p t h -> p (t h)")
                    pe.matmul(ps[:, TRN[0], 0:NCOL], tri[:], gflat, start=True, stop=True)
                    pe.matmul(ps[:, TRN[0], NCOL:2 * NCOL], blk[:], gflat, start=True, stop=True).then_inc(G_ready.sem, 1)

                for i in range(2, N_IN2):
                    unit(V + i // 2, i % 2, KD, h_hi, h_lo, need_h(G))
                    if i - 2 < 2 * NA:
                        partners(i - 2)
                    if i == 4:
                        gate_columns()
                    if i == 5:
                        turn_gates()
                    if i == 7:
                        turn_values()
                    for h in range(AH):
                        for b in range(2):
                            if i == 10 + 2 * h + b:
                                scores_turned(h, 2 * b)
                                scores_turned(h, 2 * b + 1)
                    for h in range(AH):
                        for b in range(2):
                            if i == 7 + 2 * h + b:
                                scores(h, b)
                            if i == 12 + 2 * h + b:
                                probs_values(h, 2 * b)
                                probs_values(h, 2 * b + 1)
                    if i == 20:
                        decay_sums()
                    if i in (22, 24):
                        for n in range(4):
                            l2_sums(2 * (i - 22) + n)
                pe.wait_ge(acc_free.sem, V * 2 + N_IN2 + 2)
                pe.wait_ge(l2n.sem, l2n.at(L, 2 * GH - 1))
                pe.wait_ge(beg_ready.sem, beg_ready.at(L, 0))

                def head_in(h):
                    if h >= 2:
                        pe.wait_ge(head_ready.sem, head_ready.at(L, h - 2))
                    for tb in range(TB):
                        mm = pe.matmul(ps[:, ROT[h % 2], tb * P:(tb + 1) * P], cols["g"][:, tb, h:h + 1].to_broadcast([P, P]),
                                       tri[:], start=True, stop=True)
                    mm.then_inc(grow_ready.sem, 1)
                    for tb in range(TB):
                        mm = pe.matmul(ps[:, STAT[h % 2], tb * P:(tb + 1) * P], cols["beta"][:, tb, h:h + 1].to_broadcast([P, P]),
                                       ident[:], start=True, stop=True)
                    mm.then_inc(brow_ready.sem, 1)
                    if h >= 1:
                        pe.wait_ge(turned_used.sem, turned_used.at(L, h - 1))
                    for tb in range(TB):
                        mm = pe.transpose(ps[:, TRN[0], tb * P:(tb + 1) * P], gk[:, h, tb * P:(tb + 1) * P], ident[:])
                    mm.then_inc(kT_ready.sem, 1)
                    for tb in range(TB):
                        mm = pe.transpose(ps[:, TRN[1], tb * P:(tb + 1) * P], gv[:, h, tb * P:(tb + 1) * P], ident[:])
                    mm.then_inc(gvT_ready.sem, 1)

                def head_products(h):
                    pe.wait_ge(kb_ready.sem, kb_ready.at(L, h))
                    if h >= 1:
                        pe.wait_ge(head_ready.sem, head_ready.at(L, h - 1))
                    for tb in range(TB):
                        mm = pe.matmul(ps[:, ACC[0], tb * P:(tb + 1) * P], gk[:, h, tb * P:(tb + 1) * P],
                                       kb[:, h % 2, tb * P:(tb + 1) * P], start=True, stop=True)
                    mm.then_inc(kk_ready.sem, 1)
                    for tb in range(TB):
                        mm = pe.matmul(ps[:, ACC[1], tb * P:(tb + 1) * P], gk[:, h, tb * P:(tb + 1) * P],
                                       gq[:, h, tb * P:(tb + 1) * P], start=True, stop=True)
                    mm.then_inc(qk_ready.sem, 1)

                head_in(0)
                for h in range(GH):
                    if h + 1 < GH:
                        head_in(h + 1)
                    head_products(h)

                def level_first(n):
                    h = n % GH
                    pe.wait_ge(lt_ready.sem, lt_ready.at(L, n))
                    if 2 <= n < GH + 2:
                        pe.wait_ge(x_new.sem, x_new.at(L, n - 2))
                    elif n >= GH + 2:
                        pe.wait_ge(p1_kept.sem, p1_kept.at(L, n - 2 - GH))
                    for tb in range(TB):
                        c = slice(tb * P, (tb + 1) * P)
                        if n < GH:
                            mm = pe.transpose(ps[:, ROT[n % 2], c], lt[:, n % 2, c], ident[:])
                        else:
                            mm = pe.matmul(ps[:, ROT[n % 2], c], lt[:, n % 2, c], gk[:, h, c], start=True, stop=True)
                    mm.then_inc(p1_ready.sem, 1)

                def level_second(n):
                    h = n % GH
                    pe.wait_ge(p1_kept.sem, p1_kept.at(L, n - GH))
                    if n >= GH + 2:
                        pe.wait_ge(x_new.sem, x_new.at(L, n - 2))
                    if n < GH * (LEVELS - 1):
                        for tb in range(TB):
                            c = slice(tb * P, (tb + 1) * P)
                            mm = pe.matmul(ps[:, STAT[n % 2], c], xT[:, h, c], p1[:, n % 2, c], start=True, stop=True)
                        mm.then_inc(xp_ready.sem, 1)
                    for tb in range(TB):
                        c = slice(tb * P, (tb + 1) * P)
                        mm = pe.matmul(ps[:, TRN[n % 2], c], p1[:, n % 2, c], xT[:, h, c], start=True, stop=True)
                    mm.then_inc(xpt_ready.sem, 1)

                def mean_sum():
                    for i in range(NC):
                        pe.wait_ge(dw_ready.sem, dw_ready.at(L, i))
                        mm = pe.matmul(ps[:, ACC[0], :], ones[:], yc[:, i, :], start=(i == 0), stop=(i == NC - 1))
                    mm.then_inc(mean_ready.sem, 1)

                def centered_sum():
                    for i in range(NC):
                        pe.wait_ge(lnsq.sem, lnsq.at(L, i))
                        pe.matmul(ps[:, ACC[1], :], ones[:], msq2[:, i % 2, :], start=(i == 0), stop=(i == NC - 1))\
                            .then_inc(lnsq_used.sem, 1)

                pe.wait_ge(head_ready.sem, head_ready.at(L, GH - 1))
                for n in range(GH * LEVELS + 1):
                    if n < GH * LEVELS:
                        level_first(n)
                    if n == 6:
                        mean_sum()
                    if n == 13:
                        centered_sum()
                    if n >= GH + 1:
                        level_second(n - 1)
                for h in range(GH):
                    pe.wait_ge(x_new.sem, x_new.at(L, GH * (LEVELS - 1) + h))
                    if h == 0:
                        pe.wait_ge(x_new.sem, x_new.at(L, GH * LEVELS - 1))
                    if h >= 2:
                        pe.wait_ge(uu_kept.sem, uu_kept.at(L, h - 2))
                    for tb in range(TB):
                        mm = pe.matmul(ps[:, ROT[h % 2], tb * P:(tb + 1) * P], xT[:, h, tb * P:(tb + 1) * P], vb[:, h, tb, :],
                                       start=True, stop=True)
                    mm.then_inc(uu_ready.sem, 1)
                    if h >= 2:
                        pe.wait_ge(ww_kept.sem, ww_kept.at(L, h - 2))
                    for tb in range(TB):
                        mm = pe.matmul(ps[:, STAT[h % 2], tb * P:(tb + 1) * P], kbeg[:, h, tb, :], xT[:, h, tb * P:(tb + 1) * P],
                                       start=True, stop=True)
                    mm.then_inc(ww_ready.sem, 1)
                pe.wait_ge(uu_kept.sem, uu_kept.at(L, GH - 1))
                pe.wait_ge(ww_kept.sem, ww_kept.at(L, GH - 1))
                wTf = kbeg[:].rearrange("p h t d -> p h (t d)")

                def chunk_out(c):
                    r, at = CH * (c % 2), slice(c * CH, (c + 1) * CH)
                    if c >= 2:
                        pe.wait_ge(o_kept.sem, o_kept.at(L, c - 2))
                    if c == NCH - 1:
                        pe.wait_ge(vn_ready.sem, vn_ready.at(L, c))
                    for h in range(GH):
                        pe.matmul(ps[:, STAT[c % 2], h * CH:(h + 1) * CH], states[c % 2][:, h, :], gq[:, h, at], start=True, stop=False)
                        mm = pe.matmul(ps[:, STAT[c % 2], h * CH:(h + 1) * CH], vn[r:r + CH, h, :], intraT[r:r + CH, h, at],
                                       start=False, stop=True)
                    mm.then_inc(o_ready.sem, 1)

                for c in range(NCH):
                    tb, r = c // 2, CH * (c % 2)
                    at = slice(c * CH, (c + 1) * CH)
                    pe.wait_ge(state_ready.sem, state_ready.at(L, c))
                    for h in range(GH):
                        mm = pe.matmul(ps[r:r + CH, ROT[c % 2], h * P:(h + 1) * P], wTf[:, h, at], states[c % 2][:, h, :],
                                       start=True, stop=True)
                    mm.then_inc(ws_ready.sem, 1)
                    if c >= 1:
                        chunk_out(c - 1)
                    if c < NCH - 1:
                        pe.wait_ge(vn_ready.sem, vn_ready.at(L, c))
                        for h in range(GH):
                            mm = pe.matmul(ps[:, TRN[c % 2], h * P:(h + 1) * P], kout[r:r + CH, h, tb, :], vn[r:r + CH, h, :],
                                           start=True, stop=True)
                        mm.then_inc(ds_ready.sem, 1)
                chunk_out(NCH - 1)
                for h in range(GH):
                    pe.wait_ge(ogsq.sem, ogsq.at(L, h))
                    if h >= 2:
                        pe.wait_ge(ogrs.sem, ogrs.at(L, h - 2))
                    pe.matmul(ps[:, STAT[h % 2], :], ones[:], msq2[:, h % 2, :], start=True, stop=True).then_inc(ogstat.sem, 1)

                def need_merged2(k, s):
                    if s == 0:
                        pe.wait_ge(merged2_ready.sem, merged2_ready.at(L, k))

                def post_sum(i):
                    pe.wait_ge(yssq_done.sem, yssq_done.at(L, i * KD + KD - 1))
                    pe.matmul(ps[:, STAT[1], :], ones[:], prod[:], start=True, stop=True).then_inc(ystat_ready.sem, 1)

                with pe.Fori(0, PAIRS_O) as j:
                    for s in range(2):
                        unit(V + OFF_O2 + j, s, KD, a_hi, a_lo, need_merged2)
                post_sum(0)
                first_pair(V + OFF_UP2[0], KD, h_hi, h_lo, need_h(G + 1), (KD - 1, lambda: norm_sum(G + 1)))
                for hf in range(2):
                    with pe.Fori(1 - hf, PAIRS_UP) as j:
                        for s in range(2):
                            unit(V + OFF_UP2[hf] + j, s, KD, h_hi, h_lo, need_h(G + 1))

                    def need_a2(k, s, hf=hf):
                        if s == 0:
                            pe.wait_ge(a2_ready.sem, a2_ready.at(L, hf * HALF + k))

                    with pe.Fori(0, PAIRS_DOWN) as j:
                        for s in range(2):
                            unit(V + OFF_DOWN2[hf] + j, s, HALF, a_hi, a_lo, need_a2)
                post_sum(1)

            pe.wait_ge(h_ready.sem, h_ready.at(4 * DEPTH, KD - 1))
            for tb in range(TB):
                for hf in range(2):
                    i = tb * 2 + hf
                    if i >= 2:
                        pe.wait_ge(out_kept.sem, i - 1)
                    for n in range(4):
                        mm = pe.transpose(ps[:, ROT[i % 2], n * P:(n + 1) * P],
                                          x[:, 4 * hf + n, tb * P:(tb + 1) * P], ident[:])
                    mm.then_inc(out_turned.sem, 1)

        @block.scalar
        def _(act):
            order = Order(act, act_step.sem, consts_made)

            act.wait_ge(consts_made.sem, 1)
            count = 0
            for dst, src in setup_rows():
                act.dma_start(dst, src).then_inc(setup_loaded.sem, 16)
                count += 16
            assert count == SETUP[0]

            def hi_next(v, s, kt):
                act.wait_ge(w_loaded[s].sem, v * 16 + 16)
                act.wait_ge(unit_done.sem, v * 2 + (s + 1))
                act.activation(whi[s][:, 0:kt, :], raw[s][:, 0:kt, :], ACT.Copy).then_inc(w_hi_ready.sem, 1)

            def rs(dst, src, width, e=0):
                act.activation(lnt[:], src, ACT.Ln, bias=eps[:, e:e + 1], scale=1.0 / width).then_inc(act_step.sem, 1)
                order.n += 1
                act.wait_ge(act_step.sem, order.n)
                return act.activation(dst, lnt[:], ACT.Exp, scale=-0.5)

            def logs_and_exps():
                act.preload_act_table_set("natural_log_exp_and_others")

            def norm_rstd(gen):
                logs_and_exps()
                act.wait_ge(stat_ready.sem, stat_ready.at(gen, 0))
                order.settle()
                order.told(rs(rstd[:], ps[:, STAT[0], :], DM), rstd_ready, gen, 0)

            def split_h(gen, n, s, wait_x):
                wait_x()
                if not (isinstance(gen, int) and n < 2):
                    act.wait_ge(ssq_done.sem, ssq_done.at(gen, n - 2))
                act.activation(sqt[:, s, :], tile(x, n), ACT.Square).then_inc(sq_ready.sem, 1)
                act.activation(tile(h_hi, n), tile(x, n), ACT.Identity, scale=gain(gen * KD + n))\
                    .then_inc(hhi_ready.sem, 1)

            for s in range(2):
                hi_next(0, s, KD)
            act.wait_ge(consts_made.sem, 1)
            act.wait_ge(params_kept.sem, N_ROWS)
            for n in range(KD):
                split_h(0, n, n % 2, lambda n=n: act.wait_ge(x_ready.sem, n + 1))

            with act.Fori(0, DEPTH) as L:
                V = L * PAIRS1
                act.wait_ge(unit_done.sem, V * 2 + 2)
                act.wait_ge(params_kept.sem, N_ROWS)
                act.dma_start(sgw, D["sg_w"][ds(L, 1)].rearrange("l h p q -> p (l h) q")).then_inc(sgw_loaded.sem, 16)
                for r in range(2):
                    act.dma_start(sgb[64 * r:64 * r + 64, :, :],
                                  D["sg_b"][ds(L, 1), r::2, :].to_broadcast([64, NS, P])).then_inc(sgb_loaded.sem, 16)
                norm_rstd(L * 2)

                def head_rs(i, stat, rsig):
                    act.wait_ge(stat.sem, stat.at(L, i))
                    order.settle()
                    order.told(rs(mrs[:, i % 2, :], ps[:, STAT[i % 2], :], HD), rsig, L, i)

                def qk_square(i):
                    act.wait_ge(acc_free.sem, V * 2 + i + 4)
                    if i >= 2:
                        act.wait_ge(qkstat_ready.sem, qkstat_ready.at(L, i - 2))
                    order.told(act.activation(msq[:, i % 2, :], zk[:] if i == 0 else zq[:, i - 1, :], ACT.Square), qksq_ready, L, i)

                def qk_rs(i):
                    if i >= 2:
                        act.wait_ge(qkn_ready.sem, qkn_ready.at(L, i - 2))
                    head_rs(i, qkstat_ready, qkrs_ready)

                def qk_high(i):
                    act.wait_ge(rope_ready.sem, rope_ready.at(L, i))
                    if i == 0:
                        for g in range(NKV):
                            for r in range(2):
                                order.step(act.activation(kd2[64 * r:64 * r + 64, g, :], zk[64 * g:64 * g + 64, :], ACT.Copy))
                        order.settle()
                        order.step(act.activation(kr[0][:], kd[0], ACT.Copy))
                        order.told(act.activation(kr[1][:], kd[1], ACT.Copy), qr_ready, L, 0)
                    else:
                        order.step(act.activation(qab[0:64, i - 1, 0, :], zq[0:64, i - 1, :], ACT.Copy))
                        order.told(act.activation(qab[64:128, i - 1, 1, :], zq[64:128, i - 1, :], ACT.Copy), qr_ready, L, i)

                def gelu(i):
                    z = vv[:, i, :] if i < NS else u[:, i - NS, :]
                    act.wait_ge(acc_free.sem, V * 2 + (NQ + 2 + i + 3))
                    order.told(act.activation(z, z, ACT.Gelu_apprx_tanh), gelu_ready, L, i)

                def vv_square(t):
                    if t < 2:
                        act.wait_ge(qkstat_ready.sem, qkstat_ready.at(L, NQ))
                    else:
                        act.wait_ge(vvstat_ready.sem, vvstat_ready.at(L, t - 2))
                    order.settle()
                    order.told(act.activation(msq[:, t % 2, :], vv[:, t, :], ACT.Square), vvsq_ready, L, t)

                def vv_rs(t):
                    if t < 2:
                        act.wait_ge(qkn_ready.sem, qkn_ready.at(L, NQ))
                    else:
                        act.wait_ge(vvn_ready.sem, vvn_ready.at(L, t - 2))
                    head_rs(t, vvstat_ready, vvrs_ready)

                def vvT_copy(t):
                    act.wait_ge(vvT_ready.sem, vvT_ready.at(L, t))
                    order.told(act.activation(vvT[:, :, t * P:(t + 1) * P],
                                              ps[:, TRN[t % 2], :].rearrange("q (c f) -> q c f", f=P), ACT.Copy),
                               vvT_kept, L, t)

                for i in range(N_IN):
                    hi_next(V + (i // 2 + 1), i % 2, KD)
                    if 0 <= i - 1 <= NQ:
                        qk_square(i - 1)
                    if 0 <= i - 2 <= NQ:
                        qk_rs(i - 2)
                    if 0 <= i - 4 <= NQ:
                        qk_high(i - 4)
                    if i == 5:
                        for b in range(2):
                            act.wait_ge(wT_ready.sem, wT_ready.at(L, b))
                            order.told(act.activation(wT[:, 4 * b:4 * b + 4, :].rearrange("q h p -> q (h p)"),
                                                      ps[:, TRN[b], :], ACT.Copy), wT_kept, L, b)
                    if i == 7:
                        act.wait_ge(vT_ready.sem, vT_ready.at(L, 0))
                        act.wait_ge(vones_ready.sem, vones_ready.at(L, 0))
                        for g in range(NKV):
                            for r in range(2):
                                ins = act.activation(vaug[:, g, r, :, 64 * r:64 * r + 64],
                                                     ps[:, TRN[0], :].rearrange("q (k f) -> q k f", f=P)[:, :, 64 * g:64 * g + 64],
                                                     ACT.Copy)
                                if (g, r) == (NKV - 1, 1):
                                    order.told(ins, vaug_ready, L, 0)
                                else:
                                    order.step(ins)
                        gelu(0)
                    if i == 8:
                        gelu(1)
                        gelu(2)
                        vv_square(0)
                    if i == 9:
                        gelu(3)
                        vv_square(1)
                    if i == 10:
                        gelu(NS)
                    if i == 11:
                        logs_and_exps()
                        vv_rs(0)
                        vv_rs(1)
                        vv_square(2)
                        vv_square(3)
                    if i == 13:
                        vvT_copy(0)
                        vvT_copy(1)
                        vv_rs(2)
                        vv_rs(3)
                for t in range(1, NS):
                    gelu(NS + t)
                logs_and_exps()
                vvT_copy(2)
                vvT_copy(3)

                def exponentials(h, kt):
                    n = h * TB + kt
                    act.wait_ge(ST_ready.sem, ST_ready.at(L, n))
                    if n >= TB:
                        act.wait_ge(PV_done.sem, PV_done.at(L, n - TB))
                    else:
                        act.wait_ge(wT_ready.sem, wT_ready.at(L, 1))
                    order.told(act.activation(probs[:, kt, :], ps[:, ROT[kt % 2], :], ACT.Exp, scale=HD ** -0.5), P_ready, L, n)

                def sums_inverted(h):
                    r = 64 * (h % 2)
                    act.wait_ge(PV_done.sem, PV_done.at(L, h * TB + TB - 1))
                    order.settle()
                    order.step(act.activation(lnt[r:r + 64, :], ps[64 - r:128 - r, TRN[h % 2], :], ACT.Ln))
                    if h >= 2:
                        act.wait_ge(ao_ready.sem, ao_ready.at(L, h - 2))
                    else:
                        act.wait_ge(vvn_ready.sem, vvn_ready.at(L, NS - 1))
                    order.settle()
                    order.told(act.activation(mrs[r:r + 64, 0, :], lnt[r:r + 64, :], ACT.Exp, scale=-1.0), rl_ready, L, h)

                def mixer_square(i):
                    if i < NS:
                        act.wait_ge(sg_ready.sem, sg_ready.at(L, i))
                    else:
                        act.wait_ge(ao_ready.sem, ao_ready.at(L, 2 * (i - NS) + 1))
                    if i >= 2:
                        act.wait_ge(osq_used.sem, osq_used.at(L, i - 2))
                    else:
                        act.wait_ge(vvstat_ready.sem, vvstat_ready.at(L, NS - 1))
                    order.told(act.activation(msq[:, i % 2, :], u[:, i, :] if i < NS else ao[:, i - NS, :], ACT.Square), osq_ready, L, i)

                def mixer_rs(b):
                    act.wait_ge(osq_used.sem, osq_used.at(L, b * NS + NS - 1))
                    order.settle()
                    order.told(rs(ors[:, b, :], ps[:, (ACC[0], STAT[1])[b], :], (SGW, AW)[b]), ors_ready, L, b)

                def merged_high(i):
                    act.wait_ge(mtmp_ready.sem, mtmp_ready.at(L, i))
                    order.told(act.activation(a_hi[:, (i + NQ) % KD, :], mtmp[:, i % 2, :], ACT.Copy), mhi_ready, L, i)

                for h in range(NH):
                    for kt in range(TB):
                        exponentials(h, kt)
                        if kt == 1 and h >= 1:
                            sums_inverted(h - 1)
                    if h in (1, 2):
                        mixer_square(2 * h - 2)
                        mixer_square(2 * h - 1)
                    if h == 4:
                        mixer_rs(0)
                    if h in (3, 5):
                        mixer_square(NS + (h - 3) // 2)
                    if h in (5, 6):
                        merged_high(2 * h - 10)
                        merged_high(2 * h - 9)
                mixer_square(NS + 2)
                sums_inverted(NH - 1)
                mixer_square(NS + 3)
                mixer_rs(1)
                for i in range(NS, NS + NQ):
                    merged_high(i)

                order.restart()
                with act.Fori(0, PAIRS_O) as j:
                    for s in range(2):
                        hi_next(V + OFF_O + 1 + j, s, KD)
                        split_h(L * 2 + 1, j * 2 + s, s, lambda: act.wait_ge(acc_free.sem, (V + OFF_O + j) * 2 + (s + 3)))
                norm_rstd(L * 2 + 1)
                order.restart()
                for hf in range(2):
                    def feed(j, kt, hf=hf):
                        v = V + OFF_UP[hf] + j
                        for s in range(2):
                            hi_next(v + 1, s, kt)
                            act.wait_ge(acc_free.sem, v * 2 + (s + 3))
                            col = s * NF + hf * HALF + j
                            act.activation(cv[s][:], pad[s][:, 1:SEQ + 1], ACT.Identity,
                                           scale=param(pb, L, 2 * NF + col), bias=param(pc, L, 2 * NF + col))\
                                .then_inc(center_ready.sem, 1)
                        t = hf * HALF + j
                        act.wait_ge(conv_ready.sem, L * 2 * NF + 2 * t + 1)
                        act.activation(cv[0][:], cv[0][:], ACT.Silu).then_inc(silu_ready.sem, 1)
                        act.wait_ge(prod_ready.sem, prod_ready.at(L, t))
                        act.activation(tile(a_hi, j), prod[:], ACT.Copy).then_inc(ahi_ready.sem, 1)

                    act.preload_act_table(ACT.Silu)
                    with act.Fori(0, PAIRS_UP - 1) as j:
                        feed(j, KD)
                    feed(PAIRS_UP - 1, HALF)

                    def drain(j, kt, hf=hf):
                        v = V + OFF_DOWN[hf] + j
                        for s in range(2):
                            hi_next(v + 1, s, kt)
                            if hf == 1:
                                split_h(L * 2 + 2, j * 2 + s, s, lambda: act.wait_ge(acc_free.sem, v * 2 + (s + 3)))

                    with act.Fori(0, PAIRS_DOWN - 1) as j:
                        drain(j, HALF)
                    drain(PAIRS_DOWN - 1, KD)

            with act.Fori(0, DEPTH) as L:
                V = BASE2 + L * PAIRS2
                G = L * 2 + 2 * DEPTH
                norm_rstd(G)
                NCOL = TB * GH
                flat = lambda n: cols[n][:].rearrange("p t h -> p (t h)")

                def gates():
                    act.wait_ge(gate_in.sem, gate_in.at(L, 0))
                    order.settle()
                    order.step(act.activation(expa[:], gate_par[:, 0, ds(L, 1), :].rearrange("p l h -> p (l h)"), ACT.Exp))
                    order.step(act.activation(cols["e"][:], cols["ax"][:], ACT.Exp, scale=-1.0))
                    order.told(act.activation(cols["beta"][:], cols["b"][:], ACT.Exp, scale=-1.0), gate_e1, L, 0)
                    order.settle()
                    order.told(act.activation(cols["l"][:], cols["e"][:], ACT.Ln, bias=ones[:, 0:1]), gate_e2, L, 0)

                def values_kept():
                    act.wait_ge(v2ones_ready.sem, v2ones_ready.at(L, 0))
                    for i in range(NA):
                        act.wait_ge(v2T_ready.sem, v2T_ready.at(L, i))
                        for r in range(2):
                            ins = act.activation(vaug2[:, 2 * i + r, :, 64 * r:64 * r + 64],
                                                 ps[:, TRN[i], :].rearrange("q (k f) -> q k f", f=P)[:, :, 64 * r:64 * r + 64], ACT.Copy)
                            if r:
                                order.told(ins, vaug2_ready, L, i)
                            else:
                                order.step(ins)

                def exponentials(h, kt):
                    n, q0 = h * TB + kt, kt * P
                    act.wait_ge(ST2_ready.sem, ST2_ready.at(L, n))
                    if n >= TB:
                        act.wait_ge(PV2_done.sem, PV2_done.at(L, n - TB))
                    order.told(act.activation(probs2[:, kt, q0:], ps[:, ROT[n % 2], q0:], ACT.Exp, scale=64 ** -0.5), E2_ready, L, n)

                def sums_inverted(h):
                    r = 64 * (h % 2)
                    act.wait_ge(PV2_done.sem, PV2_done.at(L, h * TB + TB - 1))
                    order.settle()
                    order.step(act.activation(lnt[r:r + 64, :], ps[64 - r:128 - r, TRN[h % 2], :], ACT.Ln))
                    act.wait_ge(rope2_ready.sem, rope2_ready.at(L, 2 * NA - 1))
                    if h >= 2:
                        act.wait_ge(ya_ready.sem, ya_ready.at(L, h - 2))
                    order.settle()
                    order.told(act.activation(ta[r:r + 64, :], lnt[r:r + 64, :], ACT.Exp, scale=-1.0), rl2_ready, L, h)

                def l2_square(i):
                    if i >= 4:
                        act.wait_ge(l2stat.sem, l2stat.at(L, i - 4))
                    order.settle()
                    order.told(act.activation(l2s[:, i % 4, :], gqkv[i], ACT.Square), l2sq, L, i)

                def l2_rs(i):
                    act.wait_ge(l2stat.sem, l2stat.at(L, i))
                    if i >= 4:
                        act.wait_ge(l2n.sem, l2n.at(L, i - 4))
                    order.settle()
                    order.told(rs(l2r[:, i % 4, :], ps[:, (STAT + ROT)[i % 4], :], 1), l2rs, L, i)

                def short_silu(i):
                    act.wait_ge(sc_ready.sem, sc_ready.at(L, i))
                    order.told(act.activation(gqkv[i], gqkv[i], ACT.Silu), sc_silu, L, i)

                for i in range(N_IN2):
                    hi_next(V + (i // 2 + 1), i % 2, KD)
                    n = i - 3 * NA - 2 * NC
                    if 0 <= n < NG:
                        act.wait_ge(acc_free.sem, V * 2 + i + 3)
                        order.told(act.activation(gqkv[n], zp[:, n % 2, GT - 1:GT - 1 + SEQ], ACT.Copy,
                                                  scale=param(pd, L, D_SC + (GT - 1) * NG + n)), sc_center, L, n)
                    if 0 <= i - 3 < 2 * NA:
                        act.wait_ge(rope2_ready.sem, rope2_ready.at(L, i - 3))
                        order.told(act.activation(qkr2[:, i - 3, :], za[:, i - 3, :], ACT.Copy), qkr2_ready, L, i - 3)
                    if i == 7:
                        gates()
                    if i == 8:
                        values_kept()
                    if i == 10:
                        for t in range(NC):
                            act.wait_ge(acc_free.sem, V * 2 + (3 * NA + NC + t + 3))
                            order.told(act.activation(cg[:, t, :], cg[:, t, :], ACT.Sigmoid), cg_ready, L, t)
                        logs_and_exps()
                    for h in range(AH):
                        if i == 14 + 2 * h:
                            sums_inverted(h)
                    for h in range(AH):
                        if i - 10 - 2 * h in (0, 1):
                            for kt in range(2 * (i - 10 - 2 * h), 2 * (i - 10 - 2 * h) + 2):
                                exponentials(h, kt)
                    if 20 <= i <= 22:
                        for t in range(4 * (i - 20), 4 * (i - 20) + 4):
                            short_silu(t)
                    if i == 21:
                        for t in range(4):
                            l2_square(t)
                    if i == 22:
                        logs_and_exps()
                    if i == 23:
                        for t in range(4):
                            l2_rs(t)
                        for t in range(4, 8):
                            l2_square(t)
                        act.wait_ge(gc_kept.sem, gc_kept.at(L, 0))
                        order.step(act.activation(flat("egc"), flat("gc"), ACT.Exp))
                        act.wait_ge(dg_ready.sem, dg_ready.at(L, 0))
                        order.told(act.activation(flat("egl"), flat("dg"), ACT.Exp), eg_cols, L, 0)
                    if i == 25:
                        for t in range(4, 8):
                            l2_rs(t)
                for h in range(GH):
                    act.wait_ge(gap_ready.sem, gap_ready.at(L, h))
                    if h >= 2:
                        act.wait_ge(head_ready.sem, head_ready.at(L, h - 2))
                    order.told(act.activation(eg[:, h % 2, :], ps[:, ROT[h % 2], :], ACT.Exp), eg_ready, L, h)
                    order.told(act.activation(dm[:, h % 2, :], dm[:, h % 2, :], ACT.Exp), decay_ready, L, h)
                for n in range(GH, GH * LEVELS):
                    act.wait_ge(p1_ready.sem, p1_ready.at(L, n))
                    if n >= GH + 2:
                        act.wait_ge(xpt_ready.sem, xpt_ready.at(L, n - 2 - GH))
                    else:
                        act.wait_ge(head_ready.sem, head_ready.at(L, GH - 1))
                    order.told(act.activation(p1[:, n % 2, :], ps[:, ROT[n % 2], :], ACT.Copy), p1_kept, L, n - GH)
                    if n == 8:
                        act.wait_ge(mean_ready.sem, mean_ready.at(L, 0))
                        order.told(act.activation(lnt[:], ps[:, ACC[0], :], ACT.Copy, scale=1.0 / CC), mean_kept, L, 0)
                    if n == 11:
                        for i in range(NC):
                            act.wait_ge(centered.sem, centered.at(L, i))
                            order.told(act.activation(msq2[:, i % 2, :], yc[:, i, :], ACT.Square), lnsq, L, i)
                    if n == 15:
                        act.wait_ge(lnsq_used.sem, lnsq_used.at(L, NC - 1))
                        order.settle()
                        order.told(rs(mrs2[:, 0, :], ps[:, ACC[1], :], CC, 1), ln_rs, L, 0)
                for h in range(GH):
                    act.wait_ge(uu_ready.sem, uu_ready.at(L, h))
                    order.told(act.activation(vb[:, h, :, :].rearrange("p t d -> p (t d)"), ps[:, ROT[h % 2], :], ACT.Copy), uu_kept, L, h)
                act.wait_ge(ww_ready.sem, ww_ready.at(L, GH - 1))
                for c in range(NCH):
                    act.wait_ge(o_ready.sem, o_ready.at(L, c))
                    order.told(act.activation(og[:, :, c * CH:(c + 1) * CH],
                                              ps[:, STAT[c % 2], 0:GH * CH].rearrange("p (h t) -> p h t", t=CH), ACT.Copy), o_kept, L, c)
                    if c == 0:
                        for i in range(NC):
                            act.wait_ge(ln_scaled.sem, ln_scaled.at(L, i))
                            order.told(act.activation(yc[:, i, :], yc[:, i, :], ACT.Silu, bias=param(pd, L, D_LNB + i)), yc_ready, L, i)
                        for h in range(GH):
                            act.wait_ge(acc_free.sem, V * 2 + (N_IN2 - GH + h + 3))
                            order.told(act.activation(gz[:, h, :], gz[:, h, :], ACT.Silu), gate_ready, L, h)
                        logs_and_exps()
                order.settle()
                for i in range(GH + 1):
                    if i < GH:
                        if i >= 2:
                            act.wait_ge(ogstat.sem, ogstat.at(L, i - 2))
                        order.told(act.activation(msq2[:, i % 2, :], og[:, i, :], ACT.Square), ogsq, L, i)
                    if i >= 1:
                        act.wait_ge(ogstat.sem, ogstat.at(L, i - 1))
                        if i >= 3:
                            act.wait_ge(og_ready.sem, og_ready.at(L, i - 3))
                        order.settle()
                        order.told(rs(mrs2[:, (i - 1) % 2, :], ps[:, STAT[(i - 1) % 2], :], P), ogrs, L, i - 1)
                act.wait_ge(og_ready.sem, og_ready.at(L, GH - 1))
                for n, src in enumerate(mixed):
                    order.told(act.activation(a_hi[:, n, :], src, ACT.Copy), m2hi_ready, L, n)

                order.settle()
                order.step(act.activation(after_core[:], ones[:, 0:1], ACT.Copy))
                order.restart()

                def post_squares(i, v, j, hi_kt):
                    for s in range(2):
                        hi_next(v + 1, s, hi_kt)
                        act.wait_ge(acc_free.sem, v * 2 + (s + 3))
                        n = j * 2 + s
                        if not (isinstance(j, int) and j == 0):
                            act.wait_ge(yssq_done.sem, yssq_done.at(L, i * KD + n - 2))
                        act.activation(cv[s][:], tile(y, n), ACT.Square).then_inc(ysq_ready.sem, 1)

                def post_norm(i, gen):
                    logs_and_exps()
                    act.wait_ge(ystat_ready.sem, ystat_ready.at(L, i))
                    order.settle()
                    order.told(rs(cv[0][:], ps[:, STAT[1], :], DM), yrs_ready, L, i)
                    order.restart()
                    with act.Fori(0, PAIRS_O) as j:
                        for s in range(2):
                            split_h(gen, j * 2 + s, s, lambda: act.wait_ge(x2_ready.sem, x2_ready.at(L, i * KD + j * 2 + s)))

                post_squares(0, V + OFF_O2, 0, KD)
                with act.Fori(1, PAIRS_O) as j:
                    post_squares(0, V + OFF_O2 + j, j, KD)
                post_norm(0, G + 1)
                norm_rstd(G + 1)
                order.restart()
                for hf in range(2):
                    def feed2(j, kt, hf=hf):
                        v = V + OFF_UP2[hf] + j
                        t = hf * HALF + j
                        hi_next(v + 1, 0, kt)
                        act.wait_ge(acc_free.sem, v * 2 + 3)
                        act.activation(cv[0][:], cv[0][:], ACT.Silu).then_inc(silu2_ready.sem, 1)
                        hi_next(v + 1, 1, kt)
                        act.wait_ge(prod2_ready.sem, prod2_ready.at(L, t))
                        act.activation(tile(a_hi, j), prod[:], ACT.Copy).then_inc(a2hi_ready.sem, 1)

                    act.preload_act_table(ACT.Silu)
                    with act.Fori(0, PAIRS_UP - 1) as j:
                        feed2(j, KD)
                    feed2(PAIRS_UP - 1, HALF)
                    if hf == 0:
                        with act.Fori(0, PAIRS_DOWN - 1) as j:
                            for s in range(2):
                                hi_next(V + OFF_DOWN2[hf] + 1 + j, s, HALF)
                        for s in range(2):
                            hi_next(V + OFF_DOWN2[hf] + PAIRS_DOWN, s, KD)
                    else:
                        post_squares(1, V + OFF_DOWN2[hf], 0, HALF)
                        with act.Fori(1, PAIRS_DOWN - 1) as j:
                            post_squares(1, V + OFF_DOWN2[hf] + j, j, HALF)
                        post_squares(1, V + OFF_DOWN2[hf] + PAIRS_DOWN - 1, PAIRS_DOWN - 1, KD)
                post_norm(1, G + 2)

        @block.vector
        def _(dve):
            order = Order(dve, dve_step.sem, consts_made)
            dve.memset(ones[:], 1.0).then_inc(dve_step.sem, 1)
            dve.memset(eps[:, 0:1], EPS).then_inc(dve_step.sem, 1)
            dve.memset(eps[:, 1:2], LN_EPS).then_inc(dve_step.sem, 1)
            dve.memset(rows[:], 1.0).then_inc(dve_step.sem, 1)
            order.n, order.last = 4, (dve_step.sem, 4)
            order.settle()
            dve.tensor_scalar(negones[:], ones[:], -1.0, None, ALU.mult).then_inc(consts_made.sem, 1)
            dve.wait_ge(consts_made.sem, 1)
            dve.sem_inc(acc_free.sem, 2)
            for i, r in enumerate(ROWS):
                dve.wait_ge(params_turned.sem, i + 1)
                dve.tensor_copy(COLS[i], ps[:, TRN[i % 2], 0:r]).then_inc(params_kept.sem, 1)

            def grown(gen, n, s, first):
                dve.wait_ge(sq_ready.sem, sq_ready.at(gen, n))
                if not first:
                    dve.wait_ge(ssq_done.sem, ssq_done.at(gen, n - 1))
                if first:
                    ins = dve.tensor_copy(ssq[:], sqt[:, s, :])
                else:
                    ins = dve.tensor_tensor(ssq[:], ssq[:], sqt[:, s, :], ALU.add)
                order.told(ins, ssq_done, gen, n)

            def low_half(gen, n):
                dve.wait_ge(hhi_ready.sem, hhi_ready.at(gen, n))
                ins = dve.scalar_tensor_tensor(tile(h_lo, n), tile(x, n), gain(gen * KD + n),
                                               tile(h_hi, n).bitcast(F32), ALU.mult, ALU.subtract)
                order.told(ins, h_ready, gen, n)

            def tail(gen, n, s, first):
                grown(gen, n, s, first)
                low_half(gen, n)

            for n in range(KD):
                dve.wait_ge(x_turned.sem, n + 1)
                order.told(dve.tensor_copy(x[:, n, :], ps[:, ROT[n % 2], :]), x_ready, 0, n)
                tail(0, n, n % 2, n == 0)

            order.restart()
            with dve.Fori(0, DEPTH) as L:
                V = L * PAIRS1
                dve.wait_ge(rstd_ready.sem, rstd_ready.at(L * 2, 0))
                dests = [zv[:], zk[:]] + [t[:, i, :] for t, m in ((zq, NQ), (vv, NS), (u, NS)) for i in range(m)]

                def qk_norm(i):
                    z = dests[i + 1]
                    dve.wait_ge(qkrs_ready.sem, qkrs_ready.at(L, i))
                    order.told(dve.scalar_tensor_tensor(z, z, param(pa, L, 1 if i == 0 else 0), mrs[:, i % 2, :],
                                                        ALU.mult, ALU.mult), qkn_ready, L, i)

                def qk_rotary(i):
                    z = dests[i + 1]
                    dve.wait_ge(rot_ready.sem, rot_ready.at(L, i))
                    order.settle()
                    order.told(dve.tensor_tensor(t2[:], ps[:, ROT[i % 2], :], rope[:, 1, :], ALU.mult), rot_used, L, i)
                    order.step(dve.tensor_tensor(t1[:], z, rope[:, 0, :], ALU.mult))
                    order.settle()
                    order.told(dve.tensor_tensor(z, t1[:], t2[:], ALU.add), rope_ready, L, i)

                def qk_low(i):
                    dve.wait_ge(qr_ready.sem, qr_ready.at(L, i))
                    if i == 0:
                        order.step(dve.tensor_tensor(kl[0][:], kd[0], kr[0][:].bitcast(F32), ALU.subtract))
                        order.told(dve.tensor_tensor(kl[1][:], kd[1], kr[1][:].bitcast(F32), ALU.subtract), ql_ready, L, 0)
                    else:
                        order.step(dve.tensor_tensor(qab[64:128, i - 1, 0, :], zq[0:64, i - 1, :],
                                                     qab[0:64, i - 1, 0, :].bitcast(F32), ALU.subtract))
                        order.told(dve.tensor_tensor(qab[0:64, i - 1, 1, :], zq[64:128, i - 1, :],
                                                     qab[64:128, i - 1, 1, :].bitcast(F32), ALU.subtract), ql_ready, L, i)

                def vv_norm(t):
                    dve.wait_ge(vvrs_ready.sem, vvrs_ready.at(L, t))
                    order.told(dve.scalar_tensor_tensor(vv[:, t, :], vv[:, t, :], param(pa, L, 2 + t), mrs[:, t % 2, :],
                                                        ALU.mult, ALU.mult), vvn_ready, L, t)

                for i, z in enumerate(dests):
                    dve.wait_ge(unit_done.sem, V * 2 + i + 3)
                    dve.tensor_tensor(z, ps[:, ACC[i % 2], :], rstd[:], ALU.mult).then_inc(acc_free.sem, 1)
                    order.last = (acc_free.sem, V * 2 + i + 3)
                    if i == 1:
                        for g in range(NKV):
                            for r in range(2):
                                ins = dve.memset(vaug[:, g, r, :, 64 - 64 * r:128 - 64 * r], 1.0)
                                if (g, r) == (NKV - 1, 1):
                                    order.told(ins, vones_ready, L, 0)
                                else:
                                    order.step(ins)
                    if 0 <= i - 3 <= NQ:
                        qk_rotary(i - 3)
                    if 0 <= i - 2 <= NQ:
                        qk_norm(i - 2)
                    if 0 <= i - 5 <= NQ:
                        qk_low(i - 5)
                    if i in (11, 13):
                        vv_norm(i - 11)
                        vv_norm(i - 10)

                def row_max(h):
                    for b in range(2):
                        dve.wait_ge(S_ready.sem, S_ready.at(L, 2 * h + b))
                        order.settle()
                        order.told(dve.tensor_reduce(mx[:, h % 2, 2 * b:2 * b + 2], ps[:, STAT[0]:STAT[1] + 1, :], AX, ALU.max),
                                   S_used, L, 2 * h + b)
                    if h >= 2:
                        dve.wait_ge(ST_ready.sem, ST_ready.at(L, (h - 1) * TB - 1))
                    order.settle()
                    order.told(dve.tensor_tensor(diag[:, h % 2, :, :], ident[:].unsqueeze(1).to_broadcast([P, TB, P]),
                                                 mx[:, h % 2, :].unsqueeze(2).to_broadcast([P, TB, P]), ALU.mult),
                               diag_ready, L, h)

                def gating(t):
                    dve.wait_ge(mix_ready.sem, mix_ready.at(L, t))
                    order.settle()
                    order.told(dve.tensor_tensor(
                        t1[:].rearrange("p (c q) -> p c q", q=P), ps[:, ACC[t % 2], :].rearrange("p (c q) -> p c q", q=P),
                        sgb[:, t, :].unsqueeze(1).to_broadcast([P, TB, P]), ALU.add), mix_used, L, t)
                    dve.wait_ge(gelu_ready.sem, gelu_ready.at(L, NS + t))
                    order.settle()
                    order.told(dve.tensor_tensor(u[:, t, :], u[:, t, :], t1[:], ALU.mult), sg_ready, L, t)

                def normed(h):
                    t, r = h // 2, 64 * (h % 2)
                    dve.wait_ge(rl_ready.sem, rl_ready.at(L, h))
                    order.told(dve.tensor_tensor(ao[r:r + 64, t, :], ps[r:r + 64, TRN[h % 2], :], mrs[r:r + 64, 0, :], ALU.mult),
                               ao_ready, L, h)

                def merge(i):
                    if i % NS == 0:
                        dve.wait_ge(ors_ready.sem, ors_ready.at(L, i // NS))
                    z, g = (u[:, i, :], 6 + NQ + i) if i < NS else (ao[:, i - NS, :], 6 + i - NS)
                    order.settle()
                    order.told(dve.scalar_tensor_tensor(mtmp[:, i % 2, :], z, param(pa, L, g), ors[:, i // NS, :],
                                                        ALU.mult, ALU.mult), mtmp_ready, L, i)

                def merged_low(i):
                    dve.wait_ge(mhi_ready.sem, mhi_ready.at(L, i))
                    k = (i + NQ) % KD
                    order.told(dve.tensor_tensor(a_lo[:, k, :], mtmp[:, i % 2, :], a_hi[:, k, :].bitcast(F32), ALU.subtract),
                               merged_ready, L, i)

                dve.wait_ge(sgb_loaded.sem, L * 32 + 32)
                row_max(0)
                gating(0)
                gating(1)
                for h in range(NH):
                    if h + 1 < NH:
                        row_max(h + 1)
                    if h >= 1:
                        normed(h - 1)
                    if h == 1:
                        gating(2)
                        gating(3)
                    if h == 6:
                        merged_low(0)
                        merged_low(1)
                    if h in (5, 6):
                        merge(2 * h - 10)
                        merge(2 * h - 9)
                    if h == 7:
                        merged_low(2)
                        merged_low(3)
                normed(NH - 1)
                for i in range(NS, NS + NQ + 1):
                    if i < NS + NQ:
                        merge(i)
                    if i > NS:
                        merged_low(i - 1)

                def residual(v, s, n):
                    dve.wait_ge(unit_done.sem, v * 2 + (s + 3))
                    dve.tensor_tensor(tile(x, n), tile(x, n), ps[:, ACC[s], :], ALU.add).then_inc(acc_free.sem, 1)
                    order.last = (acc_free.sem, v * 2 + (s + 3))

                def residual_norm(gen, v, j, first):
                    for s in range(2):
                        residual(v, s, j * 2 + s)
                        tail(gen, j * 2 + s, s, first and s == 0)

                order.restart()
                residual_norm(L * 2 + 1, V + OFF_O, 0, True)
                order.restart()
                with dve.Fori(1, PAIRS_O) as j:
                    residual_norm(L * 2 + 1, V + OFF_O + j, j, False)
                    order.restart()
                order.settle()
                for s in range(2):
                    for e in (0, SEQ + 1):
                        order.step(dve.memset(pad[s][:, e:e + 1], 0.0))
                order.restart()
                order.wait_alone(rstd_ready.sem, rstd_ready.at(L * 2 + 1, 0))
                for hf in range(2):
                    with dve.Fori(0, PAIRS_UP) as j:
                        v = V + OFF_UP[hf] + j
                        for s in range(2):
                            dve.wait_ge(unit_done.sem, v * 2 + (s + 3))
                            if s == 0:
                                order.settle()
                            dve.tensor_tensor(pad[s][:, 1:SEQ + 1], ps[:, ACC[s], :], rstd[:], ALU.mult)\
                                .then_inc(acc_free.sem, 1)
                            col = s * NF + hf * HALF + j
                            i = 2 * (hf * HALF + j) + s
                            dve.wait_ge(center_ready.sem, L * 2 * NF + i + 1)
                            order.step(dve.scalar_tensor_tensor(cv[s][:], pad[s][:, 0:SEQ], param(pb, L, col), cv[s][:],
                                                                ALU.mult, ALU.add))
                            order.settle()
                            order.told(dve.scalar_tensor_tensor(cv[s][:], pad[s][:, 2:SEQ + 2], param(pc, L, col), cv[s][:],
                                                                ALU.mult, ALU.add), conv_ready, L, i)
                        t = hf * HALF + j
                        dve.wait_ge(silu_ready.sem, silu_ready.at(L, t))
                        order.settle()
                        order.told(dve.tensor_tensor(prod[:], cv[0][:], cv[1][:], ALU.mult), prod_ready, L, t)
                        dve.wait_ge(ahi_ready.sem, ahi_ready.at(L, t))
                        order.told(dve.tensor_tensor(tile(a_lo, j), prod[:], tile(a_hi, j).bitcast(F32), ALU.subtract),
                                   a_ready, L, t)
                        order.restart()
                    if hf == 0:
                        with dve.Fori(0, PAIRS_DOWN) as j:
                            for s in range(2):
                                residual(V + OFF_DOWN[hf] + j, s, j * 2 + s)
                            order.restart()
                    else:
                        residual_norm(L * 2 + 2, V + OFF_DOWN[hf], 0, True)
                        order.restart()
                        with dve.Fori(1, PAIRS_DOWN) as j:
                            residual_norm(L * 2 + 2, V + OFF_DOWN[hf] + j, j, False)
                            order.restart()

            with dve.Fori(0, DEPTH) as L:
                V = BASE2 + L * PAIRS2
                G = L * 2 + 2 * DEPTH
                dve.wait_ge(rstd_ready.sem, rstd_ready.at(G, 0))
                order.step(dve.memset(zp[:, :, 0:GT - 1], 0.0))
                order.step(dve.memset(ypad[:, :, 0:CT - 1], 0.0))
                for i in range(NA):
                    order.step(dve.memset(vaug2[:, 2 * i, :, 64:128], 1.0))
                    ins = dve.memset(vaug2[:, 2 * i + 1, :, 0:64], 1.0)
                    if i == NA - 1:
                        order.told(ins, v2ones_ready, L, 0)
                    else:
                        order.step(ins)

                def project(i, dst):
                    dve.wait_ge(unit_done.sem, V * 2 + i + 3)
                    order.settle()
                    dve.tensor_tensor(dst, ps[:, ACC[i % 2], :], rstd[:], ALU.mult).then_inc(acc_free.sem, 1)
                    order.last = (acc_free.sem, V * 2 + i + 3)

                def split_gate_weights():
                    dve.wait_ge(wab_loaded.sem, L * 16 + 16)
                    order.settle()
                    order.told(dve.tensor_copy(wab_hi[:], wab[:]), wab_split, L, 0)
                    order.settle()
                    order.told(dve.tensor_tensor(wab_lo[:], wab[:], wab_hi[:].bitcast(F32), ALU.subtract), wab_split, L, 1)

                def gate_arguments():
                    dve.wait_ge(abT_ready.sem, abT_ready.at(L, 0))
                    abp = ps[:, TRN[1], :].rearrange("p (t c) -> p t c", c=P)
                    dtb = gate_par[:, 1, ds(L, 1), :].to_broadcast([P, TB, GH])
                    order.step(dve.tensor_tensor(cols["a"][:], abp[:, :, 0:GH], dtb, ALU.add))
                    order.step(dve.tensor_copy(cols["b"][:], abp[:, :, GH:2 * GH]))
                    order.settle()
                    order.step(dve.tensor_scalar(cols["ax"][:], cols["a"][:], -1.0, None, ALU.mult))
                    order.settle()
                    order.told(dve.tensor_tensor(cols["ax"][:], cols["ax"][:], cols["a"][:], ALU.max), gate_in, L, 0)

                def gates():
                    dve.wait_ge(gate_e1.sem, gate_e1.at(L, 0))
                    order.step(dve.tensor_scalar(cols["beta"][:], cols["beta"][:], 1.0, None, ALU.add))
                    order.settle()
                    order.step(dve.reciprocal(cols["beta"][:], cols["beta"][:]))
                    dve.wait_ge(gate_e2.sem, gate_e2.at(L, 0))
                    order.step(dve.scalar_tensor_tensor(cols["a"][:], cols["a"][:], 0.0, cols["l"][:], ALU.max, ALU.add))
                    order.settle()
                    order.told(dve.scalar_tensor_tensor(cols["g"][:], cols["a"][:], -1.0,
                                                        expa[:].unsqueeze(1).to_broadcast([P, TB, GH]), ALU.mult, ALU.mult), g_ready, L, 0)

                def rotary(i):
                    z = za[:, i, :]
                    if i == 0:
                        dve.wait_ge(c2_loaded.sem, 3 * 16)
                    dve.wait_ge(rot2_ready.sem, rot2_ready.at(L, i))
                    order.settle()
                    order.told(dve.tensor_tensor(ta[:], ps[:, ROT[i % 2], :], rope2[:, 1, :], ALU.mult), rot2_used, L, i)
                    order.step(dve.tensor_tensor(tb2[:], z, rope2[:, 0, :], ALU.mult))
                    order.settle()
                    order.told(dve.tensor_tensor(z, ta[:], tb2[:], ALU.add), rope2_ready, L, i)

                def row_max(h, b):
                    dve.wait_ge(S2_ready.sem, S2_ready.at(L, 2 * h + b))
                    order.settle()
                    order.told(dve.tensor_reduce(mx2[:, h % 2, 2 * b:2 * b + 2], ps[:, STAT[0]:STAT[1] + 1, :], AX, ALU.max),
                               S2_used, L, 2 * h + b)

                def maxima(h):
                    if h >= 2:
                        dve.wait_ge(ST2_ready.sem, ST2_ready.at(L, (h - 1) * TB - 1))
                    order.settle()
                    order.told(dve.tensor_tensor(diag2[:, h % 2, :, :], ident[:].unsqueeze(1).to_broadcast([P, TB, P]),
                                                 mx2[:, h % 2, :].unsqueeze(2).to_broadcast([P, TB, P]), ALU.mult), diag2_ready, L, h)

                def counted(h, kt):
                    n, q0, o = h * TB + kt, kt * P, (TB - 1 - kt) * P
                    if n == 0:
                        dve.wait_ge(c2_cast.sem, 5 * 16)
                    dve.wait_ge(E2_ready.sem, E2_ready.at(L, n))
                    order.told(dve.tensor_tensor(probs2[:, kt, q0:], probs2[:, kt, q0:], times[:, o + q0:o + SEQ], ALU.mult),
                               P2_ready, L, n)

                def attended(h):
                    t, r = h // 2, 64 * (h % 2)
                    dve.wait_ge(rl2_ready.sem, rl2_ready.at(L, h))
                    order.told(dve.tensor_tensor(ya[r:r + 64, t, :], ps[r:r + 64, TRN[h % 2], :], ta[r:r + 64, :], ALU.mult), ya_ready, L, h)

                def short_taps(n):
                    dve.wait_ge(sc_center.sem, sc_center.at(L, n))
                    for k in range(GT - 1):
                        order.settle()
                        ins = dve.scalar_tensor_tensor(gqkv[n], zp[:, n % 2, k:k + SEQ], param(pd, L, D_SC + k * NG + n), gqkv[n],
                                                       ALU.mult, ALU.add)
                        if k == GT - 2:
                            order.told(ins, sc_ready, L, n)
                        else:
                            order.step(ins)

                def glu():
                    for t in range(NC):
                        dve.wait_ge(cg_ready.sem, cg_ready.at(L, t))
                        order.step(dve.tensor_tensor(ypad[:, t, CT - 1:], ypad[:, t, CT - 1:], cg[:, t, :], ALU.mult))
                    order.settle()

                def taps(k0, k1):
                    for k in range(k0, k1):
                        order.settle()
                        for t in range(NC):
                            w = param(pd, L, D_DW + k * NC + t)
                            src = ypad[:, t, k:k + SEQ]
                            if k == 0:
                                ins = dve.tensor_scalar(yc[:, t, :], src, w, param(pd, L, D_BIAS + t), ALU.mult, ALU.add)
                            else:
                                ins = dve.scalar_tensor_tensor(yc[:, t, :], src, w, yc[:, t, :], ALU.mult, ALU.add)
                            if k == CT - 1:
                                order.told(ins, dw_ready, L, t)
                            else:
                                order.step(ins)

                def l2_scaled(i):
                    dve.wait_ge(l2rs.sem, l2rs.at(L, i))
                    order.told(dve.scalar_tensor_tensor(gqkv[i], gqkv[i], float(P) ** -0.5 if i < GH else 1.0, l2r[:, i % 4, :],
                                                        ALU.mult, ALU.mult), l2n, L, i)

                NCOL = TB * GH
                flat = lambda n: cols[n][:].rearrange("p t h -> p (t h)")
                dests = [*(za[:, i, :] for i in range(3 * NA)), *(ypad[:, t, CT - 1:] for t in range(NC)), *(cg[:, t, :] for t in range(NC)),
                         *(zp[:, n % 2, GT - 1:GT - 1 + SEQ] for n in range(NG)), *(gz[:, h, :] for h in range(GH))]
                beside = [2] * 14 + [3]
                assert sum(beside) == CT and 11 + len(beside) == N_IN2
                for i, dst in enumerate(dests):
                    project(i, dst)
                    if 0 <= i - 2 < 2 * NA:
                        rotary(i - 2)
                    if i == 3:
                        split_gate_weights()
                        order.step(dve.memset(probs2[:, 0, :], 0.0))
                    if i == 5:
                        dve.wait_ge(ab_ready.sem, ab_ready.at(L, 0))
                        order.told(dve.tensor_tensor(ab, ps[0:2 * GH, TRN[0], :], rstd[0:2 * GH, :], ALU.mult), ab_kept, L, 0)
                    if i == 6:
                        gate_arguments()
                    if i == 8:
                        gates()
                    for h in range(AH):
                        if i - 8 - 2 * h in (0, 1):
                            row_max(h, i - 8 - 2 * h)
                        if i == 9 + 2 * h:
                            maxima(h)
                    for h in range(AH):
                        if i - 11 - 2 * h in (0, 1):
                            for kt in range(2 * (i - 11 - 2 * h), 2 * (i - 11 - 2 * h) + 2):
                                counted(h, kt)
                        if i == 15 + 2 * h:
                            attended(h)
                    n = i - 3 * NA - 2 * NC
                    if 0 <= n < NG:
                        short_taps(n)
                    if i == 11:
                        glu()
                    if i >= 11:
                        taps(sum(beside[:i - 11]), sum(beside[:i - 10]))
                    if i == 21:
                        dve.wait_ge(G_ready.sem, G_ready.at(L, 0))
                        order.told(dve.tensor_copy(flat("gc"), ps[:, TRN[0], 0:NCOL]), gc_kept, L, 0)
                        order.settle()
                        order.told(dve.tensor_tensor(flat("dg"), ps[:, TRN[0], NCOL:2 * NCOL], flat("gc"), ALU.subtract), dg_ready, L, 0)
                    if i == 24:
                        for t in range(4):
                            l2_scaled(t)
                        dve.wait_ge(eg_cols.sem, eg_cols.at(L, 0))
                        order.told(dve.tensor_tensor(flat("beg"), flat("beta"), flat("egc"), ALU.mult), beg_ready, L, 0)
                for t in range(4, 8):
                    l2_scaled(t)
                order.settle()

                def by_token(t):
                    return t.rearrange("p (t d) -> p t d", d=P)

                def column(n, h):
                    return cols[n][:, :, h:h + 1].to_broadcast([P, TB, P])

                for h in range(GH):
                    s = h % 2
                    dve.wait_ge(grow_ready.sem, grow_ready.at(L, h))
                    order.settle()
                    order.step(dve.tensor_tensor(by_token(dm[:, s, :]), by_token(ps[:, ROT[s], :]), column("gc", h), ALU.subtract))
                    order.settle()
                    order.told(dve.tensor_scalar(dm[:, s, :], dm[:, s, :], 0.0, None, ALU.min), gap_ready, L, h)
                    dve.wait_ge(brow_ready.sem, brow_ready.at(L, h))
                    order.told(dve.tensor_tensor(kb[:, s, :], ps[:, STAT[s], :], gk[:, h, :], ALU.mult), kb_ready, L, h)
                    dve.wait_ge(kT_ready.sem, kT_ready.at(L, h))
                    order.step(dve.tensor_tensor(kbeg[:, h, :, :], by_token(ps[:, TRN[0], :]), column("beg", h), ALU.mult))
                    order.step(dve.tensor_tensor(kout[:, h, :, :], by_token(ps[:, TRN[0], :]), column("egl", h), ALU.mult))
                    dve.wait_ge(gvT_ready.sem, gvT_ready.at(L, h))
                    order.told(dve.tensor_tensor(vb[:, h, :, :], by_token(ps[:, TRN[1], :]), column("beta", h), ALU.mult), turned_used, L, h)
                    dve.wait_ge(decay_ready.sem, decay_ready.at(L, h))
                    dve.wait_ge(kk_ready.sem, kk_ready.at(L, h))
                    order.settle()
                    order.step(dve.tensor_tensor(gv[:, h, :], ps[:, ACC[0], :], dm[:, s, :], ALU.mult))
                    dve.wait_ge(qk_ready.sem, qk_ready.at(L, h))
                    order.step(dve.tensor_tensor(intraT[:, h, :], ps[:, ACC[1], :], dm[:, s, :], ALU.mult))
                    order.settle()
                    order.step(dve.tensor_tensor(by_token(intraT[:, h, :]), by_token(intraT[:, h, :]),
                                                 tri[:].unsqueeze(1).to_broadcast([P, TB, P]), ALU.mult))
                    dve.wait_ge(eg_ready.sem, eg_ready.at(L, h))
                    order.step(dve.tensor_tensor(gq[:, h, :], gq[:, h, :], eg[:, s, :], ALU.mult))
                    order.told(dve.tensor_copy(eg_last[:, h, :], eg[:, s, CH - 1::CH]), head_ready, L, h)
                unit_blocks = ident[:].unsqueeze(1).to_broadcast([P, TB, P])
                for n in range(GH * LEVELS + 2):
                    if n < GH * LEVELS:
                        if n >= 2:
                            dve.wait_ge(p1_ready.sem, p1_ready.at(L, n - 2))
                        order.settle()
                        order.told(dve.tensor_tensor(by_token(lt[:, n % 2, :]), by_token(gv[:, n % GH, :]),
                                                     lev[:, n // GH, :].unsqueeze(1).to_broadcast([P, TB, P]), ALU.mult), lt_ready, L, n)
                    if n < GH:
                        order.settle()
                        order.step(dve.tensor_tensor(by_token(xT[:, n, :]), unit_blocks, by_token(lt[:, n % 2, :]), ALU.subtract))
                    if n == 10:
                        dve.wait_ge(mean_kept.sem, mean_kept.at(L, 0))
                        for i in range(NC):
                            order.told(dve.tensor_tensor(yc[:, i, :], yc[:, i, :], lnt[:], ALU.subtract), centered, L, i)
                    if n == 18:
                        dve.wait_ge(ln_rs.sem, ln_rs.at(L, 0))
                        for i in range(NC):
                            order.told(dve.scalar_tensor_tensor(yc[:, i, :], yc[:, i, :], param(pd, L, D_LNG + i), mrs2[:, 0, :],
                                                                ALU.mult, ALU.mult), ln_scaled, L, i)
                    m = n - 2
                    h = m % GH
                    if 0 <= m < GH:
                        dve.wait_ge(p1_ready.sem, p1_ready.at(L, m))
                        order.told(dve.tensor_tensor(by_token(gk[:, h, :]), unit_blocks, by_token(ps[:, ROT[m % 2], :]), ALU.subtract),
                                   x_new, L, m)
                    elif m >= GH:
                        if m < GH * (LEVELS - 1):
                            dve.wait_ge(xp_ready.sem, xp_ready.at(L, m - GH))
                            order.step(dve.tensor_tensor(gk[:, h, :], gk[:, h, :], ps[:, STAT[m % 2], :], ALU.subtract))
                        dve.wait_ge(xpt_ready.sem, xpt_ready.at(L, m - GH))
                        order.told(dve.tensor_tensor(xT[:, h, :], xT[:, h, :], ps[:, TRN[m % 2], :], ALU.subtract), x_new, L, m)
                for h in range(GH):
                    dve.wait_ge(ww_ready.sem, ww_ready.at(L, h))
                    order.told(dve.tensor_copy(kbeg[:, h, :, :].rearrange("p t d -> p (t d)"), ps[:, STAT[h % 2], :]), ww_kept, L, h)
                order.told(dve.memset(states[0], 0.0), state_ready, L, 0)
                for c in range(NCH):
                    tb, r = c // 2, CH * (c % 2)
                    if c < NCH - 1:
                        order.settle()
                        for h in range(GH):
                            order.step(dve.tensor_scalar(decayed[:, h, :], states[c % 2][:, h, :], eg_last[:, h, c:c + 1], None, ALU.mult))
                    dve.wait_ge(ws_ready.sem, ws_ready.at(L, c))
                    if c == 0:
                        dve.wait_ge(uu_kept.sem, uu_kept.at(L, GH - 1))
                    order.told(dve.tensor_tensor(vn[r:r + CH, :, :], vb[r:r + CH, :, tb, :],
                                                 ps[r:r + CH, ROT[c % 2], :].rearrange("p (h d) -> p h d", d=P), ALU.subtract), vn_ready, L, c)
                    if c < NCH - 1:
                        dve.wait_ge(ds_ready.sem, ds_ready.at(L, c))
                        order.settle()
                        order.told(dve.tensor_tensor(states[(c + 1) % 2], decayed,
                                                     ps[:, TRN[c % 2], :].rearrange("p (h d) -> p h d", d=P), ALU.add), state_ready, L, c + 1)
                for h in range(GH):
                    dve.wait_ge(ogrs.sem, ogrs.at(L, h))
                    order.step(dve.scalar_tensor_tensor(og[:, h, :], og[:, h, :], param(pd, L, D_ON), mrs2[:, h % 2, :], ALU.mult, ALU.mult))
                    order.settle()
                    order.told(dve.tensor_tensor(og[:, h, :], og[:, h, :], gz[:, h, :], ALU.mult), og_ready, L, h)
                for n, src in enumerate(mixed):
                    dve.wait_ge(m2hi_ready.sem, m2hi_ready.at(L, n))
                    order.settle()
                    order.told(dve.tensor_tensor(a_lo[:, n, :], src, a_hi[:, n, :].bitcast(F32), ALU.subtract), merged2_ready, L, n)
                order.restart()

                def branch(i, v, j, more):
                    for s in range(2):
                        n = j * 2 + s
                        dve.wait_ge(unit_done.sem, v * 2 + (s + 3))
                        if more:
                            ins = dve.tensor_tensor(tile(y, n), tile(y, n), ps[:, ACC[s], :], ALU.add)
                        else:
                            ins = dve.tensor_copy(tile(y, n), ps[:, ACC[s], :])
                        ins.then_inc(acc_free.sem, 1)
                        order.last = (acc_free.sem, v * 2 + (s + 3))
                        if i is None:
                            continue
                        dve.wait_ge(ysq_ready.sem, ysq_ready.at(L, i * KD + n))
                        if isinstance(n, int) and n == 0:
                            ins = dve.tensor_copy(prod[:], cv[s][:])
                        else:
                            dve.wait_ge(yssq_done.sem, yssq_done.at(L, i * KD + n - 1))
                            ins = dve.tensor_tensor(prod[:], prod[:], cv[s][:], ALU.add)
                        order.told(ins, yssq_done, L, i * KD + n)
                    order.restart()

                def post_norm(i, gen):
                    dve.wait_ge(yrs_ready.sem, yrs_ready.at(L, i))

                    for n in range(KD + 1):
                        if n < KD:
                            scaled = (cv[1], prod)[n % 2]
                            order.step(dve.scalar_tensor_tensor(scaled[:], y[:, n, :], gain(L * 2 * KD + ((GENS + i) * KD + n)), cv[0][:],
                                                                ALU.mult, ALU.mult))
                            order.settle()
                            order.told(dve.tensor_tensor(x[:, n, :], x[:, n, :], scaled[:], ALU.add), x2_ready, L, i * KD + n)
                        if n == 1:
                            grown(gen, 0, 0, True)
                        if n >= 1:
                            low_half(gen, n - 1)
                    order.restart()

                branch(0, V + OFF_O2, 0, False)
                with dve.Fori(1, PAIRS_O) as j:
                    branch(0, V + OFF_O2 + j, j, False)
                post_norm(0, G + 1)
                for hf in range(2):
                    with dve.Fori(0, PAIRS_UP) as j:
                        v = V + OFF_UP2[hf] + j
                        t = hf * HALF + j
                        dve.wait_ge(rstd_ready.sem, rstd_ready.at(G + 1, 0))
                        for s in range(2):
                            dve.wait_ge(unit_done.sem, v * 2 + (s + 3))
                            dve.tensor_tensor(cv[s][:], ps[:, ACC[s], :], rstd[:], ALU.mult).then_inc(acc_free.sem, 1)
                            order.last = (acc_free.sem, v * 2 + (s + 3))
                        dve.wait_ge(silu2_ready.sem, silu2_ready.at(L, t))
                        order.settle()
                        order.told(dve.tensor_tensor(prod[:], cv[0][:], cv[1][:], ALU.mult), prod2_ready, L, t)
                        dve.wait_ge(a2hi_ready.sem, a2hi_ready.at(L, t))
                        order.told(dve.tensor_tensor(tile(a_lo, j), prod[:], tile(a_hi, j).bitcast(F32), ALU.subtract), a2_ready, L, t)
                        order.restart()
                    if hf == 0:
                        with dve.Fori(0, PAIRS_DOWN) as j:
                            branch(None, V + OFF_DOWN2[hf] + j, j, False)
                    else:
                        branch(1, V + OFF_DOWN2[hf], 0, True)
                        with dve.Fori(1, PAIRS_DOWN) as j:
                            branch(1, V + OFF_DOWN2[hf] + j, j, True)
                post_norm(1, G + 2)

            for i in range(TB * 2):
                tb, hf = i // 2, i % 2
                dve.wait_ge(out_turned.sem, i + 1)
                dve.tensor_copy(xs[:, tb, hf * SEQ:(hf + 1) * SEQ], ps[:, ROT[i % 2], :]).then_inc(out_kept.sem, 1)


def constants(seq, head_dim, grid_w, theta, patterns):
    import numpy as np

    f = np.float32
    ident = np.eye(P, dtype=f)
    blk = np.kron(np.eye(2, dtype=f), np.ones((64, 64), f))
    half = head_dim // 2
    inv = f(1) / (f(theta) ** (np.arange(0, half, 2, dtype=f) / f(half)))
    pos = np.arange(seq)
    rope, perm = np.zeros((2, P, seq), f), np.zeros((P, P), f)
    for p in range(P):
        d = p % head_dim
        axis = (pos // grid_w if d < half else pos % grid_w).astype(f)
        i = d % half
        ang = axis * inv[i % (half // 2)]
        rope[0, p], rope[1, p] = np.cos(ang), np.sin(ang) * (f(-1) if i < half // 2 else f(1))
        perm[p ^ (half // 2), p] = 1
    half = head_dim // 2
    inv = np.exp(f(-math.log(theta)) * np.arange(half, dtype=f) * f(2.0 / head_dim))
    rope2, perm2 = np.zeros((2, P, seq), f), np.zeros((P, P), f)
    for p in range(P):
        d = p % head_dim
        ang = pos.astype(f) * inv[d % half]
        rope2[0, p], rope2[1, p] = np.cos(ang), np.sin(ang) * (f(-1) if d < half else f(1))
        perm2[p ^ half, p] = 1
    def held(d):
        return sum((d >= 0) & (d <= window) & (d % dilation == 0) for window, dilation in patterns).astype(f)

    p, c = np.arange(P)[:, None], np.arange(2 * seq - P)[None, :]
    by_query, by_key = held(p + (seq - P) - c), held(c - (seq - P) - p)
    low = lambda n: np.where(n > 0, f(0), f(-1e30))
    j, i = np.arange(P)[:, None], np.arange(P)[None, :]
    tri = ((j // 64 == i // 64) & (j <= i)).astype(f)
    lev = np.stack([((j // (2 << s) == i // (2 << s)) & (j // (1 << s) < i // (1 << s))).astype(f) for s in range(6)])
    return {"c_ident": ident, "c_blk": blk, "c_rope": rope, "c_perm": perm, "c_rope2": rope2, "c_perm2": perm2,
            "c_mask_s": low(by_query), "c_mask_t": low(by_key), "c_times": by_key, "c_tri": tri, "c_lev": lev}


def kernel(**inputs):
    import numpy as np
    import concourse.bacc as bacc
    from concourse.bass_utils import run_bass_kernel_spmd

    nc = bacc.Bacc("TRN2", target_bir_lowering=False, num_devices=1)
    arrays = {f"in_{n}": np.ascontiguousarray(a) for n, a in inputs.items()}
    arrays |= {f"in_{n}": a for n, a in constants(inputs["x"].shape[1], inputs["q_norm_g"].shape[1], 64, 10000.0,
                                                        ((128, 1), (512, 4), (2048, 16))).items()}
    D = {n[3:]: nc.dram_tensor(n, a.shape, mybir.dt.from_np(a.dtype), kind="ExternalInput").ap() for n, a in arrays.items()}
    out = nc.dram_tensor("out", inputs["x"].shape, F32, kind="ExternalOutput").ap()
    network(nc, D, out)
    r = run_bass_kernel_spmd(nc, [arrays], core_ids=[0])
    return r.results[0]["out"]
```
